# Optimizing a Trainium2 kernel written in Bass

```python
import jax
import jax.numpy as jnp
from jax import lax
import numpy as np

D_MODEL = 1024
BATCH = 1
SEQ = 512
DEPTH = 1
DEC_BATCH = 8
DEC_SEQ = 4
PAST_LEN = 4096
PAGE_SIZE = 128

MIX_W = D_MODEL
HEAD_DIM = 64
RET_HEADS = (MIX_W // 2) // HEAD_DIM
RET_W = RET_HEADS * HEAD_DIM
MOBA_HEADS = (MIX_W - RET_W) // HEAD_DIM
MOBA_W = MOBA_HEADS * HEAD_DIM
RET_CHUNK = 128
MOBA_BLOCK = 256
MOBA_TOPK = 3
MOBA_Q_CHUNK = 16
D_FF = -(-8 * D_MODEL // (3 * 256)) * 256
ROPE_BASE = 10000.0
NORM_EPS = 1e-6
IN_COLS = 4 * RET_W + 3 * MOBA_W
SPLITS = (RET_W, 2 * RET_W, 3 * RET_W, 4 * RET_W, 4 * RET_W + MOBA_W, 4 * RET_W + 2 * MOBA_W)

kernel_name = 'hybrid_retention_moba_adaln_step'

def _rmsnorm(x, w):
    xf = x.astype(jnp.float32)
    y = xf * lax.rsqrt(jnp.mean(xf * xf, axis=-1, keepdims=True) + NORM_EPS)
    return (y * w.astype(jnp.float32)).astype(x.dtype)

def _modulation(c, w_mod, b_mod):
    m = jax.nn.silu(c) @ w_mod + b_mod
    return jnp.split(m[:, None, :], 6, axis=-1)

def _rotary(x, pos):
    half = x.shape[-1] // 2
    inv = ROPE_BASE ** (-jnp.arange(half, dtype=jnp.float32) / half)
    ang = pos.astype(jnp.float32)[:, None] * inv[None, :]
    cos = jnp.cos(ang)[None, :, None, :]
    sin = jnp.sin(ang)[None, :, None, :]
    x1 = x[..., :half].astype(jnp.float32)
    x2 = x[..., half:].astype(jnp.float32)
    return jnp.concatenate([x1 * cos - x2 * sin, x1 * sin + x2 * cos], axis=-1)

def _retention_scan(q, k, v, s0):
    B, H, L, _ = q.shape
    C = RET_CHUNK if L % RET_CHUNK == 0 else L
    n = L // C
    log_g = jnp.log1p(-jnp.exp2(-5.0 - jnp.arange(H, dtype=jnp.float32)))
    idx = jnp.arange(C, dtype=jnp.float32)
    diff = idx[:, None] - idx[None, :]
    dmat = jnp.where(diff >= 0, jnp.exp(jnp.maximum(diff, 0.0) * log_g[:, None, None]), 0.0)
    q_dec = jnp.exp((idx + 1.0) * log_g[:, None])[..., None]
    k_dec = jnp.exp((C - 1.0 - idx) * log_g[:, None])[..., None]
    c_dec = jnp.exp(C * log_g)[:, None, None]

    def blocks(t):
        return t.reshape(B, H, n, C, t.shape[-1]).transpose(2, 0, 1, 3, 4)

    def step(s, inp):
        qc, kc, vc = inp
        att = jnp.einsum('bhid,bhjd->bhij', qc, kc) * dmat
        o = jnp.einsum('bhij,bhjv->bhiv', att, vc) + jnp.einsum('bhid,bhdv->bhiv', qc, s) * q_dec
        s = s * c_dec + jnp.einsum('bhjd,bhjv->bhdv', kc * k_dec, vc)
        return s, o

    s, o = lax.scan(step, s0, (blocks(q), blocks(k), blocks(v)))
    return o.transpose(1, 2, 0, 3, 4).reshape(B, H, L, -1), s

def _retention_branch(rq, rk, rv, rg, pos, s0, gn_w):
    B, L = rq.shape[:2]
    q = _rotary(rq, pos).transpose(0, 2, 1, 3)
    k = (_rotary(rk, pos) * HEAD_DIM ** -0.5).transpose(0, 2, 1, 3)
    v = rv.astype(jnp.float32).transpose(0, 2, 1, 3)
    o, s = _retention_scan(q, k, v, s0.astype(jnp.float32))
    mu = jnp.mean(o, axis=-1, keepdims=True)
    var = jnp.mean(jnp.square(o - mu), axis=-1, keepdims=True)
    o = ((o - mu) * lax.rsqrt(var + NORM_EPS)).transpose(0, 2, 1, 3).reshape(B, L, RET_W)
    o = jax.nn.silu(rg.astype(jnp.float32)) * (o * gn_w.astype(jnp.float32))
    return o.astype(rq.dtype), s

def _moba_attend(q, k_sel, v_sel, sel_mask, k_own, v_own, own_mask):
    scale = q.shape[-1] ** -0.5
    f32 = jnp.float32
    l_sel = jnp.einsum('bhqd,bhqkd->bhqk', q, k_sel, preferred_element_type=f32) * scale
    l_own = jnp.einsum('bhqd,bhkd->bhqk', q, k_own, preferred_element_type=f32) * scale
    logits = jnp.concatenate([jnp.where(sel_mask, l_sel, -jnp.inf), jnp.where(own_mask, l_own, -jnp.inf)], axis=-1)
    p = jax.nn.softmax(logits, axis=-1)
    ns = k_sel.shape[3]
    out = (jnp.einsum('bhqk,bhqkd->bhqd', p[..., :ns], v_sel, preferred_element_type=f32)
           + jnp.einsum('bhqk,bhkd->bhqd', p[..., ns:], v_own, preferred_element_type=f32))
    return out.astype(q.dtype)

def _moba_prompt(q, k, v):
    B, S, H, d = q.shape
    nb = -(-S // MOBA_BLOCK)
    pad = nb * MOBA_BLOCK - S
    kh = jnp.pad(k, ((0, 0), (0, pad), (0, 0), (0, 0))).transpose(0, 2, 1, 3).reshape(B, H, nb, MOBA_BLOCK, d)
    vh = jnp.pad(v, ((0, 0), (0, pad), (0, 0), (0, 0))).transpose(0, 2, 1, 3).reshape(B, H, nb, MOBA_BLOCK, d)
    kmean = jnp.mean(kh, axis=3, dtype=jnp.float32)
    kk = min(MOBA_TOPK, nb)
    nq = S // MOBA_Q_CHUNK
    qs = q.reshape(B, nq, MOBA_Q_CHUNK, H, d).transpose(1, 0, 3, 2, 4)
    bi = jnp.arange(B)[:, None, None, None]
    hi = jnp.arange(H)[None, :, None, None]
    blk_ids = jnp.arange(nb)

    def one(args):
        ci, qc = args
        start = ci * MOBA_Q_CHUNK
        blk = start // MOBA_BLOCK
        qpos = start + jnp.arange(MOBA_Q_CHUNK)
        gate = jnp.einsum('bhqd,bhnd->bhqn', qc.astype(jnp.float32), kmean)
        gate = jnp.where(blk_ids < blk, gate, -jnp.inf)
        _, top_i = lax.top_k(gate, kk)
        sel_valid = top_i < blk
        k_sel = kh[bi, hi, top_i].reshape(B, H, MOBA_Q_CHUNK, kk * MOBA_BLOCK, d)
        v_sel = vh[bi, hi, top_i].reshape(B, H, MOBA_Q_CHUNK, kk * MOBA_BLOCK, d)
        sel_mask = jnp.repeat(sel_valid, MOBA_BLOCK, axis=-1)
        k_own = lax.dynamic_index_in_dim(kh, blk, axis=2, keepdims=False)
        v_own = lax.dynamic_index_in_dim(vh, blk, axis=2, keepdims=False)
        own_pos = blk * MOBA_BLOCK + jnp.arange(MOBA_BLOCK)
        own_mask = own_pos[None, :] <= qpos[:, None]
        return _moba_attend(qc, k_sel, v_sel, sel_mask, k_own, v_own, own_mask)

    out = lax.map(one, (jnp.arange(nq), qs))
    return out.transpose(1, 0, 3, 2, 4).reshape(B, S, H * d)

def _moba_sample(q, k_new, v_new, cache_k, cache_v, page_table):
    Bd, T, H, d = q.shape
    ppb = MOBA_BLOCK // PAGE_SIZE
    n_full = PAST_LEN // MOBA_BLOCK
    own_pages = (PAST_LEN % MOBA_BLOCK) // PAGE_SIZE
    qh = q.transpose(0, 2, 1, 3)
    if n_full > 0:
        kk = min(MOBA_TOPK, n_full)
        k_past = cache_k[page_table[:, :n_full * ppb]]
        kmean = jnp.mean(k_past.reshape(Bd, n_full, MOBA_BLOCK, H, d), axis=2, dtype=jnp.float32)
        gate = jnp.einsum('bhtd,bnhd->bhtn', qh.astype(jnp.float32), kmean)
        _, top_i = lax.top_k(gate, kk)
        logical = top_i[..., None] * ppb + jnp.arange(ppb)
        phys = page_table[jnp.arange(Bd)[:, None, None, None, None], logical]
        hi = jnp.arange(H)[None, :, None, None, None]
        k_sel = cache_k[phys, :, hi, :].reshape(Bd, H, T, kk * MOBA_BLOCK, d)
        v_sel = cache_v[phys, :, hi, :].reshape(Bd, H, T, kk * MOBA_BLOCK, d)
    else:
        k_sel = jnp.zeros((Bd, H, T, 0, d), q.dtype)
        v_sel = jnp.zeros((Bd, H, T, 0, d), q.dtype)
    sel_mask = jnp.ones((1, 1, 1, 1), dtype=bool)
    op = page_table[:, n_full * ppb:n_full * ppb + own_pages]
    n_own = own_pages * PAGE_SIZE
    k_own = jnp.concatenate([cache_k[op].reshape(Bd, n_own, H, d).astype(k_new.dtype), k_new], axis=1).transpose(0, 2, 1, 3)
    v_own = jnp.concatenate([cache_v[op].reshape(Bd, n_own, H, d).astype(v_new.dtype), v_new], axis=1).transpose(0, 2, 1, 3)
    kpos = jnp.arange(n_own + T)
    qpos = n_own + jnp.arange(T)
    own_mask = kpos[None, :] <= qpos[:, None]
    out = _moba_attend(qh, k_sel, v_sel, sel_mask, k_own, v_own, own_mask)
    return out.transpose(0, 2, 1, 3).reshape(Bd, T, H * d)

def _decoder_layer(x, c, pos, ret_s0, moba_mix, norm1_w, norm2_w, w_mod, b_mod, w_in,
                   ret_gn_w, moba_norm_w, w_out, w_gate, w_up, w_down):
    B, L, _ = x.shape
    sh1, sc1, g1, sh2, sc2, g2 = _modulation(c, w_mod, b_mod)
    h = _rmsnorm(x, norm1_w) * (1 + sc1) + sh1
    z = h @ w_in
    rq, rk, rv, rg, mq, mk, mv = jnp.split(z, SPLITS, axis=-1)

    def heads(t, n):
        return t.reshape(B, L, n, HEAD_DIM)

    ret_out, ret_s = _retention_branch(heads(rq, RET_HEADS), heads(rk, RET_HEADS), heads(rv, RET_HEADS),
                                       rg, pos, ret_s0, ret_gn_w)
    mk_h = heads(mk, MOBA_HEADS)
    mv_h = heads(mv, MOBA_HEADS)
    moba_out = moba_mix(heads(mq, MOBA_HEADS), mk_h, mv_h)
    moba_out = _rmsnorm(moba_out.reshape(B, L, MOBA_HEADS, HEAD_DIM),
                        moba_norm_w.reshape(MOBA_HEADS, HEAD_DIM)).reshape(B, L, MOBA_W)
    x = x + g1 * (jnp.concatenate([ret_out, moba_out], axis=-1) @ w_out)
    h2 = _rmsnorm(x, norm2_w) * (1 + sc2) + sh2
    x = x + g2 * ((jax.nn.silu(h2 @ w_gate) * (h2 @ w_up)) @ w_down)
    return x, mk_h, mv_h, ret_s

def setup_inputs(seed: int = 0) -> dict:
    key = jax.random.key(seed)
    ks = jax.random.split(key, 24)
    f32 = jnp.float32
    n_pages = PAST_LEN // PAGE_SIZE
    n_pool = (DEC_BATCH * n_pages * 5) // 4

    def nrm(k, shape, s):
        return jax.random.normal(k, shape, f32) * s

    page_table = jax.random.permutation(ks[6], n_pool)[:DEC_BATCH * n_pages].reshape(DEC_BATCH, n_pages).astype(jnp.int32)
    return {
        'x_prompt': nrm(ks[0], (BATCH, SEQ, D_MODEL), 1.0),
        'x_sample': nrm(ks[1], (DEC_BATCH, DEC_SEQ, D_MODEL), 1.0),
        'cache_k': nrm(ks[2], (DEPTH, n_pool, PAGE_SIZE, MOBA_HEADS, HEAD_DIM), 1.0),
        'cache_v': nrm(ks[3], (DEPTH, n_pool, PAGE_SIZE, MOBA_HEADS, HEAD_DIM), 1.0),
        'state_ret': nrm(ks[4], (DEPTH, DEC_BATCH, RET_HEADS, HEAD_DIM, HEAD_DIM), 0.3),
        'page_table': page_table,
        'c_prompt': nrm(ks[5], (BATCH, D_MODEL), 1.0),
        'c_sample': nrm(ks[7], (DEC_BATCH, D_MODEL), 1.0),
        'norm1_w': 1.0 + nrm(ks[8], (DEPTH, D_MODEL), 0.05),
        'norm2_w': 1.0 + nrm(ks[9], (DEPTH, D_MODEL), 0.05),
        'final_w': 1.0 + nrm(ks[10], (D_MODEL,), 0.05),
        'w_mod': nrm(ks[11], (DEPTH, D_MODEL, 6 * D_MODEL), 0.5 * D_MODEL ** -0.5),
        'b_mod': nrm(ks[12], (DEPTH, 6 * D_MODEL), 0.01),
        'w_in': nrm(ks[13], (DEPTH, D_MODEL, IN_COLS), D_MODEL ** -0.5),
        'ret_gn_w': 1.0 + nrm(ks[14], (DEPTH, RET_W), 0.05),
        'moba_norm_w': 1.0 + nrm(ks[15], (DEPTH, MOBA_W), 0.05),
        'w_out': nrm(ks[16], (DEPTH, MIX_W, D_MODEL), MIX_W ** -0.5),
        'w_gate': nrm(ks[17], (DEPTH, D_MODEL, D_FF), D_MODEL ** -0.5),
        'w_up': nrm(ks[18], (DEPTH, D_MODEL, D_FF), D_MODEL ** -0.5),
        'w_down': nrm(ks[19], (DEPTH, D_FF, D_MODEL), D_FF ** -0.5),
    }

def reference(x_prompt, x_sample, cache_k, cache_v, state_ret, page_table, c_prompt, c_sample,
              norm1_w, norm2_w, final_w, w_mod, b_mod, w_in, ret_gn_w, moba_norm_w, w_out,
              w_gate, w_up, w_down):
    Bp, S, _ = x_prompt.shape
    Bd, T, _ = x_sample.shape
    pos_p = jnp.arange(S)
    pos_s = PAST_LEN + jnp.arange(T)
    xp = x_prompt
    xs = x_sample
    kp_l, vp_l, rp_l, ks_l, vs_l, rs_l = [], [], [], [], [], []
    for l in range(DEPTH):
        lw = (norm1_w[l], norm2_w[l], w_mod[l], b_mod[l], w_in[l], ret_gn_w[l], moba_norm_w[l],
              w_out[l], w_gate[l], w_up[l], w_down[l])
        s0_p = jnp.zeros((Bp, RET_HEADS, HEAD_DIM, HEAD_DIM), jnp.float32)
        xp, kp, vp, rp = _decoder_layer(xp, c_prompt, pos_p, s0_p, _moba_prompt, *lw)
        ck = cache_k[l]
        cv = cache_v[l]
        moba_s = lambda q, k, v, ck=ck, cv=cv: _moba_sample(q, k, v, ck, cv, page_table)
        xs, ksm, vsm, rsm = _decoder_layer(xs, c_sample, pos_s, state_ret[l], moba_s, *lw)
        kp_l.append(kp); vp_l.append(vp); rp_l.append(rp)
        ks_l.append(ksm); vs_l.append(vsm); rs_l.append(rsm)
    y_prompt = _rmsnorm(xp, final_w)
    y_sample = _rmsnorm(xs, final_w)
    return (y_prompt, y_sample, jnp.stack(kp_l), jnp.stack(vp_l), jnp.stack(rp_l),
            jnp.stack(ks_l), jnp.stack(vs_l), jnp.stack(rs_l))


_drawn_inputs = setup_inputs


def setup_inputs(seed=0):
    import zlib

    import numpy as np

    out = dict(_drawn_inputs(seed))
    spreads = {}
    factors = {'norm2_w': 3.696, 'ret_gn_w': 8.0, 'moba_norm_w': 5.166}
    for name, (base, spread) in spreads.items():
        noise = np.random.default_rng([zlib.crc32(name.encode()), seed]).standard_normal(out[name].shape)
        drawn = base * np.exp(spread * noise) if base else spread * noise
        out[name] = jnp.asarray(drawn.astype(out[name].dtype))
    for name, factor in factors.items():
        out[name] = (out[name] * factor).astype(out[name].dtype)
    return out
```

```python
from contextlib import ExitStack

import numpy as np
import concourse.bass as bass
from concourse import mybir

F32, F32R, I32 = mybir.dt.float32, mybir.dt.float32r, mybir.dt.int32
ALU, ACT, AX = mybir.AluOpType, mybir.ActivationFunctionType, mybir.AxisListType

P = 128
DM = 1024
T = 512
NB_SEQ, TS = 8, 4
S = NB_SEQ * TS
HD = 64
H = 8
HP = H // 2
W = H * HD
PAST, PAGE, BLOCK, TOPK = 4096, 128, 256, 3
NPAGE = PAST // PAGE
NBLK = PAST // BLOCK
GRP = 4
NGRP = NPAGE // GRP
ROWS = PAGE // 32
DFF = 2816
KT = DM // P
FT = DFF // P
TT = T // P
EPS = 1e-6
BIG = 1e30
SCALE = HD ** -0.5
NSEQ = NB_SEQ + 1
CHUNK = 256
NIN = (4 * W + 3 * W) // CHUNK
NMOD = 6 * DM // CHUNK
RQ, RK, RV, RG, MQ, MK, MV = (W // P * i for i in range(7))
V_BMOD, V_N1, V_N2, V_GN, V_MN = 0, 48, 56, 64, 68
NVEC = 72


def constants():
    f = np.float32
    log_g = np.log1p(-np.exp2(-5.0 - np.arange(H))).astype(np.float64)
    p = np.arange(P)
    out, where = [], {}

    def put(name, a):
        a = np.asarray(a, f)
        full = np.zeros((P, int(np.prod(a.shape[1:]))), f)
        full[: a.shape[0]] = a.reshape(a.shape[0], -1)
        at = sum(x.shape[1] for x in out)
        where[name] = (at, a.shape)
        out.append(full)

    put("ident", np.eye(P))
    put("ones", np.ones((P, P)))
    inv = (f(10000.0) ** (-np.arange(32, dtype=f) / f(32))).astype(f)
    ang = (np.arange(T, dtype=f)[None, :] * inv[p % 32][:, None]).astype(f)
    put("cos", np.cos(ang))
    put("sin", np.sin(ang))
    rot = np.zeros((P, P))
    for m in range(P):
        if m % 64 < 32:
            rot[m + 32, m] = -1.0
        else:
            rot[m - 32, m] = 1.0
    put("rot", rot)
    angs = ((PAST + np.arange(S) % TS).astype(f)[:, None] * inv[None, :]).astype(f)
    put("cos_s", np.cos(angs))
    put("sin_s", np.sin(angs))
    i = np.arange(P)
    diff = i[None, :] - i[:, None]
    d = [np.where(diff >= 0, np.exp(np.maximum(diff, 0) * g) * SCALE, 0.0) for g in log_g]
    put("decay", np.stack(d, 1))
    s = np.arange(S)
    diff = s[None, :] - s[:, None]
    ok = (s[None, :] // TS == s[:, None] // TS) & (diff >= 0)
    put("decay_s", np.stack([np.where(ok, np.exp(np.maximum(diff, 0) * g) * SCALE, 0.0) for g in log_g], 1))
    hp_of = lambda hp: 2 * hp + p // 64
    put("q_dec", np.stack([np.exp((i[None, :] + 1) * log_g[hp_of(hp)][:, None]) for hp in range(HP)], 1))
    put("q_dec_s", np.stack([np.exp((s[None, :] % TS + 1) * log_g[hp_of(hp)][:, None]) for hp in range(HP)], 1))
    put("k_dec", np.exp((P - 1 - i)[:, None] * log_g[None, :]) * SCALE)
    kb = np.exp((TS - 1 - s % TS)[:, None] * log_g[None, :]) * SCALE
    put("k_dec_s", np.where((s // TS)[:, None, None] == np.arange(NB_SEQ)[None, :, None], kb[:, None, :], 0.0))
    put("c_dec", np.stack([np.exp(P * log_g[hp_of(hp)]) for hp in range(HP)], 1))
    put("c_dec_s", np.stack([np.exp(TS * log_g[hp_of(hp)]) for hp in range(HP)], 1))
    put("causal", np.where(i[None, :] <= i[:, None], 0.0, -BIG))
    h, g, t = p // 16, p // 4 % 4, p % 4
    same = (h[:, None] == h[None, :]) & (t[:, None] == t[None, :])
    put("pair0", same & (g[:, None] < 2))
    put("pair1", same & (g[:, None] >= 2))
    put("own_pair", same & (g[:, None] // 2 == g[None, :] // 2))
    n_own = 2 * np.arange(NGRP)[None, :] + (g // 2)[:, None]
    put("earlier", np.arange(NBLK)[None, None, :] < n_own[:, :, None])
    ht = np.arange(32)
    put("sum_g", (h * 4 + t)[:, None] == ht[None, :])
    put("sum_pv", (p % 32)[:, None] == ht[None, :])
    tok = np.arange(S)
    seq = np.arange(NB_SEQ)
    ok = (g == 0)[:, None, None] & (tok[None, None, :] // TS == seq[None, :, None]) & (tok % TS <= t[:, None])[:, None, :]
    put("own_mask", np.where(ok, 0.0, -BIG))
    put("head_diag", (p % 32 // 4)[:, None] == np.arange(H)[None, :])
    put("row32", (p % 32)[:, None])
    put("row128", p[:, None])
    return np.ascontiguousarray(np.concatenate(out, 1)), where


def decoder_step(nc, x_prompt, x_sample, cache_k, cache_v, state_ret, page_table, c_prompt, c_sample,
                 norm1_w, norm2_w, final_w, w_mod, b_mod, w_in, ret_gn_w, moba_norm_w, w_out,
                 w_gate, w_up, w_down, const, where,
                 y_prompt, y_sample, k_prompt, v_prompt, ret_prompt, k_sample, v_sample, ret_sample):
    NC = const.shape[1]
    persist, mid = ExitStack(), ExitStack()

    def sem(name):
        return persist.enter_context(nc.semaphore(name))

    def allocator(stack):
        return lambda name, shape, dt=F32: stack.enter_context(nc.sbuf_tensor(name, shape, dt))

    sb = allocator(persist)
    ct = sb("ct", [P, NC])

    def C(name):
        at, shape = where[name]
        n = int(np.prod(shape[1:]))
        v = ct[:shape[0], at:at + n]
        return v.rearrange("p (a b) -> p a b", a=shape[1]) if len(shape) == 3 else v

    ident, ones = C("ident"), C("ones")
    raw = [sb(f"raw{i}", [P, KT, CHUNK]) for i in range(2)]
    whi = [sb(f"whi{i}", [P, KT, P], F32R) for i in range(2)]
    wlo = [sb(f"wlo{i}", [P, KT, P], F32R) for i in range(2)]
    ahi = sb("ahi", [P, KT, T], F32R)
    alo = sb("alo", [P, KT, T], F32R)
    asT = sb("asT", [P, KT, S])
    vT = sb("vT", [P, NVEC])
    mT = sb("mT", [P, 48, NSEQ])
    gain = sb("gain", [P, KT, NSEQ])
    xs = sb("xs", [S, DM])
    stage = [sb(f"stage{i}", [P, T]) for i in range(2)]
    st = sb("st", [P, 64])
    st2 = sb("st2", [P, 64])
    kidx = sb("kidx", [P, NB_SEQ * NGRP], I32)
    kix = [sb(f"kix{i}", [P, 1], I32) for i in range(2)]
    pt = sb("pt", [P, NB_SEQ * NPAGE], I32)
    asm = sb("asm", [P, 256])
    xtmp = sb("xtmp", [S, CHUNK])
    sb2 = allocator(mid)
    zs = sb2("zs", [S, NIN * CHUNK])

    era1 = ExitStack()
    tmp = allocator(era1)
    zT = tmp("zT", [P, 28, T])
    era1a = ExitStack()
    tmp = allocator(era1a)
    vrow = tmp("vrow", [NVEC, P])
    crow = tmp("crow", [NSEQ, DM])
    cT = tmp("cT", [P, KT, NSEQ])
    xP = tmp("xP", [P, TT, DM])
    sq = tmp("sq", [P, DM])
    era1a.close()
    era1b = ExitStack()
    tmp = allocator(era1b)
    rvtok = tmp("rvtok", [P, TT, W])
    mvtok = tmp("mvtok", [P, TT, W])
    scr = tmp("scr", [P, 7, T])
    sst = tmp("sst", [P, 4, HD])
    era1b.close()
    rettok = zT[:, RV:RV + 4, :]
    mobatok = zT[:, MV:MV + 4, :]
    era1.close()

    era2 = ExitStack()
    tmp = allocator(era2)
    Kb = [tmp(f"K{i}", [P, ROWS * W]) for i in range(2)]
    KTb = [tmp(f"KT{i}", [P, ROWS, W // 32, 32]) for i in range(2)]
    VB = [tmp(f"V{i}", [P, W]) for i in range(8)]
    pe_x = tmp("pe_x", [P, NGRP, P])
    pT = tmp("pT", [P, NGRP, P])
    qbb = tmp("qbb", [P, W // 32, S])
    kbb = tmp("kbb", [P, W // 32, S])
    qbd = tmp("qbd", [P, W // 32, 32])
    state = tmp("state", [P, NB_SEQ, HP, HD])
    od = tmp("od", [P, H, HD])
    oall = tmp("oall", [32, NB_SEQ, HD])
    sm = tmp("sm", [P, 1024])
    kmask = [tmp(f"kmask{i}", [S, W]) for i in range(2)]
    qrs, krs = tmp("qrs", [S, W]), tmp("krs", [S, W])
    sT = tmp("sT", [P, 3, HP, S])
    ats = tmp("ats", [S, H, S])
    ret_s = tmp("ret_s", [S, W])
    era2.close()
    mid.close()

    era3 = ExitStack()
    tmp = allocator(era3)
    x2T = tmp("x2T", [P, KT, T])
    aT = tmp("aT", [P, FT, S])
    x2s = tmp("x2s", [S, DM])
    era3a = ExitStack()
    tmp = allocator(era3a)
    xP2 = tmp("xP2", [P, TT, DM])
    gmod = tmp("gmod", [S, DM])
    rb = tmp("rb", [P, T])
    xsn2 = tmp("xsn2", [S, DM])
    era3a.close()
    era3b = ExitStack()
    tmp = allocator(era3b)
    fhi = tmp("fhi", [P, FT, T], F32R)
    flo = tmp("flo", [P, FT, T], F32R)
    era3b.close()
    era4 = ExitStack()
    tmp = allocator(era4)
    fw = tmp("fw", [P, DM])
    ytok = [tmp(f"ytok{i}", [P, DM]) for i in range(2)]
    gmod2 = xs
    era4.close()
    era3.close()

    bank = [persist.enter_context(nc.psum_tensor(f"bank{i}", [P, 512], F32)) for i in range(8)]

    s_const, s_x, s_xs, s_c, s_vec, s_pt, s_state = (sem(n) for n in (
        "const_loaded", "x_loaded", "xs_loaded", "c_loaded", "vec_loaded", "pt_loaded", "state_loaded"))
    s_w = [sem(f"w_loaded{i}") for i in range(2)]
    s_x2l, s_fw = sem("x_reloaded"), sem("final_w_loaded")
    s_out = sem("out_stored")
    s_ytok = [sem(f"y_tile_stored{i}") for i in range(2)]
    s_hi, s_lo, s_ft, s_ev = sem("w_hi"), sem("w_lo"), sem("tile_done+2"), sem("tile_evicted+2")
    s_ss, s_sev = sem("sample_done"), sem("sample_evicted+2")
    s_md, s_mt = sem("mod_chunk_done"), sem("mod_ready")
    s_silu, s_ctp, s_ct, s_vtp, s_vt = (sem(n) for n in ("c_silu", "c_turned", "cT_ready", "vec_turned", "vecT_ready"))
    s_sqd, s_rin, s_xn, s_xsn = sem("squares"), sem("rms_inverse"), sem("x_normed"), sem("xs_normed")
    s_xt, s_stg, s_hhi, s_hlo = sem("act_turned"), sem("act_staged"), sem("act_hi"), sem("act_lo")
    s_xst, s_hs = sem("xs_turned"), sem("asT_ready")
    s_vt1, s_vt2 = sem("values_turned"), sem("values_copied")
    s_qk, s_sc, s_nm, s_p, s_ptp, s_pte, s_pv, s_on = (sem(n) for n in (
        "moba_qk", "moba_scores", "moba_negmax", "moba_probs+2", "moba_turned+2", "moba_probsT+2",
        "moba_out+2", "moba_normed+2"))
    s_rr, s_rq, s_rk, s_kt1, s_kt2, s_ra, s_rad, s_kv, s_st, s_ro, s_roc = (sem(n) for n in (
        "ret_rotated", "ret_q", "ret_k", "ret_kT", "ret_ktok", "ret_scores", "ret_decayed", "ret_kv",
        "ret_state", "ret_out", "ret_copied"))
    s_rs, s_hsq, s_hri, s_hrs, s_hn, s_sg = (sem(n) for n in (
        "ret_state_stored", "head_squares", "head_inverse", "head_rstd", "heads_normed", "gate_silu"))
    s_kst, s_vst, s_sst = sem("k_prompt_stored"), sem("v_prompt_stored"), sem("ret_sample_stored")
    s_srot, s_sqt, s_sqe, s_sa, s_sad, s_so, s_soc, s_sot, s_sor = (sem(n) for n in (
        "s_rotated", "s_qk_turned", "s_qkT", "s_scores", "s_decayed", "s_out", "s_out_copied", "s_out_turned", "s_out_row"))
    s_ssq, s_sri, s_srs, s_srn, s_srt, s_sas, s_ssg = (sem(n) for n in (
        "s_squares", "s_inverse", "s_rstd", "s_normed", "s_norm_turned", "s_ret_mixed", "s_gate_silu"))
    s_km, s_kvs, s_sts = sem("s_kmask"), sem("s_kv"), sem("s_state_new")
    s_idx, s_qz, s_qb, s_qd = sem("page_rows"), sem("qbd_zero"), sem("q_k_blocks"), sem("qbd_ready")
    s_k = [sem(f"k_loaded{i}") for i in range(2)]
    s_v = [sem(f"v_loaded{i}") for i in range(8)]
    s_kt, s_lg, s_own, s_s1, s_gt, s_mx, s_mxt, s_rm, s_mb, s_nb, s_ex, s_tp, s_te, s_rsm, s_den, s_vd, s_od, s_of, s_oe = (
        sem(n) for n in ("k_turned", "logits", "own_logits", "block_sums", "gates", "part_max", "part_max_turned",
                         "row_max", "max_spread", "exp_bias", "exps", "probs_turned", "probsT_copied", "part_den",
                         "denominators", "page_used", "out_masked", "out_folded", "out_kept"))
    s_ofs, s_ofr, s_ofq, s_oft, s_oas = (sem(n) for n in ("o_squares", "o_inverse", "o_rstd", "o_turned", "o_mixed"))
    s_sqx, s_ssm, s_r1, s_r2 = sem("x2_squares"), sem("x2_sums"), sem("x2_inverse"), sem("x2_rstd")
    s_nx, s_gmt, s_gme = sem("x2_scaled"), sem("gmod_turned"), sem("gmod_copied")
    s_xr, s_x2s, s_x2q, s_x2i, s_x2r, s_x2n = (sem(n) for n in (
        "x2T_ready", "x2s_ready", "x2s_squares", "x2s_inverse", "x2s_rstd", "x2s_normed"))
    s_sl, s_ff, s_fh, s_fl = sem("gate_silu_done"), sem("ff_staged"), sem("ff_hi"), sem("ff_lo")
    s_ssl, s_sml, s_smt, s_sme = (sem(n) for n in ("s_ffn_silu", "s_ffn_prod", "s_ffn_turned", "s_ffn_aT"))
    s_x3, s_yt, s_ysq, s_yi, s_yr, s_y = (sem(n) for n in (
        "x3_ready", "y_turned", "y_squares", "y_inverse", "y_rstd", "y_ready"))

    kview = lambda w: w[0].rearrange("(k p) f -> p k f", p=P)
    w_mod_v, w_in_v, w_out_v = kview(w_mod), kview(w_in), kview(w_out)
    w_gate_v, w_up_v, w_down_v = kview(w_gate), kview(w_up), kview(w_down)

    NMA = 2 * DM // CHUNK
    NMB = NMOD - NMA
    KD = (8, 8, 6)
    B_IN = NMA // 2
    B_MODB = B_IN + NIN // 2
    B_OUT = B_MODB + NMB // 2
    B_FFN = B_OUT + 2
    B_DOWN = B_FFN + FT // 2
    F_OUT, N_OUT = 2 * NIN, NIN
    F_FFN, N_FFN = F_OUT + 8, N_OUT + 4
    F_DOWN, N_DOWN = F_FFN + 2 * FT, N_FFN + FT
    N_STORES = [0]

    turned = lambda x: x.rearrange("p (h g t) -> p g h t", g=GRP, t=TS)
    by_page = lambda x: x.rearrange("p (g h t) -> p g h t", g=GRP, t=TS)

    block = persist.enter_context(nc.Block())

    @block.sync
    def _(sp):
        def store(dst, src):
            sp.dma_start(dst, src).then_inc(s_out, 16)
            N_STORES[0] += 1

        def chunk(u, view, at):
            sp.dma_start(raw[u][:, :, :], view[:, :, at]).then_inc(s_w[u], 16)

        sp.dma_start(crow[0:NB_SEQ, :], c_sample).then_inc(s_c, 16)
        sp.dma_start(crow[NB_SEQ:NSEQ, :], c_prompt).then_inc(s_c, 16)
        sp.dma_start(ct[:, :], const).then_inc(s_const, 16)
        for u in range(2):
            chunk(u, w_mod_v, slice(u * CHUNK, (u + 1) * CHUNK))
        sp.dma_start(vrow[V_BMOD:V_N1, :], b_mod[0].rearrange("(r c) -> r c", c=P)).then_inc(s_vec, 16)
        for at, v in ((V_N1, norm1_w), (V_N2, norm2_w), (V_GN, ret_gn_w), (V_MN, moba_norm_w)):
            n = v.shape[1] // P
            sp.dma_start(vrow[at:at + n, :], v[0].rearrange("(r c) -> r c", c=P)).then_inc(s_vec, 16)
        sp.dma_start(xP[:, :, :], x_prompt[0].rearrange("(i p) d -> p i d", p=P)).then_inc(s_x, 16)
        sp.dma_start(xs[:, :], x_sample.rearrange("b t d -> (b t) d")).then_inc(s_xs, 16)
        sp.dma_start(pt[:, :], page_table.rearrange("b n -> (b n)").partition_broadcast(P)).then_inc(s_pt, 16)
        with sp.Fori(1, NMA // 2) as i:
            for u in range(2):
                sp.wait_ge(s_md, 2 * i + u - 1)
                chunk(u, w_mod_v, bass.ds((2 * i + u) * CHUNK, CHUNK))
        for u in range(2):
            sp.wait_ge(s_md, NMA - 1 + u)
            chunk(u, w_in_v, slice(u * CHUNK, (u + 1) * CHUNK))
        with sp.Fori(1, NIN // 2) as i:
            for u in range(2):
                sp.wait_ge(s_ss, 2 * i + u - 1)
                chunk(u, w_in_v, bass.ds((2 * i + u) * CHUNK, CHUNK))
        for u in range(2):
            sp.wait_ge(s_ss, NIN - 1 + u)
            chunk(u, w_mod_v, slice((NMA + u) * CHUNK, (NMA + u + 1) * CHUNK))
        with sp.Fori(1, NMB // 2) as i:
            for u in range(2):
                sp.wait_ge(s_md, NMA + 2 * i + u - 1)
                chunk(u, w_mod_v, bass.ds((NMA + 2 * i + u) * CHUNK, CHUNK))
        sp.wait_ge(s_vt2, 4)
        sp.dma_start(k_prompt[0, 0].rearrange("(i p) h d -> p i (h d)", p=P), scr[:, 0:4, :]).then_inc(s_kst, 16)
        sp.wait_ge(s_vt2, 8)
        sp.dma_start(v_prompt[0, 0].rearrange("(i p) h d -> p i (h d)", p=P), mvtok[:, :, :]).then_inc(s_vst, 16)
        sp.wait_ge(s_sev, NIN + 2)
        store(k_sample[0].rearrange("b t h d -> (b t) (h d)"), zs[:, 5 * W:6 * W])
        store(v_sample[0].rearrange("b t h d -> (b t) (h d)"), zs[:, 6 * W:7 * W])
        with sp.Fori(0, HP) as hp:
            sp.wait_ge(s_st, hp + 1)
            sp.dma_start(ret_prompt[0, 0].rearrange("h d v -> (h d) v")[bass.ds(hp * P, P), :], sst[:, 3, :]).then_inc(s_rs, 16)
        sp.wait_ge(s_hlo, 2 * KT)
        sp.wait_ge(s_kst, 16)
        sp.wait_ge(s_vst, 16)
        sp.wait_ge(s_rs, 16 * HP)
        sp.dma_start(state[:, :, :, :], state_ret[0].rearrange("b (hp h2) d v -> (h2 d) b hp v", h2=2)).then_inc(s_state, 16)
        cv = cache_v[0].rearrange("n p h d -> n p (h d)")
        for s in range(8):
            r = sp.value_load(pt[0:1, s:s + 1], min_val=0, max_val=cv.shape[0] - 1)
            sp.dma_start(VB[s][:, :], cv[bass.ds(r, 1), :, :].rearrange("a p c -> (a p) c")).then_inc(s_v[s], 16)
        with sp.Fori(1, NB_SEQ * NPAGE // 8) as i:
            for s in range(8):
                r = sp.value_load(pt[0:1, bass.ds(i * 8 + s, 1)], min_val=0, max_val=cv.shape[0] - 1)
                sp.wait_ge(s_vd, i * 8 + s - 7)
                sp.dma_start(VB[s][:, :], cv[bass.ds(r, 1), :, :].rearrange("a p c -> (a p) c")).then_inc(s_v[s], 16)
        sp.wait_ge(s_sts, NB_SEQ)
        sp.dma_start(ret_sample[0].rearrange("b (hp h2) d v -> (h2 d) b hp v", h2=2), state[:, :, :, :]).then_inc(s_sst, 16)
        sp.wait_ge(s_oas, 1)
        sp.wait_ge(s_sst, 16)
        sp.dma_start(xP2[:, :, :], x_prompt[0].rearrange("(i p) d -> p i d", p=P)).then_inc(s_x2l, 16)
        for u in range(2):
            sp.wait_ge(s_md, NMOD - 1 + u)
            chunk(u, w_out_v, slice(u * CHUNK, (u + 1) * CHUNK))
        for u in range(2):
            sp.wait_ge(s_ss, N_OUT + u + 1)
            chunk(u, w_out_v, slice((2 + u) * CHUNK, (3 + u) * CHUNK))

        def ffn_chunk(u, at):
            sp.dma_start(raw[u][:, :, 0:P], w_gate_v[:, :, at]).then_inc(s_w[u], 16)
            sp.dma_start(raw[u][:, :, P:2 * P], w_up_v[:, :, at]).then_inc(s_w[u], 16)

        for u in range(2):
            sp.wait_ge(s_ss, N_OUT + 2 + u + 1)
            ffn_chunk(u, slice(u * P, (u + 1) * P))
        with sp.Fori(1, FT // 2) as i:
            for u in range(2):
                sp.wait_ge(s_ss, N_FFN + 2 * i + u - 1)
                ffn_chunk(u, bass.ds((2 * i + u) * P, P))
        c = 0
        for fb in range(DM // CHUNK):
            for n, kd in enumerate(KD):
                sp.wait_ge(s_ss, N_DOWN + c - 1)
                sp.dma_start(raw[c % 2][:, 0:kd, :], w_down_v[:, 8 * n:8 * n + kd, fb * CHUNK:(fb + 1) * CHUNK]).then_inc(s_w[c % 2], 16)
                c += 1
        sp.wait_ge(s_ft, F_DOWN + 24 + 2)
        sp.dma_start(fw[:, :], final_w.partition_broadcast(P)).then_inc(s_fw, 16)
        for i in range(TT):
            sp.wait_ge(s_y, i + 1)
            sp.dma_start(y_prompt[0, i * P:(i + 1) * P, :], ytok[i % 2][:, :]).then_inc(s_ytok[i % 2], 16)
        sp.wait_ge(s_y, TT + 1)
        store(y_sample.rearrange("b t d -> (b t) d"), x2s[:, :])
        for i in range(2):
            sp.wait_ge(s_ytok[i], 16 * TT // 2)
        sp.wait_ge(s_out, 16 * N_STORES[0])

    @block.gpsimd
    def _(pool):
        pool.wait_ge(s_idx, 1)
        pool.wait_ge(s_hlo, 2 * KT)
        pool.wait_ge(s_kst, 16)
        pool.wait_ge(s_vst, 16)
        pool.wait_ge(s_rs, 16 * HP)
        ck = cache_k[0].rearrange("n (a r) h d -> (n a) (r h d)", r=ROWS)
        for u in range(2):
            pool.indirect_dma_start(Kb[u][:, :], None, ck, bass.IndirectOffsetOnAxis(kidx[:, u:u + 1], 0)).then_inc(s_k[u], 16)
        with pool.Fori(1, NB_SEQ * NGRP // 2) as i:
            for u in range(2):
                pool.wait_ge(s_kt, 2 * i + u - 1)
                pool.tensor_copy(kix[u][:, :], kidx[:, bass.ds(2 * i + u, 1)])
                pool.drain()
                pool.indirect_dma_start(Kb[u][:, :], None, ck, bass.IndirectOffsetOnAxis(kix[u][:, :], 0)).then_inc(s_k[u], 16)

    def chunk_pair(base, i, j):
        return j // 2, 16 * (base + i + 1)

    @block.scalar
    def _(act):
        act.sem_inc(s_p, 2)
        act.sem_inc(s_pte, 2)
        act.wait_ge(s_c, 32)
        act.activation(crow[:, :], crow[:, :], ACT.Silu).then_inc(s_silu, 1)
        act.wait_ge(s_x, 16)
        for i in range(TT):
            act.activation(sq[:, :], xP[:, i, :], ACT.Square, accum_out=st[:, i:i + 1])
            act.drain()
        act.wait_ge(s_xs, 16)
        act.activation(sq[0:S, :], xs[:, :], ACT.Square, accum_out=st[0:S, 4:5]).then_inc(s_sqd, 1)
        act.wait_ge(s_rin, 1)
        act.activation(st2[:, 0:4], st2[:, 8:12], ACT.Sqrt)
        act.activation(st2[0:S, 4:5], st2[0:S, 12:13], ACT.Sqrt)
        act.drain()
        for i in range(TT):
            last = act.activation(xP[:, i, :], xP[:, i, :], ACT.Copy, scale=st2[:, i:i + 1])
        last.then_inc(s_xn, 1)
        act.activation(sq[0:S, :], xs[:, :], ACT.Copy, scale=st2[0:S, 4:5]).then_inc(s_xsn, 1)
        act.wait_ge(s_mt, 1)

        def stage_hi(k, n):
            act.wait_ge(s_stg, n + 1)
            act.activation(ahi[:, k, :], stage[k % 2][:, :], ACT.Copy).then_inc(s_hhi, 1)

        for k in range(KT):
            act.wait_ge(s_xt, k + 1)
            if k >= 2:
                act.wait_ge(s_hlo, k - 1)
            act.activation(stage[k % 2][:, :], bank[2 + k % 2][:, :], ACT.Identity,
                           scale=gain[:, k, NB_SEQ:NSEQ], bias=mT[:, k, NB_SEQ:NSEQ]).then_inc(s_stg, 1)
            stage_hi(k, k)

        def split_hi(m, q, kd=KT):
            act.wait_ge(s_ft, m + 1)
            act.activation(whi[q % 2][:, 0:kd, :], raw[q // 2][:, 0:kd, q % 2 * P:(q % 2 + 1) * P], ACT.Copy).then_inc(s_hi, 1)

        def stage_pairs(F, B, pairs, loads, evict):
            act.wait_ge(s_w[0], loads(0))
            split_hi(F, 0)

            def body(i, last):
                for q in range(4):
                    if not (last and q == 3):
                        n = (q + 1) % 4
                        if n % 2 == 0:
                            act.wait_ge(s_w[n // 2], loads(i + (n == 0)))
                        split_hi(F + 4 * i + q + 1, n)
                    if evict:
                        evict(i, q)

            if pairs > 1:
                with act.Fori(0, pairs - 1) as i:
                    body(i, False)
            body(pairs - 1, True)

        def evict_z(i, q):
            act.wait_ge(s_ft, 4 * i + q + 3)
            act.activation(zT[:, bass.ds(4 * i + q, 1), :].rearrange("p a t -> p (a t)"), bank[q % 2][:, :], ACT.Copy).then_inc(s_ev, 1)

        stage_pairs(0, B_IN, NIN // 2, lambda i: 16 * (B_IN + i + 1), evict_z)

        act.wait_ge(s_kst, 16)
        with act.Fori(0, HP) as hp:
            act.wait_ge(s_on, 8 * hp + 2)
            act.activation(scr[:, 0, :], zT[:, bass.ds(MQ + hp, 1), :].rearrange("p a t -> p (a t)"), ACT.Copy)
            act.activation(scr[:, 1, :], zT[:, bass.ds(MK + hp, 1), :].rearrange("p a t -> p (a t)"), ACT.Copy).then_inc(s_qk, 1)

            def probs(u):
                n = (u % 4 + 1) * P
                act.wait_ge(s_nm, 8 * hp + u + 1)
                act.wait_ge(s_ptp, 8 * hp + u + 1)
                act.activation(scr[:, 2 + u % 2, 0:n], bank[u % 2][:, 0:n], ACT.Exp, scale=SCALE,
                               bias=st2[:, 20 + u % 2:21 + u % 2], accum_out=st[:, 16 + u:17 + u]).then_inc(s_p, 1)

            def probs_t(u):
                n = (u % 4 + 1) * P
                act.wait_ge(s_ptp, 8 * hp + u + 3)
                act.wait_ge(s_pv, 8 * hp + u + 1)
                act.activation(scr[:, 4 + u % 2, 0:n], bank[4 + u % 2][:, 0:n], ACT.Copy).then_inc(s_pte, 1)

            probs(0)
            for u in range(8):
                if u < 7:
                    probs(u + 1)
                probs_t(u)
        with act.Fori(0, HP) as hp:
            act.wait_ge(s_ro, hp + 1)
            for h2 in range(2):
                act.activation(rettok[:, :, bass.ds(hp * P + h2 * HD, HD)],
                               bank[6 + h2][:, 0:4 * HD].rearrange("p (c v) -> p c v", c=4), ACT.Copy).then_inc(s_roc, 1)
        act.wait_ge(s_hn, 1)
        act.activation(rvtok[:, :, :], rettok, ACT.Square)
        act.wait_ge(s_on, 8 * HP + 2)
        act.activation(mvtok[:, :, :], mobatok, ACT.Square).then_inc(s_hsq, 1)
        act.activation(zT[:, RG:RG + 4, :], zT[:, RG:RG + 4, :], ACT.Silu).then_inc(s_sg, 1)
        act.wait_ge(s_hri, 1)
        act.activation(gain[:, :, 0:8].rearrange("p a b -> p a b"), gain[:, :, 0:8], ACT.Sqrt).then_inc(s_hrs, 1)
        for k in range(KT):
            stage_hi(k, KT + k)

        act.wait_ge(s_srot, 1)
        act.activation(zs[:, 3 * W:4 * W], zs[:, 3 * W:4 * W], ACT.Silu).then_inc(s_ssg, 1)
        act.wait_ge(s_ssq, 1)
        act.activation(st2[0:S, 0:H], st2[0:S, 8:8 + H], ACT.Sqrt).then_inc(s_srs, 1)

        with act.Fori(0, NB_SEQ) as b:
            act.wait_ge(s_nb, b + 1)
            for g in range(NGRP):
                act.activation(pe_x[:, g, :].rearrange("p (a r) -> p r a", r=ROWS),
                               bank[g // 4][:, (g % 4) * P:(g % 4 + 1) * P].rearrange("p (r a) -> p r a", r=ROWS),
                               ACT.Exp, scale=SCALE, bias=sm[:, 320 + g:321 + g], accum_out=sm[:, 640 + g:641 + g])
            act.activation(sm[:, 576:608], sm[:, 512:544], ACT.Exp, scale=SCALE, bias=sm[:, 328:329],
                           accum_out=sm[:, 648:649]).then_inc(s_ex, 1)
            act.wait_ge(s_tp, b + 1)
            for n in range(4):
                last = act.activation(by_page(pT[:, n, :]), turned(bank[4][:, n * P:(n + 1) * P]), ACT.Copy)
            last.then_inc(s_te, 1)
        act.wait_ge(s_ofs, 1)
        act.activation(st2[0:32, 0:8], st2[0:32, 8:16], ACT.Sqrt).then_inc(s_ofq, 1)

        for k in range(KT):
            act.wait_ge(s_xt, 2 * KT + k + 1)
            act.activation(x2T[:, k, :], bank[2 + k % 2][:, :], ACT.Copy).then_inc(s_xr, 1)
        stage_pairs(F_OUT, B_OUT, 2, lambda i: 16 * (B_OUT + i + 1), None)
        act.wait_ge(s_ev, F_OUT + 8 + 2)
        for k in range(KT):
            if k >= 2:
                act.wait_ge(s_ssm, k - 1)
            act.activation(stage[k % 2][:, :], x2T[:, k, :], ACT.Square).then_inc(s_sqx, 1)
        act.wait_ge(s_x2s, 1)
        act.activation(xsn2[:, :], x2s[:, :], ACT.Square, accum_out=st[0:S, 0:1]).then_inc(s_x2q, 1)
        act.wait_ge(s_r1, 1)
        act.activation(rb[:, :], rb[:, :], ACT.Sqrt).then_inc(s_r2, 1)
        act.wait_ge(s_x2i, 1)
        act.activation(st2[0:S, 1:2], st2[0:S, 0:1], ACT.Sqrt)
        act.drain()
        act.activation(xsn2[:, :], x2s[:, :], ACT.Copy, scale=st2[0:S, 1:2]).then_inc(s_x2n, 1)
        for k in range(KT):
            act.wait_ge(s_nx, k + 1)
            act.activation(stage[k % 2][:, :], stage[k % 2][:, :], ACT.Identity,
                           scale=gain[:, k, NB_SEQ:NSEQ], bias=mT[:, 24 + k, NB_SEQ:NSEQ]).then_inc(s_stg, 1)
            stage_hi(k, 2 * KT + k)

        def evict_ffn(i, q):
            act.wait_ge(s_ft, F_FFN + 4 * i + q + 3)
            if q % 2 == 0:
                act.wait_ge(s_fl, 2 * i + q // 2)
                act.activation(stage[0][:, :], bank[0][:, :], ACT.Silu).then_inc(s_ev, 1)
            else:
                act.wait_ge(s_ev, F_FFN + 4 * i + q + 3)
                act.activation(fhi[:, bass.ds(2 * i + q // 2, 1), :].rearrange("p a t -> p (a t)"), stage[1][:, :], ACT.Copy).then_inc(s_fh, 1)
                act.wait_ge(s_ss, N_FFN + 2 * i + q // 2 + 1)
                act.wait_ge(s_smt, 2 * i + q // 2)
                act.activation(asm[0:64, 0:64], bank[4 + q // 2][0:64, 0:64], ACT.Silu).then_inc(s_ssl, 1)

        stage_pairs(F_FFN, B_FFN, FT // 2, lambda i: 16 * (B_FFN + 2 * i + 2), evict_ffn)
        c = 0
        for fb in range(DM // CHUNK):
            for n, kd in enumerate(KD):
                act.wait_ge(s_w[c % 2], 16 * (B_FFN + FT + c // 2 + 1))
                for half in range(2):
                    split_hi(F_DOWN + 2 * c + half, 2 * (c % 2) + half, kd)
                c += 1
        for i in range(TT + 1):
            n = P if i < TT else S
            if i < TT:
                act.wait_ge(s_yt, i + 1)
            else:
                act.wait_ge(s_x3, 1)
            y = ytok[i % 2][0:n, :] if i < TT else x2s[:, :]
            if i >= 2 and i < TT:
                act.wait_ge(s_ytok[i % 2], 16)
            if i < TT:
                for e in range(2):
                    act.activation(y[:, e * 512:(e + 1) * 512], bank[2 * (i % 2) + e][0:n, :], ACT.Square,
                                   accum_out=st[0:n, e:e + 1])
            else:
                act.activation(gmod2[:, :], x2s[:, :], ACT.Square, accum_out=st[0:n, 0:1])
            act.drain().then_inc(s_ysq, 1)
            act.wait_ge(s_yi, i + 1)
            act.activation(st2[0:n, 1:2], st2[0:n, 0:1], ACT.Sqrt).then_inc(s_yr, 1)

    @block.tensor
    def _(pe):
        for s in (s_ft, s_ptp, s_pv):
            pe.sem_inc(s, 2)
        pe.wait_ge(s_const, 16)
        pe.wait_ge(s_silu, 1)
        for k in range(KT):
            last = pe.transpose(bank[4][:, k * NSEQ:(k + 1) * NSEQ], crow[:, k * P:(k + 1) * P], ident[0:NSEQ, 0:NSEQ])
        last.then_inc(s_ctp, 1)
        pe.wait_ge(s_vec, 80)
        pe.transpose(bank[5][:, 0:NVEC], vrow[:, :], ident[0:NVEC, 0:NVEC]).then_inc(s_vtp, 1)
        pe.wait_ge(s_ct, 1)

        def mod_chunk(u, f):
            for half in range(2):
                at = (f + half) * NSEQ
                for k in range(KT):
                    last = pe.matmul(bank[6][:, bass.ds(at, NSEQ)], raw[u][:, k, half * P:(half + 1) * P], cT[:, k, :],
                                     start=(k == 0), stop=(k == KT - 1))
            last.then_inc(s_md, 1)

        with pe.Fori(0, NMA // 2) as i:
            for u in range(2):
                pe.wait_ge(s_w[u], 16 * (i + 1))
                mod_chunk(u, 4 * i + 2 * u)
        pe.wait_ge(s_xn, 1)

        def turn_rows(src, k, n):
            for i in range(TT):
                last = pe.transpose(bank[2 + k % 2][:, i * P:(i + 1) * P], src(i), ident)
            last.then_inc(s_xt, 1)

        for k in range(KT):
            if k >= 2:
                pe.wait_ge(s_stg, k - 1)
            turn_rows(lambda i: xP[:, i, k * P:(k + 1) * P], k, k)
        pe.wait_ge(s_xsn, 1)
        for k in range(KT):
            last = pe.transpose(bank[7][:, k * S:(k + 1) * S], sq[0:S, k * P:(k + 1) * P], ident[0:S, 0:S])
        last.then_inc(s_xst, 1)

        def tile(m, q, kd=KT, hi=None, lo=None, k0=0, out=None, first=True, final=True):
            hi, lo = (ahi, alo) if hi is None else (hi, lo)
            out = bank[q % 2] if out is None else out
            pe.wait_ge(s_lo, m + 1)
            for k in range(kd):
                pe.matmul(out[:, :], whi[q % 2][:, k, :], hi[:, k0 + k, :], start=(first and k == 0), stop=False)
                pe.matmul(out[:, :], whi[q % 2][:, k, :], lo[:, k0 + k, :], start=False, stop=False)
                last = pe.matmul(out[:, :], wlo[q % 2][:, k, :], hi[:, k0 + k, :], start=False, stop=(final and k == kd - 1))
            last.then_inc(s_ft, 1)

        def sample_chunk(u, n, lhs, kd=KT, first=True, final=True, out=None):
            out = bank[4 + u] if out is None else out
            for k in range(kd):
                for g in range(4):
                    last = pe.matmul(out[32 * g:32 * g + 32, 0:64], lhs(k), raw[u][:, k, 64 * g:64 * g + 64],
                                     start=(first and k == 0), stop=(final and k == kd - 1))
            last.then_inc(s_ss, 1)

        def stage_pairs(F, N, pairs, after=None):
            def body(i):
                for q in range(4):
                    pe.wait_ge(s_ev, F + 4 * i + q + 1)
                    tile(F + 4 * i + q, q)
                    if q % 2:
                        pe.wait_ge(s_sev, N + 2 * i + q // 2 + 1)
                        sample_chunk(q // 2, N, lambda k: asT[:, k, :])
                        if after:
                            after(i, q // 2)
            with pe.Fori(0, pairs) as i:
                body(i)

        pe.wait_ge(s_hlo, KT)
        pe.wait_ge(s_hs, 1)
        stage_pairs(0, 0, NIN // 2)
        with pe.Fori(0, NMB // 2) as i:
            for u in range(2):
                pe.wait_ge(s_w[u], 16 * (B_MODB + i + 1))
                mod_chunk(u, 2 * NMA + 4 * i + 2 * u)
        pe.wait_ge(s_ev, 2 * NIN + 2)
        n = 0
        for sec in (MK, MV, RV):
            for j in range(4):
                if n >= 2:
                    pe.wait_ge(s_vt2, n - 1)
                for i in range(TT):
                    last = pe.transpose(bank[2 + n % 2][:, i * P:(i + 1) * P], zT[:, sec + j, i * P:(i + 1) * P], ident)
                last.then_inc(s_vt1, 1)
                n += 1
        pe.wait_ge(s_vt2, 12)
        with pe.Fori(0, HP) as hp:
            pe.wait_ge(s_qk, hp + 1)

            def scores(u):
                r, n = 64 * (u // 4), (u % 4 + 1) * P
                pe.wait_ge(s_p, 8 * hp + u + 1)
                pe.matmul(bank[u % 2][:, 0:n], scr[r:r + 64, 0, n - P:n], scr[r:r + 64, 1, 0:n],
                          start=True, stop=True).then_inc(s_sc, 1)

            def turn(u):
                pe.wait_ge(s_p, 8 * hp + u + 3)
                pe.wait_ge(s_pte, 8 * hp + u + 1)
                for j in range(u % 4 + 1):
                    last = pe.transpose(bank[4 + u % 2][:, j * P:(j + 1) * P], scr[:, 2 + u % 2, j * P:(j + 1) * P], ident)
                last.then_inc(s_ptp, 1)

            def weigh(u):
                pe.wait_ge(s_pte, 8 * hp + u + 3)
                pe.wait_ge(s_on, 8 * hp + u + 1)
                for j in range(u % 4 + 1):
                    last = pe.matmul(bank[6 + u % 2][:, 0:HD], scr[:, 4 + u % 2, j * P:(j + 1) * P],
                                     mvtok[:, j, bass.ds(hp * P + (u // 4) * HD, HD)], start=(j == 0), stop=(j == u % 4))
                last.then_inc(s_pv, 1)

            scores(0)
            for u in range(8):
                if u < 7:
                    scores(u + 1)
                turn(u)
                if u >= 1:
                    weigh(u - 1)
            weigh(7)
        pe.wait_ge(s_on, 8 * HP + 2)
        with pe.Fori(0, HP) as hp:
            for n, sec in enumerate((RQ, RK)):
                pe.matmul(bank[n][:, :], C("rot"), zT[:, bass.ds(sec + hp, 1), :].rearrange("p a t -> p (a t)"),
                          start=True, stop=True).then_inc(s_rr, 1)
            pe.wait_ge(s_rk, hp + 1)
            for c in range(TT):
                last = pe.transpose(bank[2][:, c * P:(c + 1) * P], scr[:, 1, c * P:(c + 1) * P], ident)
            last.then_inc(s_kt1, 1)
            for h2 in range(2):
                r = 64 * h2
                for c in range(TT):
                    last = pe.matmul(bank[4 + h2][:, c * P:(c + 1) * P], scr[r:r + 64, 1, c * P:(c + 1) * P],
                                     scr[r:r + 64, 0, c * P:(c + 1) * P], start=True, stop=True)
            last.then_inc(s_ra, 1)
            pe.wait_ge(s_kt2, hp + 1)
            for c in range(TT):
                last = pe.matmul(bank[3][:, c * P:(c + 1) * P], scr[:, 4, c * P:(c + 1) * P],
                                 rvtok[:, c, bass.ds(hp * P, P)], start=True, stop=True)
            last.then_inc(s_kv, 1)
            pe.wait_ge(s_rad, hp + 1)
            pe.wait_ge(s_st, hp + 1)
            pe.wait_ge(s_roc, 2 * hp)
            for h2 in range(2):
                r = 64 * h2
                for c in range(TT):
                    last = pe.matmul(bank[6 + h2][:, c * HD:(c + 1) * HD], scr[:, 5 + h2, c * P:(c + 1) * P],
                                     rvtok[:, c, bass.ds(hp * P + r, HD)], start=True, stop=(c == 0))
                    if c:
                        last = pe.matmul(bank[6 + h2][:, c * HD:(c + 1) * HD], scr[r:r + 64, 2, c * P:(c + 1) * P],
                                         sst[r:r + 64, c - 1, :], start=False, stop=True)
            last.then_inc(s_ro, 1)
        pe.wait_ge(s_hn, 2)
        for k in range(KT):
            src = rettok if k < 4 else mobatok
            if k >= 2:
                pe.wait_ge(s_stg, KT + k - 1)
            turn_rows(lambda i: src[:, i, (k % 4) * P:(k % 4 + 1) * P], k, KT + k)

        pe.wait_ge(s_srot, 1)
        for n, x in enumerate((qrs, krs)):
            for hp in range(HP):
                last = pe.transpose(bank[0][:, (n * HP + hp) * S:(n * HP + hp + 1) * S], x[:, hp * P:(hp + 1) * P], ident[0:S, 0:S])
        last.then_inc(s_sqt, 1)
        pe.wait_ge(s_sqe, 1)
        for h2 in range(2):
            r = 64 * h2
            for hp in range(HP):
                last = pe.matmul(bank[4 + h2][0:S, hp * S:(hp + 1) * S], sT[r:r + 64, 1, hp, :], sT[r:r + 64, 0, hp, :],
                                 start=True, stop=True)
        last.then_inc(s_sa, 1)
        pe.wait_ge(s_sad, 1)
        pe.wait_ge(s_state, 16)
        for h2 in range(2):
            r = 64 * h2
            for hp in range(HP):
                at = 2 * W + (2 * hp + h2) * HD
                pe.matmul(bank[6 + h2][r:r + 64, hp * S:(hp + 1) * S], zs[:, at:at + HD], ats[:, 2 * hp + h2, :],
                          start=True, stop=False, skip_group_check=True)
                for b in range(NB_SEQ):
                    last = pe.matmul(bank[6 + h2][r:r + 64, hp * S + TS * b:hp * S + TS * (b + 1)],
                                     state[r:r + 64, b, hp, :], sT[r:r + 64, 2, hp, TS * b:TS * (b + 1)],
                                     start=False, stop=(b == NB_SEQ - 1), skip_group_check=True)
        last.then_inc(s_so, 1)
        pe.wait_ge(s_soc, 1)
        for hp in range(HP):
            last = pe.transpose(bank[0][0:S, hp * P:(hp + 1) * P], sT[:, 0, :, :].rearrange("p a b -> p (a b)")[:, hp * S:(hp + 1) * S], ident)
        last.then_inc(s_sot, 1)
        for b in range(NB_SEQ):
            pe.wait_ge(s_km, b + 1)
            if b >= 2:
                pe.wait_ge(s_sts, b - 1)
            for hp in range(HP):
                last = pe.matmul(bank[2 + b % 2][:, hp * P:(hp + 1) * P], kmask[b % 2][:, hp * P:(hp + 1) * P],
                                 zs[:, 2 * W + hp * P:2 * W + (hp + 1) * P], start=True, stop=True)
            last.then_inc(s_kvs, 1)
        pe.wait_ge(s_srn, 1)
        for hp in range(HP):
            last = pe.transpose(bank[1][:, hp * S:(hp + 1) * S], ret_s[:, hp * P:(hp + 1) * P], ident[0:S, 0:S])
        last.then_inc(s_srt, 1)
        pe.wait_ge(s_sas, 1)

        with pe.Fori(0, NB_SEQ) as b:
            pe.wait_ge(s_qd, b + 1)
            for g in range(NGRP):
                pe.wait_ge(s_kt, NGRP * b + g + 1)
                for jj in range(4):
                    for gq in range(4):
                        j = 4 * gq + jj
                        last = pe.matmul(bank[g // 4][32 * gq:32 * gq + 32, (g % 4) * P:(g % 4 + 1) * P],
                                         qbd[:, j, :], KTb[g % 2][:, :, j, :], start=(jj == 0), stop=(jj == 3))
                last.then_inc(s_lg, 1)
            for jj in range(4):
                for gq in range(4):
                    j = 4 * gq + jj
                    last = pe.matmul(bank[2][32 * gq:32 * gq + 32, 0:S], qbd[0:32, j, :], kbb[0:32, j, :],
                                     start=(jj == 0), stop=(jj == 3))
            last.then_inc(s_own, 1)
            pe.wait_ge(s_s1, b + 1)
            for n, name in enumerate(("pair0", "pair1", "own_pair")):
                last = pe.matmul(bank[3][:, n * NGRP:(n + 1) * NGRP], C(name), sm[:, 0:NGRP], start=True, stop=True)
            last.then_inc(s_gt, 1)
            pe.wait_ge(s_mx, b + 1)
            pe.transpose(bank[6][0:1, 0:P], sm[:, 56:57], ident).then_inc(s_mxt, 1)
            pe.wait_ge(s_rm, b + 1)
            pe.matmul(bank[3][:, 0:1], sm[0:1, 384:512], ones[0:1, 0:1], start=True, stop=True).then_inc(s_mb, 1)
            pe.wait_ge(s_ex, b + 1)
            for g in range(NGRP):
                pe.transpose(bank[4 + g // 4][:, (g % 4) * P:(g % 4 + 1) * P], pe_x[:, g, :], ident)
            pe.transpose(bank[6][0:S, 0:P], sm[:, 576:608], ident).then_inc(s_tp, 1)
            pe.wait_ge(s_rsm, b + 1)
            pe.matmul(bank[3][0:32, 0:1], C("sum_g"), sm[:, 650:651], start=True, stop=True).then_inc(s_den, 1)
            pe.wait_ge(s_te, 2 * b + 2)
            for g in range(NGRP):
                for pg in range(GRP):
                    s = (4 * g + pg) % 8
                    pe.wait_ge(s_v[s], 16 * (4 * b + (4 * g + pg) // 8 + 1))
                    pe.matmul(bank[7][32 * pg:32 * pg + 32, :], pT[:, g, 32 * pg:32 * pg + 32],
                              VB[s][:, :], start=(g == 0), stop=(g == NGRP - 1 and pg > 0)).then_inc(s_vd, 1)
            pe.matmul(bank[7][0:32, :], sm[0:S, 704:736],
                      zs[:, 6 * W:7 * W], start=False, stop=True).then_inc(s_od, 1)
            pe.wait_ge(s_of, b + 1)
            pe.matmul(bank[2][0:32, 0:HD], C("sum_pv"), sm[:, 832:896], start=True, stop=True).then_inc(s_oe, 1)
        pe.wait_ge(s_ofr, 1)
        for b in range(NB_SEQ):
            last = pe.transpose(bank[0][0:HD, b * 32:(b + 1) * 32], oall[:, b, :], ident[0:32, 0:32])
        last.then_inc(s_oft, 1)

        pe.wait_ge(s_x2l, 16)
        for k in range(KT):
            if k >= 2:
                pe.wait_ge(s_xr, k - 1)
            turn_rows(lambda i: xP2[:, i, k * P:(k + 1) * P], k, 2 * KT + k)

        def gates_to_rows(n):
            pe.wait_ge(s_hs, 2 + 2 * n)
            for k in range(KT):
                last = pe.transpose(bank[6 + k // 4][0:S, (k % 4) * P:(k % 4 + 1) * P], asm[:, k * S:(k + 1) * S], ident)
            last.then_inc(s_gmt, 1)

        gates_to_rows(0)
        pe.wait_ge(s_hlo, 2 * KT)
        pe.wait_ge(s_oas, 1)
        stage_pairs(F_OUT, N_OUT, 2)
        for k in range(KT):
            pe.wait_ge(s_sqx, k + 1)
            pe.matmul(bank[2][:, :], ones, stage[k % 2][:, :], start=(k == 0), stop=(k == KT - 1)).then_inc(s_ssm, 1)
        pe.wait_ge(s_x2n, 1)
        for k in range(KT):
            last = pe.transpose(bank[7][:, k * S:(k + 1) * S], xsn2[:, k * P:(k + 1) * P], ident[0:S, 0:S])
        last.then_inc(s_xst, 1)
        pe.wait_ge(s_hlo, 3 * KT)
        pe.wait_ge(s_hs, 3)

        def turn_ff(i, u):
            pe.wait_ge(s_sev, N_FFN + 2 * i + u + 3)
            pe.transpose(bank[7][:, 0:P], asm[:, 64:192], ident).then_inc(s_smt, 1)

        stage_pairs(F_FFN, N_FFN, FT // 2, turn_ff)
        gates_to_rows(1)
        pe.wait_ge(s_fl, FT)
        pe.wait_ge(s_sme, FT)
        c = 0
        for fb in range(DM // CHUNK):
            for n, kd in enumerate(KD):
                for half in range(2):
                    if n == 0:
                        pe.wait_ge(s_ev, F_DOWN + 2 * fb + half + 1)
                    tile(F_DOWN + 2 * c + half, half, kd, fhi, flo, 8 * n, bank[2 * (fb % 2) + half], n == 0, n == 2)
                if n == 0:
                    pe.wait_ge(s_sev, N_DOWN + fb + 1)
                sample_chunk(c % 2, 0, lambda k: aT[:, 8 * n + k, :], kd, n == 0, n == 2, bank[4 + fb % 2])
                c += 1
        pe.wait_ge(s_ev, F_DOWN + 8 + 2)
        for i in range(TT):
            if i >= 2:
                pe.wait_ge(s_y, i - 1)
            for k in range(KT):
                last = pe.transpose(bank[2 * (i % 2) + k // 4][:, (k % 4) * P:(k % 4 + 1) * P], x2T[:, k, i * P:(i + 1) * P], ident)
            last.then_inc(s_yt, 1)

    @block.vector
    def _(dve):
        tt, ts, cp = dve.tensor_tensor, dve.tensor_scalar, dve.tensor_copy
        for s in (s_ev, s_sev, s_on):
            dve.sem_inc(s, 2)

        def then(ins):
            dve.drain()
            return ins

        dve.wait_ge(s_ctp, 1)
        cp(cT[:, :, :], bank[4][:, 0:KT * NSEQ].rearrange("p (k s) -> p k s", k=KT)).then_inc(s_ct, 1)
        dve.wait_ge(s_vtp, 1)
        then(cp(vT[:, :], bank[5][:, 0:NVEC]))
        dve.wait_ge(s_pt, 16)
        for g in range(GRP):
            q = slice(32 * g, 32 * g + 32)
            last = ts(kidx[q, :], pt[q, :].rearrange("p (n g) -> p n g", g=GRP)[:, :, g], 32.0, C("row32")[q, :], ALU.mult, ALU.add)
        last.then_inc(s_idx, 1)
        dve.wait_ge(s_sqd, 1)
        ts(st2[:, 8:12], st[:, 0:4], 1.0 / DM, EPS, ALU.mult, ALU.add)
        then(ts(st2[0:S, 12:13], st[0:S, 4:5], 1.0 / DM, EPS, ALU.mult, ALU.add))
        dve.reciprocal(st2[:, 8:12], st2[:, 8:12])
        dve.reciprocal(st2[0:S, 12:13], st2[0:S, 12:13])
        dve.drain().then_inc(s_rin, 1)

        def modulation(f0, n):
            then(tt(mT[:, f0:f0 + n, :], bank[6][:, f0 * NSEQ:(f0 + n) * NSEQ].rearrange("p (f s) -> p f s", f=n),
                    vT[:, f0:f0 + n].unsqueeze(2).broadcast_to((P, n, NSEQ)), ALU.add))

        def gains(f0, v0):
            dve.scalar_tensor_tensor(gain[:, :, :], mT[:, f0:f0 + KT, :], 1.0,
                                     vT[:, v0:v0 + KT].unsqueeze(2).broadcast_to((P, KT, NSEQ)), ALU.add, ALU.mult)
            dve.drain().then_inc(s_mt, 1)

        dve.wait_ge(s_md, NMA)
        modulation(0, 16)
        gains(8, V_N1)

        def act_lo(k, n):
            dve.wait_ge(s_hhi, n + 1)
            tt(alo[:, k, :], stage[k % 2][:, :], ahi[:, k, :].bitcast(F32), ALU.subtract).then_inc(s_hlo, 1)

        for k in range(KT):
            act_lo(k, k)

        def by_seq(x):
            return x.unsqueeze(3).broadcast_to((P, KT, NB_SEQ, TS))

        asT4 = asT[:, :, :].rearrange("p k (b t) -> p k b t", t=TS)

        def sample_h(n, f_shift):
            dve.wait_ge(s_xst, n)
            then(tt(asT4, bank[7][:, 0:KT * S].rearrange("p (k b t) -> p k b t", k=KT, t=TS), by_seq(gain[:, :, 0:NB_SEQ]), ALU.mult))
            tt(asT4, asT4, by_seq(mT[:, f_shift:f_shift + KT, 0:NB_SEQ]), ALU.add).then_inc(s_hs, 1)

        sample_h(1, 0)

        def split_lo(m, q, kd=KT):
            dve.wait_ge(s_hi, m + 1)
            tt(wlo[q % 2][:, 0:kd, :], raw[q // 2][:, 0:kd, q % 2 * P:(q % 2 + 1) * P],
               whi[q % 2][:, 0:kd, :].bitcast(F32), ALU.subtract).then_inc(s_lo, 1)

        def stage_pairs(F, pairs, evict, sample):
            split_lo(F, 0)

            def body(i, last):
                for q in range(4):
                    if not (last and q == 3):
                        split_lo(F + 4 * i + q + 1, (q + 1) % 4)
                    if evict:
                        evict(i, q)
                    if q % 2:
                        sample(i, q // 2)

            if pairs > 1:
                with dve.Fori(0, pairs - 1) as i:
                    body(i, False)
            body(pairs - 1, True)

        def sample_z(i, u):
            dve.wait_ge(s_ss, 2 * i + u + 1)
            for g in range(4):
                last = cp(zs[:, bass.ds((2 * i + u) * CHUNK + 64 * g, 64)], bank[4 + u][32 * g:32 * g + 32, 0:64])
            last.then_inc(s_sev, 1)

        stage_pairs(0, NIN // 2, None, sample_z)
        dve.wait_ge(s_md, NMOD)
        modulation(16, 32)
        n = 0
        for dst in (scr, mvtok, rvtok):
            for j in range(4):
                dve.wait_ge(s_vt1, n + 1)
                cp(dst[:, 0:4, j * P:(j + 1) * P], bank[2 + n % 2][:, :].rearrange("p (i f) -> p i f", i=TT)).then_inc(s_vt2, 1)
                n += 1
        with dve.Fori(0, HP) as hp:
            def negmax(u):
                n = (u % 4 + 1) * P
                dve.wait_ge(s_sc, 8 * hp + u + 1)
                then(tt(bank[u % 2][:, n - P:n], bank[u % 2][:, n - P:n], C("causal"), ALU.add))
                then(dve.tensor_reduce(st2[:, 16 + u % 2:17 + u % 2], bank[u % 2][:, 0:n], AX.X, ALU.max))
                ts(st2[:, 20 + u % 2:21 + u % 2], st2[:, 16 + u % 2:17 + u % 2], -SCALE, None, ALU.mult).then_inc(s_nm, 1)

            def norm(u):
                dve.wait_ge(s_pv, 8 * hp + u + 3)
                then(dve.reciprocal(st2[:, 24 + u % 2:25 + u % 2], st[:, 16 + u:17 + u]))
                ts(mobatok[:, u % 4, bass.ds(hp * P + (u // 4) * HD, HD)], bank[6 + u % 2][:, 0:HD],
                   st2[:, 24 + u % 2:25 + u % 2], None, ALU.mult).then_inc(s_on, 1)

            for u in range(8):
                negmax(u)
                if u >= 2:
                    norm(u - 2)
            norm(6)
            norm(7)
        dec3 = C("decay")
        with dve.Fori(0, HP) as hp:
            for n, (sec, done) in enumerate(((RQ, s_rq), (RK, s_rk))):
                dve.wait_ge(s_rr, 2 * hp + n + 1)
                tt(scr[:, 3, :], zT[:, bass.ds(sec + hp, 1), :].rearrange("p a t -> p (a t)"), C("cos"), ALU.mult)
                then(tt(stage[0][:, :], bank[n][:, :], C("sin"), ALU.mult))
                then(tt(scr[:, n, :], scr[:, 3, :], stage[0][:, :], ALU.add))
                if n == 0:
                    then(tt(scr[:, 2, :].rearrange("p (c i) -> p c i", c=4), scr[:, 0, :].rearrange("p (c i) -> p c i", c=4),
                            C("q_dec")[:, bass.ds(hp, 1), :].broadcast_to((P, 4, P)), ALU.mult))
                dve.drain().then_inc(done, 1)
            dve.wait_ge(s_kt1, hp + 1)
            tt(scr[:, 4, :].rearrange("p (c h d) -> p c h d", c=4, h=2), bank[2][:, :].rearrange("p (c h d) -> p c h d", c=4, h=2),
               C("k_dec")[:, bass.ds(2 * hp, 2)].unsqueeze(1).unsqueeze(3).broadcast_to((P, 4, 2, HD)), ALU.mult).then_inc(s_kt2, 1)
            dve.wait_ge(s_ra, hp + 1)
            for h2 in range(2):
                last = tt(scr[:, 5 + h2, :].rearrange("p (c i) -> p c i", c=4), bank[4 + h2][:, :].rearrange("p (c i) -> p c i", c=4),
                          dec3[:, bass.ds(2 * hp + h2, 1), :].broadcast_to((P, 4, P)), ALU.mult)
            last.then_inc(s_rad, 1)
            dve.wait_ge(s_kv, hp + 1)
            dve.wait_ge(s_rs, 16 * hp)
            for c in range(TT):
                for h2 in range(2):
                    r = 64 * h2
                    kv = bank[3][r:r + 64, c * P + r:c * P + r + HD]
                    if c == 0:
                        cp(sst[r:r + 64, 0, :], kv)
                    else:
                        dve.scalar_tensor_tensor(sst[r:r + 64, c, :], sst[r:r + 64, c - 1, :],
                                                 C("c_dec")[r:r + 64, bass.ds(hp, 1)], kv, ALU.mult, ALU.add)
                if c < TT - 1:
                    dve.drain()
                else:
                    dve.drain().then_inc(s_st, 1)
            dve.wait_ge(s_ro, hp + 1)
        dve.wait_ge(s_roc, 2 * HP)
        heads = lambda x: x.rearrange("p i (h d) -> p i h d", h=H)
        s1 = gain[:, 0:4, 0:8]
        s2 = gain[:, 4:8, 0:8]
        spread = lambda x: x.unsqueeze(3).broadcast_to((P, TT, H, HD))
        then(dve.tensor_reduce(s1, heads(rettok), AX.X, ALU.add))
        then(ts(s1, s1, 1.0 / HD, None, ALU.mult))
        tt(heads(rettok), heads(rettok), spread(s1), ALU.subtract).then_inc(s_hn, 1)
        dve.wait_ge(s_hsq, 1)
        dve.drain()
        dve.tensor_reduce(s1, heads(rvtok[:, :, :]), AX.X, ALU.add)
        then(dve.tensor_reduce(s2, heads(mvtok[:, :, :]), AX.X, ALU.add))
        both = gain[:, :, 0:8]
        then(ts(both, both, 1.0 / HD, EPS, ALU.mult, ALU.add))
        dve.reciprocal(both, both).then_inc(s_hri, 1)
        dve.wait_ge(s_hrs, 1)
        tt(heads(rettok), heads(rettok), spread(s1), ALU.mult)
        tt(heads(mobatok), heads(mobatok), spread(s2), ALU.mult).then_inc(s_hn, 1)
        dve.wait_ge(s_sg, 1)
        for k in range(KT):
            dve.wait_ge(s_xt, KT + k + 1)
            if k < 4:
                dve.scalar_tensor_tensor(stage[k % 2][:, :], bank[2 + k % 2][:, :], vT[:, V_GN + k:V_GN + k + 1],
                                         zT[:, RG + k, :], ALU.mult, ALU.mult).then_inc(s_stg, 1)
            else:
                ts(stage[k % 2][:, :], bank[2 + k % 2][:, :], vT[:, V_MN + k - 4:V_MN + k - 3], None, ALU.mult).then_inc(s_stg, 1)
            act_lo(k, KT + k)
            dve.drain()

        dve.wait_ge(s_kst, 16)
        dve.wait_ge(s_vst, 16)
        dve.wait_ge(s_rs, 16 * HP)
        cos = C("cos_s").unsqueeze(1).broadcast_to((S, H, 32))
        sin = C("sin_s").unsqueeze(1).broadcast_to((S, H, 32))
        ta = kmask[0][:, 0:256].rearrange("p (h d) -> p h d", h=H)
        tb = kmask[1][:, 0:256].rearrange("p (h d) -> p h d", h=H)
        for n, dst in enumerate((qrs, krs)):
            z = zs[:, n * W:(n + 1) * W].rearrange("p (h c d) -> p h c d", h=H, c=2)
            o = dst[:, :].rearrange("p (h c d) -> p h c d", h=H, c=2)
            tt(ta, z[:, :, 0, :], cos, ALU.mult)
            then(tt(tb, z[:, :, 1, :], sin, ALU.mult))
            then(tt(o[:, :, 0, :], ta, tb, ALU.subtract))
            tt(ta, z[:, :, 1, :], cos, ALU.mult)
            then(tt(tb, z[:, :, 0, :], sin, ALU.mult))
            then(tt(o[:, :, 1, :], ta, tb, ALU.add))
        dve.drain().then_inc(s_srot, 1)
        dve.wait_ge(s_sqt, 1)
        cp(sT[:, 0, :, :], bank[0][:, 0:P].rearrange("p (h s) -> p h s", h=HP))
        then(cp(sT[:, 1, :, :], bank[0][:, P:2 * P].rearrange("p (h s) -> p h s", h=HP)))
        tt(sT[:, 2, :, :], sT[:, 0, :, :], C("q_dec_s"), ALU.mult).then_inc(s_sqe, 1)
        dve.wait_ge(s_sa, 1)
        byh2 = lambda x: x.rearrange("p (hp h2) s -> p h2 hp s", h2=2)
        for h2 in range(2):
            last = tt(byh2(ats[:, :, :])[:, h2], bank[4 + h2][0:S, 0:P].rearrange("p (h s) -> p h s", h=HP),
                      byh2(C("decay_s"))[:, h2], ALU.mult)
        last.then_inc(s_sad, 1)
        dve.wait_ge(s_so, 1)
        for h2 in range(2):
            r = 64 * h2
            last = cp(sT[r:r + 64, 0, :, :], bank[6 + h2][r:r + 64, 0:P].rearrange("p (h s) -> p h s", h=HP))
        last.then_inc(s_soc, 1)
        cd = C("c_dec_s").unsqueeze(1).unsqueeze(3).broadcast_to((P, NB_SEQ, HP, HD))
        then(tt(state[:, :, :, :], state[:, :, :, :], cd, ALU.mult))

        def masked_k(b):
            if b >= 2:
                dve.wait_ge(s_kvs, b - 1)
            tt(kmask[b % 2][:, :].rearrange("p (h d) -> p h d", h=H), krs[:, :].rearrange("p (h d) -> p h d", h=H),
               C("k_dec_s")[:, b, :].unsqueeze(2).broadcast_to((S, H, HD)), ALU.mult).then_inc(s_km, 1)

        masked_k(0)
        for b in range(NB_SEQ):
            if b < NB_SEQ - 1:
                masked_k(b + 1)
            dve.wait_ge(s_kvs, b + 1)
            for h2 in range(2):
                r = 64 * h2
                last = tt(state[r:r + 64, b, :, :], state[r:r + 64, b, :, :],
                          bank[2 + b % 2][r:r + 64, :].rearrange("p (h c) -> p h c", h=HP)[:, :, r:r + HD], ALU.add)
            last.then_inc(s_sts, 1)
        dve.wait_ge(s_sot, 1)
        dve.wait_ge(s_ssg, 1)
        r3 = ret_s[:, :].rearrange("p (h d) -> p h d", h=H)
        k3 = kmask[0][:, :].rearrange("p (h d) -> p h d", h=H)
        sp3 = lambda x: x.unsqueeze(2).broadcast_to((S, H, HD))
        dve.drain()
        dve.wait_ge(s_kvs, NB_SEQ)
        then(dve.tensor_reduce(st[0:S, 0:H], bank[0][0:S, :].rearrange("p (h d) -> p h d", h=H), AX.X, ALU.add))
        then(ts(st[0:S, 0:H], st[0:S, 0:H], 1.0 / HD, None, ALU.mult))
        then(tt(r3, bank[0][0:S, :].rearrange("p (h d) -> p h d", h=H), sp3(st[0:S, 0:H]), ALU.subtract))
        then(tt(k3, r3, r3, ALU.mult))
        then(dve.tensor_reduce(st[0:S, 8:8 + H], k3, AX.X, ALU.add))
        then(ts(st2[0:S, 8:8 + H], st[0:S, 8:8 + H], 1.0 / HD, EPS, ALU.mult, ALU.add))
        dve.reciprocal(st2[0:S, 8:8 + H], st2[0:S, 8:8 + H]).then_inc(s_ssq, 1)
        dve.wait_ge(s_srs, 1)
        then(tt(r3, r3, sp3(st2[0:S, 0:H]), ALU.mult))
        tt(ret_s[:, :], ret_s[:, :], zs[:, 3 * W:4 * W], ALU.mult).then_inc(s_srn, 1)
        dve.wait_ge(s_srt, 1)
        tt(asT[:, 0:4, :], bank[1][:, 0:P].rearrange("p (h s) -> p h s", h=HP),
           vT[:, V_GN:V_GN + 4].unsqueeze(2).broadcast_to((P, HP, S)), ALU.mult).then_inc(s_sas, 1)

        dve.transpose(qbb[0:32, :, :], zs[:, 4 * W:5 * W])
        dve.transpose(kbb[0:32, :, :], zs[:, 5 * W:6 * W])
        then(dve.memset(qbd[:, :, :], 0.0))
        with dve.Fori(0, NB_SEQ) as b:
            dve.wait_ge(s_own, b)
            qv = qbd[:, :, :].rearrange("p (g hh half) c -> p g hh half c", g=4, hh=2)
            qi = qbb[0:32, :, :].rearrange("p (g hh half) s -> p g hh half s", g=4, hh=2)
            for pg in range(GRP):
                for hh in range(2):
                    last = cp(qv[32 * pg:32 * pg + 32, :, hh, :, hh * 16 + pg * 4:hh * 16 + pg * 4 + 4],
                              qi[:, :, hh, :, bass.ds(TS * b, TS)])
            last.then_inc(s_qd, 1)
            for g in range(NGRP):
                dve.wait_ge(s_k[g % 2], 16 * (NGRP // 2 * b + g // 2 + 1))
                if g >= 2:
                    dve.wait_ge(s_lg, NGRP * b + g - 1)
                else:
                    dve.wait_ge(s_lg, NGRP * b)
                dve.transpose(KTb[g % 2][:, :, :, :], Kb[g % 2][:, :]).then_inc(s_kt, 1)
            dve.wait_ge(s_own, b + 1)
            for e in range(2):
                lg = bank[e][:, :].rearrange("p (g c) -> p g c", g=4)
                dve.tensor_reduce(sm[:, 4 * e:4 * e + 4], lg, AX.X, ALU.add)
                last = dve.tensor_reduce(sm[:, 8 + 4 * e:12 + 4 * e], lg, AX.X, ALU.max)
            dve.drain().then_inc(s_s1, 1)
            tt(sm[:, 512:544], bank[2][:, 0:S], C("own_mask")[:, bass.ds(b, 1), :].rearrange("p a s -> p (a s)"), ALU.add)
            dve.wait_ge(s_gt, b + 1)
            cp(sm[:, 16:32].rearrange("p (g e) -> p e g", e=2), bank[3][:, 0:16].rearrange("p (e g) -> p e g", e=2))
            then(cp(sm[:, 32:40], bank[3][:, 16:24]))
            gall = sm[:, 16:32].unsqueeze(1).broadcast_to((P, NGRP, NBLK))
            gown = sm[:, 32:40].unsqueeze(2).broadcast_to((P, NGRP, NBLK))
            gt = sm[:, 64:192].rearrange("p (n m) -> p n m", n=NGRP)
            eq = sm[:, 192:320].rearrange("p (n m) -> p n m", n=NGRP)
            tt(gt, gall, gown, ALU.is_gt)
            then(tt(eq, gall, gown, ALU.is_equal))
            then(tt(eq, eq, C("earlier"), ALU.mult))
            then(tt(gt, gt, eq, ALU.add))
            then(dve.tensor_reduce(sm[:, 40:48], gt, AX.X, ALU.add))
            then(ts(sm[:, 48:56], sm[:, 40:48], TOPK - 0.5, -BIG, ALU.is_gt, ALU.mult))
            then(tt(sm[:, 8:16], sm[:, 8:16], sm[:, 48:56], ALU.add))
            dve.tensor_reduce(sm[:, 57:58], sm[:, 8:16], AX.X, ALU.max)
            then(dve.tensor_reduce(sm[:, 58:59], sm[:, 512:544], AX.X, ALU.max))
            tt(sm[:, 56:57], sm[:, 57:58], sm[:, 58:59], ALU.max).then_inc(s_mx, 1)
            dve.wait_ge(s_mxt, b + 1)
            then(dve.tensor_reduce(sm[0:1, 900:932], bank[6][0:1, 0:P].rearrange("p (h g t) -> p h t g", g=4, t=4), AX.X, ALU.max))
            cp(sm[0:1, 384:512].rearrange("p (h g t) -> p h g t", g=4, t=4),
               sm[0:1, 900:932].rearrange("p (h t) -> p h t", t=4).unsqueeze(2).broadcast_to((1, 8, 4, 4))).then_inc(s_rm, 1)
            dve.wait_ge(s_mb, b + 1)
            then(ts(sm[:, 328:329], bank[3][:, 0:1], -SCALE, None, ALU.mult))
            ts(sm[:, 320:328], sm[:, 48:56], SCALE, sm[:, 328:329], ALU.mult, ALU.add).then_inc(s_nb, 1)
            dve.wait_ge(s_tp, b + 1)
            dve.tensor_reduce(sm[:, 650:651], sm[:, 640:649], AX.X, ALU.add).then_inc(s_rsm, 1)
            for n in range(4):
                cp(by_page(pT[:, 4 + n, :]), turned(bank[5][:, n * P:(n + 1) * P]))
            cp(by_page(sm[0:S, 704:832]), turned(bank[6][0:S, 0:P])).then_inc(s_te, 1)
            dve.wait_ge(s_den, b + 1)
            dve.reciprocal(sm[0:32, 940:941], bank[3][0:32, 0:1])
            dve.wait_ge(s_od, b + 1)
            then(tt(od[:, :, :], bank[7][:, :].rearrange("p (h d) -> p h d", h=H),
                    C("head_diag").unsqueeze(2).broadcast_to((P, H, HD)), ALU.mult))
            dve.tensor_reduce(sm[:, 832:896], od[:, :, :].rearrange("p h d -> p d h"), AX.X, ALU.add).then_inc(s_of, 1)
            dve.wait_ge(s_oe, b + 1)
            ts(oall[:, bass.ds(b, 1), :].rearrange("p a d -> p (a d)"), bank[2][0:32, 0:HD], sm[0:32, 940:941], None, ALU.mult)
            dve.drain()
        o2 = sm[0:32, 0:512].rearrange("p (b d) -> p b d", b=NB_SEQ)
        then(tt(o2, oall[:, :, :], oall[:, :, :], ALU.mult))
        then(dve.tensor_reduce(st[0:32, 0:8], o2, AX.X, ALU.add))
        then(ts(st2[0:32, 8:16], st[0:32, 0:8], 1.0 / HD, EPS, ALU.mult, ALU.add))
        dve.reciprocal(st2[0:32, 8:16], st2[0:32, 8:16]).then_inc(s_ofs, 1)
        dve.wait_ge(s_ofq, 1)
        tt(oall[:, :, :], oall[:, :, :], st2[0:32, 0:8].unsqueeze(2).broadcast_to((32, NB_SEQ, HD)), ALU.mult).then_inc(s_ofr, 1)
        dve.wait_ge(s_oft, 1)
        for h2 in range(2):
            for hp in range(HP):
                ob = bank[0][0:HD, 0:256].rearrange("p (b h t) -> p h b t", b=NB_SEQ, t=TS)[:, 2 * hp + h2]
                cp(asT[64 * h2:64 * h2 + 64, 4 + hp, :].rearrange("p (b t) -> p b t", t=TS), ob)
        dve.drain()
        tt(asT[:, 4:8, :], asT[:, 4:8, :], vT[:, V_MN:V_MN + 4].unsqueeze(2).broadcast_to((P, HP, S)), ALU.mult)
        dve.drain().then_inc(s_oas, 1)

        asm4 = asm[:, 0:256].rearrange("p (k b t) -> p k b t", k=KT, t=TS)

        def gates(f0, n, dst):
            cp(asm4, by_seq(mT[:, f0:f0 + KT, 0:NB_SEQ]))
            dve.drain().then_inc(s_hs, 1)
            dve.wait_ge(s_gmt, n + 1)
            for e in range(2):
                cp(dst[:, e * 512:(e + 1) * 512], bank[6 + e][0:S, :])
            dve.drain().then_inc(s_gme, 1)

        gates(16, 0, gmod)
        dve.wait_ge(s_xr, KT)

        def residual(f, gate_col, out):
            g = mT[:, gate_col, NB_SEQ:NSEQ]
            dve.scalar_tensor_tensor(x2T[:, f, :], out[:, :], g, x2T[:, f, :], ALU.mult, ALU.add).then_inc(s_ev, 1)

        def evict_out(i, q):
            f = 4 * i + q
            dve.wait_ge(s_ft, F_OUT + f + 3)
            residual(f, 16 + f, bank[q % 2])

        def sample_rows(n, at, src, g, base):
            for e in range(4):
                c = slice(at + 64 * e, at + 64 * e + 64)
                tt(xtmp[:, 64 * e:64 * e + 64], src[32 * e:32 * e + 32, 0:64], g[:, c], ALU.mult)
            dve.drain().then_inc(s_sev, 1)
            tt(x2s[:, at:at + CHUNK], base[:, at:at + CHUNK], xtmp[:, 0:256], ALU.add)
            dve.drain()

        def sample_out(i, u):
            dve.wait_ge(s_ss, N_OUT + 2 * i + u + 1)
            sample_rows(2 * i + u, (2 * i + u) * CHUNK, bank[4 + u], gmod, xs)

        split_lo(F_OUT, 0)
        for i in range(2):
            for q in range(4):
                if 4 * i + q < 7:
                    split_lo(F_OUT + 4 * i + q + 1, (q + 1) % 4)
                evict_out(i, q)
                if q % 2:
                    sample_out(i, q // 2)
        dve.drain().then_inc(s_x2s, 1)
        gains(32, V_N2)
        dve.wait_ge(s_ssm, KT)
        then(ts(rb[:, :], bank[2][:, :], 1.0 / DM, EPS, ALU.mult, ALU.add))
        dve.reciprocal(rb[:, :], rb[:, :]).then_inc(s_r1, 1)
        dve.wait_ge(s_x2q, 1)
        then(ts(st2[0:S, 0:1], st[0:S, 0:1], 1.0 / DM, EPS, ALU.mult, ALU.add))
        dve.reciprocal(st2[0:S, 0:1], st2[0:S, 0:1]).then_inc(s_x2i, 1)
        dve.wait_ge(s_r2, 1)
        for k in range(KT):
            tt(stage[k % 2][:, :], x2T[:, k, :], rb[:, :], ALU.mult).then_inc(s_nx, 1)
            if k >= 1:
                act_lo(k - 1, 2 * KT + k - 1)
                dve.drain()
        act_lo(KT - 1, 3 * KT - 1)
        sample_h(2, 24)

        def evict_ffn(i, q):
            n = 2 * i + q // 2
            if q % 2:
                dve.wait_ge(s_ft, F_FFN + 4 * i + q + 3)
                dve.wait_ge(s_ev, F_FFN + 4 * i + q + 2)
                tt(stage[1][:, :], stage[0][:, :], bank[1][:, :], ALU.mult).then_inc(s_ev, 1)
                dve.wait_ge(s_fh, n + 1)
                tt(flo[:, bass.ds(n, 1), :].rearrange("p a t -> p (a t)"), stage[1][:, :],
                   fhi[:, bass.ds(n, 1), :].rearrange("p a t -> p (a t)").bitcast(F32), ALU.subtract)
                dve.drain().then_inc(s_fl, 1)

        def sample_ffn(i, u):
            n = 2 * i + u
            dve.wait_ge(s_ssl, n + 1)
            tt(asm[0:64, 64:128], asm[0:64, 0:64], bank[4 + u][64:128, 0:64], ALU.mult).then_inc(s_sev, 1)
            dve.wait_ge(s_smt, n + 1)
            for e in range(2):
                cp(aT[64 * e:64 * e + 64, bass.ds(n, 1), :].rearrange("p a s -> p (a s)"), bank[7][0:64, 32 * e:32 * e + 32])
            dve.drain().then_inc(s_sme, 1)

        stage_pairs(F_FFN, FT // 2, evict_ffn, sample_ffn)
        gates(40, 1, gmod2)
        c = 0
        for fb in range(DM // CHUNK):
            for n, kd in enumerate(KD):
                for half in range(2):
                    split_lo(F_DOWN + 2 * c + half, 2 * (c % 2) + half, kd)
                c += 1
            for half in range(2):
                dve.wait_ge(s_ft, F_DOWN + 6 * fb + 4 + half + 3)
                residual(2 * fb + half, 40 + 2 * fb + half, bank[2 * (fb % 2) + half])
            dve.wait_ge(s_ss, N_DOWN + 3 * fb + 3)
            sample_rows(fb, fb * CHUNK, bank[4 + fb % 2], gmod2, x2s)
        dve.drain().then_inc(s_x3, 1)
        dve.wait_ge(s_fw, 16)
        for i in range(TT + 1):
            n = P if i < TT else S
            dve.wait_ge(s_ysq, i + 1)
            if i < TT:
                then(tt(st2[0:n, 2:3], st[0:n, 0:1], st[0:n, 1:2], ALU.add))
                then(ts(st2[0:n, 0:1], st2[0:n, 2:3], 1.0 / DM, EPS, ALU.mult, ALU.add))
            else:
                then(ts(st2[0:n, 0:1], st[0:n, 0:1], 1.0 / DM, EPS, ALU.mult, ALU.add))
            dve.reciprocal(st2[0:n, 0:1], st2[0:n, 0:1]).then_inc(s_yi, 1)
            dve.wait_ge(s_yr, i + 1)
            for e in range(2):
                c = slice(512 * e, 512 * e + 512)
                if i < TT:
                    dve.scalar_tensor_tensor(ytok[i % 2][:, c], bank[2 * (i % 2) + e][:, :], st2[:, 1:2], fw[:, c], ALU.mult, ALU.mult)
                else:
                    dve.scalar_tensor_tensor(x2s[:, c], x2s[:, c], st2[0:S, 1:2], fw[0:S, c], ALU.mult, ALU.mult)
            dve.drain().then_inc(s_y, 1)

    persist.close()


_INS = ['x_prompt', 'x_sample', 'cache_k', 'cache_v', 'state_ret', 'page_table', 'c_prompt', 'c_sample',
        'norm1_w', 'norm2_w', 'final_w', 'w_mod', 'b_mod', 'w_in', 'ret_gn_w', 'moba_norm_w', 'w_out',
        'w_gate', 'w_up', 'w_down']
_OUTS = [(1, T, DM), (NB_SEQ, TS, DM), (1, 1, T, H, HD), (1, 1, T, H, HD), (1, 1, H, HD, HD),
         (1, NB_SEQ, TS, H, HD), (1, NB_SEQ, TS, H, HD), (1, NB_SEQ, H, HD, HD)]


def kernel(**inputs):
    import concourse.bacc as bacc
    from concourse.bass_utils import run_bass_kernel_spmd

    nc = bacc.Bacc("TRN2", target_bir_lowering=False, num_devices=1)
    const, where = constants()
    arrays, args = {}, []
    for name, a in [(n, inputs[n]) for n in _INS] + [("const", const)]:
        a = np.ascontiguousarray(a)
        arrays[f"in_{name}"] = a
        args.append(nc.dram_tensor(f"in_{name}", a.shape, mybir.dt.from_np(a.dtype), kind="ExternalInput").ap())
    args.append(where)
    for i, shape in enumerate(_OUTS):
        args.append(nc.dram_tensor(f"out_{i}", shape, F32, kind="ExternalOutput").ap())
    decoder_step(nc, *args)
    r = run_bass_kernel_spmd(nc, [arrays], core_ids=[0])
    return tuple(r.results[0][f"out_{i}"] for i in range(len(_OUTS)))
```

```python
from contextlib import ExitStack

import numpy as np
import concourse.bass as bass
from concourse import mybir

F32, F32R, I32 = mybir.dt.float32, mybir.dt.float32r, mybir.dt.int32
ALU, ACT, AX = mybir.AluOpType, mybir.ActivationFunctionType, mybir.AxisListType

P = 128
DM = 1024
T = 512
NB_SEQ, TS = 8, 4
S = NB_SEQ * TS
HD = 64
H = 8
HP = H // 2
W = H * HD
PAST, PAGE, BLOCK, TOPK = 4096, 128, 256, 3
NPAGE = PAST // PAGE
NBLK = PAST // BLOCK
GRP = 4
NGRP = NPAGE // GRP
ROWS = PAGE // 32
DFF = 2816
KT = DM // P
FT = DFF // P
TT = T // P
EPS = 1e-6
BIG = 1e30
SCALE = HD ** -0.5
NSEQ = NB_SEQ + 1
CHUNK = 256
NIN = (4 * W + 3 * W) // CHUNK
NMOD = 6 * DM // CHUNK
RQ, RK, RV, RG, MQ, MK, MV = (W // P * i for i in range(7))
V_BMOD, V_N1, V_N2, V_GN, V_MN = 0, 48, 56, 64, 68
NVEC = 72


def constants():
    f = np.float32
    log_g = np.log1p(-np.exp2(-5.0 - np.arange(H))).astype(np.float64)
    p = np.arange(P)
    out, where = [], {}

    def put(name, a):
        a = np.asarray(a, f)
        full = np.zeros((P, int(np.prod(a.shape[1:]))), f)
        full[: a.shape[0]] = a.reshape(a.shape[0], -1)
        at = sum(x.shape[1] for x in out)
        where[name] = (at, a.shape)
        out.append(full)

    put("ident", np.eye(P))
    put("ones", np.ones((P, P)))
    inv = (f(10000.0) ** (-np.arange(32, dtype=f) / f(32))).astype(f)
    ang = (np.arange(T, dtype=f)[None, :] * inv[p % 32][:, None]).astype(f)
    put("cos", np.cos(ang))
    put("sin", np.sin(ang))
    rot = np.zeros((P, P))
    for m in range(P):
        if m % 64 < 32:
            rot[m + 32, m] = -1.0
        else:
            rot[m - 32, m] = 1.0
    put("rot", rot)
    angs = ((PAST + np.arange(S) % TS).astype(f)[:, None] * inv[None, :]).astype(f)
    put("cos_s", np.cos(angs))
    put("sin_s", np.sin(angs))
    i = np.arange(P)
    diff = i[None, :] - i[:, None]
    d = [np.where(diff >= 0, np.exp(np.maximum(diff, 0) * g) * SCALE, 0.0) for g in log_g]
    put("decay", np.stack(d, 1))
    s = np.arange(S)
    diff = s[None, :] - s[:, None]
    ok = (s[None, :] // TS == s[:, None] // TS) & (diff >= 0)
    put("decay_s", np.stack([np.where(ok, np.exp(np.maximum(diff, 0) * g) * SCALE, 0.0) for g in log_g], 1))
    hp_of = lambda hp: 2 * hp + p // 64
    put("q_dec", np.stack([np.exp((i[None, :] + 1) * log_g[hp_of(hp)][:, None]) for hp in range(HP)], 1))
    put("q_dec_s", np.stack([np.exp((s[None, :] % TS + 1) * log_g[hp_of(hp)][:, None]) for hp in range(HP)], 1))
    put("k_dec", np.exp((P - 1 - i)[:, None] * log_g[None, :]) * SCALE)
    kb = np.exp((TS - 1 - s % TS)[:, None] * log_g[None, :]) * SCALE
    put("k_dec_s", np.where((s // TS)[:, None, None] == np.arange(NB_SEQ)[None, :, None], kb[:, None, :], 0.0))
    put("c_dec", np.stack([np.exp(P * log_g[hp_of(hp)]) for hp in range(HP)], 1))
    put("c_dec_s", np.stack([np.exp(TS * log_g[hp_of(hp)]) for hp in range(HP)], 1))
    put("causal", np.where(i[None, :] <= i[:, None], 0.0, -BIG))
    h, g, t = p // 16, p // 4 % 4, p % 4
    same = (h[:, None] == h[None, :]) & (t[:, None] == t[None, :])
    put("pair0", same & (g[:, None] < 2))
    put("pair1", same & (g[:, None] >= 2))
    put("own_pair", same & (g[:, None] // 2 == g[None, :] // 2))
    n_own = 2 * np.arange(NGRP)[None, :] + (g // 2)[:, None]
    put("earlier", np.arange(NBLK)[None, None, :] < n_own[:, :, None])
    ht = np.arange(32)
    put("sum_g", (h * 4 + t)[:, None] == ht[None, :])
    put("sum_pv", (p % 32)[:, None] == ht[None, :])
    tok = np.arange(S)
    seq = np.arange(NB_SEQ)
    ok = (g == 0)[:, None, None] & (tok[None, None, :] // TS == seq[None, :, None]) & (tok % TS <= t[:, None])[:, None, :]
    put("own_mask", np.where(ok, 0.0, -BIG))
    put("head_diag", (p % 32 // 4)[:, None] == np.arange(H)[None, :])
    put("row32", (p % 32)[:, None])
    put("row128", p[:, None])
    return np.ascontiguousarray(np.concatenate(out, 1)), where


def decoder_step(nc, x_prompt, x_sample, cache_k, cache_v, state_ret, page_table, c_prompt, c_sample,
                 norm1_w, norm2_w, final_w, w_mod, b_mod, w_in, ret_gn_w, moba_norm_w, w_out,
                 w_gate, w_up, w_down, const, where,
                 y_prompt, y_sample, k_prompt, v_prompt, ret_prompt, k_sample, v_sample, ret_sample):
    NC = const.shape[1]
    persist, mid = ExitStack(), ExitStack()

    def sem(name):
        return persist.enter_context(nc.semaphore(name))

    def allocator(stack):
        return lambda name, shape, dt=F32: stack.enter_context(nc.sbuf_tensor(name, shape, dt))

    sb = allocator(persist)
    ct = sb("ct", [P, NC])

    def C(name):
        at, shape = where[name]
        n = int(np.prod(shape[1:]))
        v = ct[:shape[0], at:at + n]
        return v.rearrange("p (a b) -> p a b", a=shape[1]) if len(shape) == 3 else v

    ident, ones = C("ident"), C("ones")
    asT = sb("asT", [P, KT, S])
    vT = sb("vT", [P, NVEC])
    mT = sb("mT", [P, 48, NSEQ])
    gain = sb("gain", [P, KT, NSEQ])
    xs = sb("xs", [S, DM])
    stage = [sb(f"stage{i}", [P, T]) for i in range(2)]
    st = sb("st", [P, 64])
    st2 = sb("st2", [P, 64])
    kidx = sb("kidx", [P, NB_SEQ * NGRP], I32)
    kix = [sb(f"kix{i}", [P, 1], I32) for i in range(4)]
    pt = sb("pt", [P, NB_SEQ * NPAGE], I32)
    asm = sb("asm", [P, 256])
    xtmp = sb("xtmp", [S, CHUNK])

    dense = ExitStack()
    tmp = allocator(dense)
    raw = [tmp(f"raw{i}", [P, KT, CHUNK]) for i in range(2)]
    whi = [tmp(f"whi{i}", [P, KT, P], F32R) for i in range(2)]
    wlo = [tmp(f"wlo{i}", [P, KT, P], F32R) for i in range(2)]
    ahi = tmp("ahi", [P, KT, T], F32R)
    alo = tmp("alo", [P, KT, T], F32R)
    dense.close()
    KTb = [sb(f"KT{i}", [P, ROWS, W // 32, 32]) for i in range(2)]
    VB = [sb(f"V{i}", [P, W]) for i in range(8)]
    Kb = [sb(f"K{i}", [P, ROWS * W]) for i in range(4)]
    sb2 = allocator(mid)
    zs = sb2("zs", [S, NIN * CHUNK])
    cT = sb2("cT", [P, KT, 32])
    sm = sb2("sm", [P, 960])
    mst = sb2("mst", [P, P])

    era1 = ExitStack()
    tmp = allocator(era1)
    zT = tmp("zT", [P, 28, T])
    era1a = ExitStack()
    tmp = allocator(era1a)
    vrow = tmp("vrow", [NVEC, P])
    crow = tmp("crow", [NSEQ, DM])
    xP = tmp("xP", [P, TT, DM])
    sq = tmp("sq", [P, DM])
    rawm = tmp("rawm", [P, KT, CHUNK])
    era1a.close()
    era1b = ExitStack()
    tmp = allocator(era1b)
    rvtok = tmp("rvtok", [P, TT, W])
    mvtok = tmp("mvtok", [P, TT, W])
    scr = tmp("scr", [P, 7, T])
    sst = tmp("sst", [P, 4, HD])
    era1b.close()
    sq_ret = Kb[2][:, :].rearrange("p (i w) -> p i w", i=TT)
    sq_moba = Kb[3][:, :].rearrange("p (i w) -> p i w", i=TT)
    rettok = zT[:, RV:RV + 4, :]
    mobatok = zT[:, MV:MV + 4, :]
    era1.close()

    era2 = ExitStack()
    tmp = allocator(era2)
    state = tmp("state", [P, NB_SEQ, HP, HD])
    qrs, krs = tmp("qrs", [S, W]), tmp("krs", [S, W])
    sT = tmp("sT", [P, 3, HP, S])
    ats = tmp("ats", [S, H, S])
    era2.close()
    tmp = allocator(era2)
    lgs = tmp("lgs", [P, NGRP, P])
    pe_x = tmp("pe_x", [P, NGRP, P])
    pT = tmp("pT", [P, NGRP, P])
    qbb = tmp("qbb", [P, W // 32, S])
    kbb = tmp("kbb", [P, W // 32, S])
    era2.close()
    tmp = allocator(era2)
    below_values = tmp("below_values", [P, 28, T])
    kmask = [tmp(f"kmask{i}", [S, W]) for i in range(2)]
    ret_s = tmp("ret_s", [S, W])
    era2.close()
    tmp = allocator(era2)
    below_values = tmp("below_values2", [P, 28, T])
    qbd = [tmp(f"qbd{i}", [P, W // 32, 32]) for i in range(2)]
    od = tmp("od", [P, H, HD])
    oall = tmp("oall", [32, NB_SEQ, HD])
    era2.close()
    mid.close()

    era3 = ExitStack()
    tmp = allocator(era3)
    x2T = tmp("x2T", [P, KT, T])
    aT = tmp("aT", [P, FT, S])
    x2s = tmp("x2s", [S, DM])
    era3a = ExitStack()
    tmp = allocator(era3a)
    xP2 = tmp("xP2", [P, TT, DM])
    gmod = tmp("gmod", [S, DM])
    rb = tmp("rb", [P, T])
    xsn2 = tmp("xsn2", [S, DM])
    era3a.close()
    era3b = ExitStack()
    tmp = allocator(era3b)
    fhi = tmp("fhi", [P, FT, T], F32R)
    flo = tmp("flo", [P, FT, T], F32R)
    era3b.close()
    era4 = ExitStack()
    tmp = allocator(era4)
    fw = tmp("fw", [P, DM])
    ytok = [tmp(f"ytok{i}", [P, DM]) for i in range(2)]
    gmod2 = xs
    era4.close()
    era3.close()

    bank = [persist.enter_context(nc.psum_tensor(f"bank{i}", [P, 512], F32)) for i in range(8)]

    s_ident = sem("ident_loaded")
    s_const, s_x, s_xs, s_c = sem("const_loaded"), sem("x_loaded"), sem("xs_loaded"), sem("c_loaded")
    s_vec, s_pt, s_state = sem("vec_loaded"), sem("pt_loaded"), sem("state_loaded")
    s_w = [sem(f"w_loaded{i}") for i in range(2)]
    s_x2l, s_fw = sem("x_reloaded"), sem("final_w_loaded")
    s_out = sem("out_stored")
    s_ytok = [sem(f"y_tile_stored{i}") for i in range(2)]
    s_hi, s_lo, s_ft, s_ev = sem("w_hi"), sem("w_lo"), sem("tile_done+2"), sem("tile_evicted+2")
    s_ss, s_sev = sem("sample_done"), sem("sample_evicted+2")
    s_md, s_mt, s_wm = sem("mod_chunk_done"), sem("gain_ready"), sem("mod_w_loaded")
    s_mev, s_mtp, s_mp = sem("mod_copied+2"), sem("mod_turned+1"), sem("mod_pair_kept+1")
    s_silu, s_ctp, s_ct, s_vtp = sem("c_silu"), sem("c_turned"), sem("cT_ready"), sem("vec_turned")
    s_sqd, s_rin, s_xn, s_xsn = sem("squares"), sem("rms_inverse"), sem("x_normed"), sem("xs_normed")
    s_xt, s_stg, s_hhi, s_hlo = sem("act_turned"), sem("act_staged"), sem("act_hi"), sem("act_lo")
    s_xst, s_hs = sem("xs_turned"), sem("asT_ready")
    s_vt1, s_vt2 = sem("values_turned"), sem("values_copied")
    s_qk, s_sc, s_nm, s_p = sem("moba_qk"), sem("moba_scores"), sem("moba_negmax"), sem("moba_probs+1")
    s_ptp, s_pte, s_pv, s_on = sem("moba_turned+1"), sem("moba_probsT+1"), sem("moba_out+1"), sem("moba_normed+1")
    s_rr, s_rk, s_kt1, s_kt2 = sem("ret_rotated"), sem("ret_k"), sem("ret_kT"), sem("ret_ktok")
    s_ra, s_rad, s_kv, s_st = sem("ret_scores"), sem("ret_decayed"), sem("ret_kv"), sem("ret_state")
    s_ro, s_roc = sem("ret_out"), sem("ret_copied+1")
    s_rs, s_hsq, s_hri, s_hrs = sem("ret_state_stored+16"), sem("head_squares"), sem("head_inverse"), sem("head_rstd")
    s_hn, s_sg = sem("heads_normed"), sem("gate_silu")
    s_kst, s_vst, s_sst = sem("k_prompt_stored"), sem("v_prompt_stored"), sem("ret_sample_stored")
    s_srot, s_sqt, s_sqe, s_sa = sem("s_rotated"), sem("s_qk_turned"), sem("s_qkT"), sem("s_scores")
    s_sad, s_so, s_soc, s_sot = sem("s_decayed"), sem("s_out"), sem("s_out_copied"), sem("s_out_turned")
    s_ssq, s_srs, s_srn, s_srt = sem("s_squares"), sem("s_rstd"), sem("s_normed"), sem("s_norm_turned")
    s_sas, s_ssg = sem("s_ret_mixed"), sem("s_gate_silu")
    s_km, s_kvs, s_sts = sem("s_kmask"), sem("s_kv"), sem("s_state_new")
    s_idx, s_qd = sem("page_rows"), sem("qbd_ready")
    s_k = [sem(f"k_loaded{i}") for i in range(4)]
    s_v = [sem(f"v_loaded{i}") for i in range(8)]
    s_kt, s_lg, s_own, s_s1 = sem("k_turned"), sem("logits+2"), sem("own_logits"), sem("block_sums")
    s_gt, s_mx, s_mxt, s_rm = sem("gates"), sem("part_max"), sem("part_max_turned"), sem("row_max")
    s_mb, s_nb, s_ex, s_tp = sem("max_spread"), sem("exp_bias"), sem("exps"), sem("probs_turned")
    s_te, s_rsm, s_den, s_vd = sem("probsT_copied"), sem("part_den"), sem("denominators"), sem("page_used")
    s_od, s_of, s_oe = sem("out_masked"), sem("out_folded"), sem("out_kept")
    s_ofs, s_ofr, s_ofq, s_oft = sem("o_squares"), sem("o_inverse"), sem("o_rstd"), sem("o_turned")
    s_oas = sem("o_mixed")
    s_tt, s_oa, s_rcp = sem("own_probs_turned"), sem("out_row_kept"), sem("denominators_inverse")
    s_le, s_to = sem("logits_kept+2"), sem("own_probsT_copied")
    s_sqx, s_ssm, s_r1, s_r2 = sem("x2_squares"), sem("x2_sums"), sem("x2_inverse"), sem("x2_rstd")
    s_nx, s_gmt = sem("x2_scaled"), sem("gmod_turned")
    s_xr, s_x2s, s_x2q, s_x2i = sem("x2T_ready"), sem("x2s_ready"), sem("x2s_squares"), sem("x2s_inverse")
    s_x2n = sem("x2s_normed")
    s_fh, s_fl = sem("ff_hi"), sem("ff_lo+1")
    s_ssl, s_smt, s_sme = sem("s_ffn_silu"), sem("s_ffn_turned"), sem("s_ffn_aT")
    s_x3, s_yt, s_ysq, s_yi = sem("x3_ready"), sem("y_turned"), sem("y_squares"), sem("y_inverse")
    s_yr, s_y = sem("y_rstd"), sem("y_ready")

    kview = lambda w: w[0].rearrange("(k p) f -> p k f", p=P)
    w_mod_v, w_in_v, w_out_v = kview(w_mod), kview(w_in), kview(w_out)
    w_gate_v, w_up_v, w_down_v = kview(w_gate), kview(w_up), kview(w_down)

    NMA = 2 * DM // CHUNK
    NMB = NMOD - NMA
    KD = (8, 8, 6)
    B_IN = NMA // 2
    B_MODB = B_IN + NIN // 2
    B_OUT = B_MODB + 1
    B_FFN = B_OUT + 2
    B_DOWN = B_FFN + FT // 2
    F_OUT, N_OUT = 2 * NIN, NIN
    F_FFN, N_FFN = F_OUT + 8, N_OUT + 4
    F_DOWN, N_DOWN = F_FFN + 2 * FT, N_FFN + FT
    N_STORES = [0]

    turned = lambda x: x.rearrange("p (h g t) -> p g h t", g=GRP, t=TS)
    by_page = lambda x: x.rearrange("p (g h t) -> p g h t", g=GRP, t=TS)

    def moba_steps(eng, step):
        step(0, 0, tail=False, rest=False)
        step(1, 1, rest=False)
        with eng.Fori(1, NB_SEQ // 2 - 1) as i:
            step(2 * i, 0)
            step(2 * i + 1, 1)
        step(NB_SEQ - 2, 0)
        step(NB_SEQ - 1, 1)
        step(NB_SEQ, 0, head=False)

    block = persist.enter_context(nc.Block())

    @block.sync
    def _(sp):
        def store(dst, src):
            sp.dma_start(dst, src).then_inc(s_out, 16)
            N_STORES[0] += 1

        def chunk(u, view, at):
            sp.dma_start(raw[u][:, :, :], view[:, :, at]).then_inc(s_w[u], 16)

        sp.sem_inc(s_rs, 16)
        sp.dma_start(crow[0:NB_SEQ, :], c_sample).then_inc(s_c, 16)
        sp.dma_start(crow[NB_SEQ:NSEQ, :], c_prompt).then_inc(s_c, 16)
        sp.dma_start(ct[:, 0:P], const[:, 0:P]).then_inc(s_ident, 16)
        for u in range(2):
            chunk(u, w_mod_v, slice(u * CHUNK, (u + 1) * CHUNK))
        sp.dma_start(vrow[V_BMOD:V_N1, :], b_mod[0].rearrange("(r c) -> r c", c=P)).then_inc(s_vec, 16)
        for at, v in ((V_N1, norm1_w), (V_N2, norm2_w), (V_GN, ret_gn_w), (V_MN, moba_norm_w)):
            n = v.shape[1] // P
            sp.dma_start(vrow[at:at + n, :], v[0].rearrange("(r c) -> r c", c=P)).then_inc(s_vec, 16)
        sp.dma_start(xP[:, :, :], x_prompt[0].rearrange("(i p) d -> p i d", p=P)).then_inc(s_x, 16)
        sp.dma_start(xs[:, :], x_sample.rearrange("b t d -> (b t) d")).then_inc(s_xs, 16)
        sp.dma_start(pt[:, :], page_table.rearrange("b n -> (b n)").partition_broadcast(P)).then_inc(s_pt, 16)
        sp.dma_start(ct[:, P:], const[:, P:]).then_inc(s_const, 16)
        with sp.Fori(1, NMA // 2) as i:
            for u in range(2):
                sp.wait_ge(s_md, 2 * i + u - 1)
                chunk(u, w_mod_v, bass.ds((2 * i + u) * CHUNK, CHUNK))
        for u in range(2):
            sp.wait_ge(s_md, NMA - 1 + u)
            chunk(u, w_in_v, slice(u * CHUNK, (u + 1) * CHUNK))
        def mod_beside(n):
            sp.dma_start(rawm[:, :, :], w_mod_v[:, :, bass.ds((NMA + n) * CHUNK, CHUNK)]).then_inc(s_wm, 16)

        mod_beside(0)
        with sp.Fori(1, NIN // 2) as i:
            for u in range(2):
                sp.wait_ge(s_ss, 2 * i + u - 1)
                chunk(u, w_in_v, bass.ds((2 * i + u) * CHUNK, CHUNK))
                sp.wait_ge(s_md, NMA + 2 * i + u - 1)
                mod_beside(2 * i + u - 1)
        sp.wait_ge(s_md, NMA + NIN - 1)
        mod_beside(NIN - 1)
        for u in range(2):
            sp.wait_ge(s_ss, NIN - 1 + u)
            chunk(u, w_mod_v, slice((NMA + NIN + u) * CHUNK, (NMA + NIN + u + 1) * CHUNK))
        sp.wait_ge(s_vt2, 4)
        sp.dma_start(k_prompt[0, 0].rearrange("(i p) h d -> p i (h d)", p=P), scr[:, 0:4, :]).then_inc(s_kst, 16)
        sp.wait_ge(s_vt2, 8)
        sp.dma_start(v_prompt[0, 0].rearrange("(i p) h d -> p i (h d)", p=P), mvtok[:, :, :]).then_inc(s_vst, 16)
        sp.wait_ge(s_sev, NIN + 2)
        store(k_sample[0].rearrange("b t h d -> (b t) (h d)"), zs[:, 5 * W:6 * W])
        store(v_sample[0].rearrange("b t h d -> (b t) (h d)"), zs[:, 6 * W:7 * W])
        cv = cache_v[0].rearrange("n p h d -> n p (h d)")
        sp.wait_ge(s_ss, NIN)
        for s in range(8):
            r = sp.value_load(pt[0:1, s:s + 1], min_val=0, max_val=cv.shape[0] - 1)
            sp.dma_start(VB[s][:, :], cv[bass.ds(r, 1), :, :].rearrange("a p c -> (a p) c")).then_inc(s_v[s], 16)
        with sp.Fori(0, HP) as hp:
            sp.wait_ge(s_st, hp + 1)
            sp.dma_start(ret_prompt[0, 0].rearrange("h d v -> (h d) v")[bass.ds(hp * P, P), :], sst[:, 3, :]).then_inc(s_rs, 16)
        sp.wait_ge(s_ro, HP)
        sp.dma_start(state[:, :, :, :], state_ret[0].rearrange("b (hp h2) d v -> (h2 d) b hp v", h2=2)).then_inc(s_state, 16)
        sp.wait_ge(s_sts, NB_SEQ)
        sp.dma_start(ret_sample[0].rearrange("b (hp h2) d v -> (h2 d) b hp v", h2=2), state[:, :, :, :]).then_inc(s_sst, 16)
        with sp.Fori(1, NB_SEQ * NPAGE // 8) as i:
            for s in range(8):
                r = sp.value_load(pt[0:1, bass.ds(i * 8 + s, 1)], min_val=0, max_val=cv.shape[0] - 1)
                sp.wait_ge(s_vd, i * 8 + s - 7)
                sp.dma_start(VB[s][:, :], cv[bass.ds(r, 1), :, :].rearrange("a p c -> (a p) c")).then_inc(s_v[s], 16)
        for u in range(2):
            sp.wait_ge(s_lg, NGRP * NB_SEQ + 2)
            sp.wait_ge(s_md, NMOD - 1 + u)
            chunk(u, w_out_v, slice(u * CHUNK, (u + 1) * CHUNK))
        sp.wait_ge(s_vst, 16)
        sp.wait_ge(s_hlo, 2 * KT)
        sp.wait_ge(s_vd, NB_SEQ * NPAGE)
        sp.dma_start(xP2[:, :, :], x_prompt[0].rearrange("(i p) d -> p i d", p=P)).then_inc(s_x2l, 16)
        for u in range(2):
            sp.wait_ge(s_ss, N_OUT + u + 1)
            chunk(u, w_out_v, slice((2 + u) * CHUNK, (3 + u) * CHUNK))

        def ffn_chunk(u, at):
            sp.dma_start(raw[u][:, :, 0:P], w_gate_v[:, :, at]).then_inc(s_w[u], 16)
            sp.dma_start(raw[u][:, :, P:2 * P], w_up_v[:, :, at]).then_inc(s_w[u], 16)

        for u in range(2):
            sp.wait_ge(s_ss, N_OUT + 2 + u + 1)
            ffn_chunk(u, slice(u * P, (u + 1) * P))
        with sp.Fori(1, FT // 2) as i:
            for u in range(2):
                sp.wait_ge(s_ss, N_FFN + 2 * i + u - 1)
                ffn_chunk(u, bass.ds((2 * i + u) * P, P))
        c = 0
        for fb in range(DM // CHUNK):
            for n, kd in enumerate(KD):
                sp.wait_ge(s_ss, N_DOWN + c - 1)
                sp.dma_start(raw[c % 2][:, 0:kd, :], w_down_v[:, 8 * n:8 * n + kd, fb * CHUNK:(fb + 1) * CHUNK]).then_inc(s_w[c % 2], 16)
                c += 1
        sp.wait_ge(s_ft, F_DOWN + 24 + 2)
        sp.dma_start(fw[:, :], final_w.partition_broadcast(P)).then_inc(s_fw, 16)
        for i in range(TT):
            sp.wait_ge(s_y, i + 1)
            sp.dma_start(y_prompt[0, i * P:(i + 1) * P, :], ytok[i % 2][:, :]).then_inc(s_ytok[i % 2], 16)
        sp.wait_ge(s_y, TT + 1)
        store(y_sample.rearrange("b t d -> (b t) d"), x2s[:, :])
        for i in range(2):
            sp.wait_ge(s_ytok[i], 16 * TT // 2)
        sp.wait_ge(s_out, 16 * N_STORES[0])

    @block.gpsimd
    def _(pool):
        pool.wait_ge(s_idx, 1)
        pool.wait_ge(s_ss, NIN)
        ck = cache_k[0].rearrange("n (a r) h d -> (n a) (r h d)", r=ROWS)
        for u in range(4):
            pool.indirect_dma_start(Kb[u][:, :], None, ck, bass.IndirectOffsetOnAxis(kidx[:, u:u + 1], 0)).then_inc(s_k[u], 16)
        with pool.Fori(1, NB_SEQ * NGRP // 4) as i:
            for u in range(4):
                pool.wait_ge(s_kt, 4 * i + u - 3)
                pool.tensor_copy(kix[u][:, :], kidx[:, bass.ds(4 * i + u, 1)])
                pool.drain()
                pool.indirect_dma_start(Kb[u][:, :], None, ck, bass.IndirectOffsetOnAxis(kix[u][:, :], 0)).then_inc(s_k[u], 16)

    @block.scalar
    def _(act):
        for s in (s_p, s_pte):
            act.sem_inc(s, 1)
        act.sem_inc(s_le, 2)
        act.sem_inc(s_roc, 1)
        act.sem_inc(s_mev, 2)
        act.wait_ge(s_c, 32)
        act.activation(crow[:, :], crow[:, :], ACT.Silu).then_inc(s_silu, 1)

        def keep_mod(pair, e):
            act.wait_ge(s_md, 2 * pair + e + 1)
            act.wait_ge(s_mtp, pair + 1)
            act.activation(mst[:, 64 * e:64 * e + 64], bank[6 + e][:, 0:64], ACT.Copy).then_inc(s_mev, 1)

        def keep_mod_pair(pair):
            for e in range(2):
                keep_mod(pair, e)

        keep_mod_pair(0)
        act.wait_ge(s_x, 16)
        for i in range(TT):
            act.activation(sq[:, :], xP[:, i, :], ACT.Square, accum_out=st[:, i:i + 1])
            act.drain()
        act.wait_ge(s_xs, 16)
        act.activation(sq[0:S, :], xs[:, :], ACT.Square, accum_out=st[0:S, 4:5]).then_inc(s_sqd, 1)
        keep_mod_pair(1)
        act.wait_ge(s_rin, 1)
        act.activation(st2[:, 0:4], st2[:, 8:12], ACT.Sqrt)
        act.activation(st2[0:S, 4:5], st2[0:S, 12:13], ACT.Sqrt)
        act.drain()
        for i in range(TT):
            last = act.activation(xP[:, i, :], xP[:, i, :], ACT.Copy, scale=st2[:, i:i + 1])
        last.then_inc(s_xn, 1)
        act.activation(sq[0:S, :], xs[:, :], ACT.Copy, scale=st2[0:S, 4:5]).then_inc(s_xsn, 1)
        for pair in range(2, NMA // 2):
            keep_mod_pair(pair)
        act.wait_ge(s_mt, 1)

        def stage_hi(k, n):
            act.wait_ge(s_stg, n + 1)
            act.activation(ahi[:, k, :], stage[k % 2][:, :], ACT.Copy).then_inc(s_hhi, 1)

        def split_hi(m, q, kd=KT):
            act.wait_ge(s_ft, m + 1)
            act.activation(whi[q % 2][:, 0:kd, :], raw[q // 2][:, 0:kd, q % 2 * P:(q % 2 + 1) * P], ACT.Copy).then_inc(s_hi, 1)

        act.wait_ge(s_w[0], 16 * (B_IN + 1))
        split_hi(0, 0)
        for k in range(KT):
            act.wait_ge(s_xt, k + 1)
            if k >= 2:
                act.wait_ge(s_hlo, k - 1)
            act.activation(stage[k % 2][:, :], bank[2 + k % 2][:, :], ACT.Identity,
                           scale=gain[:, k, NB_SEQ:NSEQ], bias=mT[:, k, NB_SEQ:NSEQ]).then_inc(s_stg, 1)
            stage_hi(k, k)

        def stage_pairs(F, B, pairs, loads, evict):
            def body(i, last):
                for q in range(4):
                    if not (last and q == 3):
                        n = (q + 1) % 4
                        if n % 2 == 0:
                            act.wait_ge(s_w[n // 2], loads(i + (n == 0)))
                        split_hi(F + 4 * i + q + 1, n)
                    if evict:
                        evict(i, q)

            if pairs > 1:
                with act.Fori(0, pairs - 1) as i:
                    body(i, False)
            body(pairs - 1, True)

        def evict_z(i, q):
            act.wait_ge(s_ft, 4 * i + q + 3)
            act.activation(zT[:, bass.ds(4 * i + q, 1), :].rearrange("p a t -> p (a t)"), bank[q % 2][:, :], ACT.Copy).then_inc(s_ev, 1)
            if q % 2:
                keep_mod(NMA // 2 + i, q // 2)

        stage_pairs(0, B_IN, NIN // 2, lambda i: 16 * (B_IN + i + 1), evict_z)
        for e in range(2):
            keep_mod(NMOD // 2 - 1, e)

        with act.Fori(0, HP) as hp:
            act.wait_ge(s_ro, hp + 1)
            for h2 in range(2):
                act.activation(rettok[:, :, bass.ds(hp * P + h2 * HD, HD)],
                               bank[6 + h2][:, 0:4 * HD].rearrange("p (c v) -> p c v", c=4), ACT.Copy).then_inc(s_roc, 1)
        act.wait_ge(s_srot, 1)
        act.activation(zs[:, 3 * W:4 * W], zs[:, 3 * W:4 * W], ACT.Silu).then_inc(s_ssg, 1)
        act.wait_ge(s_ssq, 1)
        act.activation(st2[0:S, 0:H], st2[0:S, 8:8 + H], ACT.Sqrt).then_inc(s_srs, 1)

        def copy_qk(hp):
            act.activation(scr[:, 3, :], zT[:, bass.ds(MK + hp, 1), :].rearrange("p a t -> p (a t)"), ACT.Copy)
            act.activation(scr[:, 0, :], zT[:, bass.ds(MQ + hp, 1), :].rearrange("p a t -> p (a t)"), ACT.Copy).then_inc(s_qk, 1)

        def probs(b, u):
            n = (u + 1) * P
            act.wait_ge(s_nm, 4 * b + u + 1)
            act.wait_ge(s_ptp, 4 * b + u + 1)
            act.activation(scr[:, 1, 0:n], bank[5][:, 0:n], ACT.Exp, scale=SCALE,
                           bias=st2[:, 20 + u % 2:21 + u % 2], accum_out=st[:, 16 + u:17 + u]).then_inc(s_p, 1)

        def probs_t(b, u):
            n = (u + 1) * P
            act.wait_ge(s_ptp, 4 * b + u + 2)
            act.wait_ge(s_pv, 4 * b + u + 1)
            act.activation(scr[:, 2, 0:n], bank[6][:, 0:n], ACT.Copy).then_inc(s_pte, 1)

        def keep_logits(b, e):
            act.wait_ge(s_lg, NGRP * b + 4 * e + 6)
            act.activation(lgs[:, 4 * e:4 * e + 4, :], bank[e][:, :].rearrange("p (g c) -> p g c", g=4), ACT.Copy).then_inc(s_le, 1)

        def exps(b):
            act.wait_ge(s_nb, b + 1)
            for g in range(NGRP):
                last = act.activation(pe_x[:, g, :].rearrange("p (a r) -> p r a", r=ROWS), lgs[:, g, :].rearrange("p (r a) -> p r a", r=ROWS),
                                      ACT.Exp, scale=SCALE, bias=sm[:, 320 + g:321 + g], accum_out=sm[:, 640 + g:641 + g])
                if g == 3:
                    last.then_inc(s_ex, 1)
            act.activation(sm[:, 576:608], sm[:, 512:544], ACT.Exp, scale=SCALE, bias=sm[:, 328:329],
                           accum_out=sm[:, 648:649]).then_inc(s_ex, 1)

        def keep_probs(b, e):
            act.wait_ge(s_tp, 2 * b + e + 1)
            for n in range(4):
                last = act.activation(by_page(pT[:, 4 * e + n, :]), turned(bank[2][:, n * P:(n + 1) * P]), ACT.Copy)
            last.then_inc(s_te, 1)

        def step(b, par, head=True, tail=True, rest=True):
            for slot in range(8):
                if head:
                    (probs if slot % 2 == 0 else probs_t)(b, slot // 2)
                if tail and slot == 2:
                    exps(b - 1)
                if tail and slot in (3, 4):
                    keep_probs(b - 1, slot - 3)
                if head and slot in (3, 7):
                    keep_logits(b, slot // 4)
            if head and par == 1:
                act.wait_ge(s_sc, 4 * b + 4)
                if isinstance(b, int) and b == NB_SEQ - 1:
                    return
                copy_qk(b // 2 + 1 if isinstance(b, int) else (b - 1) // 2 + 1)

        act.wait_ge(s_ro, HP)
        act.wait_ge(s_sst, 16)
        copy_qk(0)
        moba_steps(act, step)
        act.wait_ge(s_hn, 1)
        act.activation(sq_ret, rettok, ACT.Square)
        act.wait_ge(s_on, 4 * H + 1)
        act.activation(sq_moba, mobatok, ACT.Square).then_inc(s_hsq, 1)
        act.activation(zT[:, RG:RG + 4, :], zT[:, RG:RG + 4, :], ACT.Silu).then_inc(s_sg, 1)
        act.wait_ge(s_hri, 1)
        act.activation(gain[:, :, 0:8].rearrange("p a b -> p a b"), gain[:, :, 0:8], ACT.Sqrt).then_inc(s_hrs, 1)
        for k in range(KT):
            stage_hi(k, KT + k)

        act.wait_ge(s_vd, NB_SEQ * NPAGE)
        act.wait_ge(s_w[0], 16 * (B_OUT + 1))
        for q in range(2):
            split_hi(F_OUT + q, q)
        act.wait_ge(s_ofs, 1)
        act.activation(st2[0:32, 0:8], st2[0:32, 8:16], ACT.Sqrt).then_inc(s_ofq, 1)

        act.wait_ge(s_oas, 1)
        for k in range(KT):
            act.wait_ge(s_xt, 2 * KT + k + 1)
            act.activation(x2T[:, k, :], bank[2 + k % 2][:, :], ACT.Copy).then_inc(s_xr, 1)
        for f in range(KT):
            if f + 2 < KT:
                if f % 2 == 0:
                    act.wait_ge(s_w[(f + 2) // 2 % 2], 16 * (B_OUT + (f + 2) // 4 + 1))
                split_hi(F_OUT + f + 2, (f + 2) % 4)
            act.wait_ge(s_ev, F_OUT + f + 3)
            if f >= 2:
                act.wait_ge(s_ssm, f - 1)
            act.activation(stage[f % 2][:, :], x2T[:, f, :], ACT.Square).then_inc(s_sqx, 1)
        act.wait_ge(s_w[0], 16 * (B_FFN + 2))
        split_hi(F_FFN, 0)
        act.wait_ge(s_x2s, 1)
        act.activation(xsn2[:, :], x2s[:, :], ACT.Square, accum_out=st[0:S, 0:1]).then_inc(s_x2q, 1)
        act.wait_ge(s_r1, 1)
        act.activation(rb[:, :], rb[:, :], ACT.Sqrt).then_inc(s_r2, 1)
        act.wait_ge(s_x2i, 1)
        act.activation(st2[0:S, 1:2], st2[0:S, 0:1], ACT.Sqrt)
        act.drain()
        act.activation(xsn2[:, :], x2s[:, :], ACT.Copy, scale=st2[0:S, 1:2]).then_inc(s_x2n, 1)
        for k in range(KT):
            act.wait_ge(s_nx, k + 1)
            act.activation(stage[k % 2][:, :], stage[k % 2][:, :], ACT.Identity,
                           scale=gain[:, k, NB_SEQ:NSEQ], bias=mT[:, 24 + k, NB_SEQ:NSEQ]).then_inc(s_stg, 1)
            stage_hi(k, 2 * KT + k)

        def evict_ffn(i, q):
            act.wait_ge(s_ft, F_FFN + 4 * i + q + 3)
            if q % 2 == 0:
                act.wait_ge(s_fl, 2 * i + q // 2 + 1)
                act.activation(stage[0][:, :], bank[0][:, :], ACT.Silu).then_inc(s_ev, 1)
            else:
                act.wait_ge(s_ev, F_FFN + 4 * i + q + 3)
                act.activation(fhi[:, bass.ds(2 * i + q // 2, 1), :].rearrange("p a t -> p (a t)"), stage[1][:, :], ACT.Copy).then_inc(s_fh, 1)
                act.wait_ge(s_ss, N_FFN + 2 * i + q // 2 + 1)
                act.wait_ge(s_sev, N_FFN + 2 * i + q // 2 + 2)
                act.activation(asm[0:64, 0:64], bank[4 + q // 2][0:64, 0:64], ACT.Silu).then_inc(s_ssl, 1)

        stage_pairs(F_FFN, B_FFN, FT // 2, lambda i: 16 * (B_FFN + 2 * i + 2), evict_ffn)
        c = 0
        for fb in range(DM // CHUNK):
            for n, kd in enumerate(KD):
                act.wait_ge(s_w[c % 2], 16 * (B_FFN + FT + c // 2 + 1))
                for half in range(2):
                    split_hi(F_DOWN + 2 * c + half, 2 * (c % 2) + half, kd)
                c += 1
        for i in range(TT + 1):
            n = P if i < TT else S
            if i < TT:
                act.wait_ge(s_yt, i + 1)
            else:
                act.wait_ge(s_x3, 1)
            y = ytok[i % 2][0:n, :] if i < TT else x2s[:, :]
            if i >= 2 and i < TT:
                act.wait_ge(s_ytok[i % 2], 16)
            if i < TT:
                for e in range(2):
                    act.activation(y[:, e * 512:(e + 1) * 512], bank[2 * (i % 2) + e][0:n, :], ACT.Square,
                                   accum_out=st[0:n, e:e + 1])
            else:
                act.activation(gmod2[:, :], x2s[:, :], ACT.Square, accum_out=st[0:n, 0:1])
            act.drain().then_inc(s_ysq, 1)
            act.wait_ge(s_yi, i + 1)
            act.activation(st2[0:n, 1:2], st2[0:n, 0:1], ACT.Sqrt).then_inc(s_yr, 1)

    @block.tensor
    def _(pe):
        for s in (s_ft, s_lg):
            pe.sem_inc(s, 2)
        for s in (s_ptp, s_pv, s_mtp):
            pe.sem_inc(s, 1)
        pe.wait_ge(s_ident, 16)
        pe.wait_ge(s_silu, 1)
        for k in range(KT):
            last = pe.transpose(bank[4][:, k * NSEQ:(k + 1) * NSEQ], crow[:, k * P:(k + 1) * P], ident[0:NSEQ, 0:NSEQ])
        last.then_inc(s_ctp, 1)
        pe.wait_ge(s_vec, 80)
        pe.transpose(bank[5][:, 0:NVEC], vrow[:, :], ident[0:NVEC, 0:NVEC]).then_inc(s_vtp, 1)
        pe.wait_ge(s_ct, 1)

        def mod_chunk(buf, pair, e):
            pe.wait_ge(s_mev, 2 * pair + e + 1)
            for k in range(KT):
                for g in range(4):
                    last = pe.matmul(bank[6 + e][32 * g:32 * g + 32, 0:64], cT[:, k, :], buf[:, k, 64 * g:64 * g + 64],
                                     start=(k == 0), stop=(k == KT - 1))
            last.then_inc(s_md, 1)

        def turn_mod(pair):
            pe.wait_ge(s_mp, pair + 1)
            pe.wait_ge(s_mev, 2 * pair + 4)
            pe.transpose(bank[3][:, 0:P], mst[:, :], ident).then_inc(s_mtp, 1)

        with pe.Fori(0, NMA // 2) as i:
            for u in range(2):
                pe.wait_ge(s_w[u], 16 * (i + 1))
                mod_chunk(raw[u], i, u)
            turn_mod(i)
        pe.wait_ge(s_mp, NMA // 2 + 1)
        pe.wait_ge(s_const, 16)
        pe.wait_ge(s_xn, 1)

        def turn_rows(src, k, n, out=None):
            out = bank[2 + k % 2] if out is None else out
            for i in range(TT):
                last = pe.transpose(out[:, i * P:(i + 1) * P], src(i), ident)
            last.then_inc(s_xt, 1)

        for k in range(KT):
            if k >= 2:
                pe.wait_ge(s_stg, k - 1)
            turn_rows(lambda i: xP[:, i, k * P:(k + 1) * P], k, k)
        pe.wait_ge(s_xsn, 1)
        for k in range(KT):
            last = pe.transpose(bank[7][:, k * S:(k + 1) * S], sq[0:S, k * P:(k + 1) * P], ident[0:S, 0:S])
        last.then_inc(s_xst, 1)

        def tile(m, q, kd=KT, hi=None, lo=None, k0=0, out=None, first=True, final=True, ready=None):
            hi, lo = (ahi, alo) if hi is None else (hi, lo)
            out = bank[q % 2] if out is None else out
            pe.wait_ge(s_lo, m + 1)
            for k in range(kd):
                if ready is not None:
                    pe.wait_ge(s_hlo, ready + k + 1)
                pe.matmul(out[:, :], whi[q % 2][:, k, :], hi[:, k0 + k, :], start=(first and k == 0), stop=False)
                pe.matmul(out[:, :], whi[q % 2][:, k, :], lo[:, k0 + k, :], start=False, stop=False)
                last = pe.matmul(out[:, :], wlo[q % 2][:, k, :], hi[:, k0 + k, :], start=False, stop=(final and k == kd - 1))
            last.then_inc(s_ft, 1)

        def sample_chunk(u, n, lhs, kd=KT, first=True, final=True, out=None):
            out = bank[4 + u] if out is None else out
            for k in range(kd):
                for g in range(4):
                    last = pe.matmul(out[32 * g:32 * g + 32, 0:64], lhs(k), raw[u][:, k, 64 * g:64 * g + 64],
                                     start=(first and k == 0), stop=(final and k == kd - 1))
            last.then_inc(s_ss, 1)

        def stage_pair(F, N, i, after=None, ready=None, sample_ready=None):
            for q in range(4):
                pe.wait_ge(s_ev, F + 4 * i + q + 1)
                tile(F + 4 * i + q, q, ready=ready if q == 0 else None)
                if q == 1 and sample_ready is not None:
                    pe.wait_ge(s_hs, sample_ready)
                if q % 2:
                    pe.wait_ge(s_sev, N + 2 * i + q // 2 + 1)
                    sample_chunk(q // 2, N, lambda k: asT[:, k, :])
                if after:
                    after(i, q)

        def mod_between(i, q):
            if q % 2:
                pe.wait_ge(s_wm, 16 * (2 * i + q // 2 + 1))
                mod_chunk(rawm, NMA // 2 + i, q // 2)
            elif q == 0 and not isinstance(i, int):
                turn_mod(NMA // 2 + i - 1)

        stage_pair(0, 0, 0, mod_between, ready=0, sample_ready=1)
        with pe.Fori(1, NIN // 2) as i:
            stage_pair(0, 0, i, mod_between)
        turn_mod(NMOD // 2 - 2)
        for u in range(2):
            pe.wait_ge(s_w[u], 16 * (B_MODB + 1))
            mod_chunk(raw[u], NMOD // 2 - 1, u)
        turn_mod(NMOD // 2 - 1)
        pe.wait_ge(s_mp, NMOD // 2 + 1)
        pe.wait_ge(s_ev, 2 * NIN + 2)
        n = 0
        for sec in (MK, MV, RV):
            for j in range(4):
                if n >= 2:
                    pe.wait_ge(s_vt2, n - 1)
                for i in range(TT):
                    last = pe.transpose(bank[2 + n % 2][:, i * P:(i + 1) * P], zT[:, sec + j, i * P:(i + 1) * P], ident)
                last.then_inc(s_vt1, 1)
                n += 1
        pe.wait_ge(s_vt2, 12)
        with pe.Fori(0, HP) as hp:
            for n, sec in enumerate((RQ, RK)):
                pe.matmul(bank[n][:, :], C("rot"), zT[:, bass.ds(sec + hp, 1), :].rearrange("p a t -> p (a t)"),
                          start=True, stop=True).then_inc(s_rr, 1)
            pe.wait_ge(s_rk, hp + 1)
            for c in range(TT):
                last = pe.transpose(bank[2][:, c * P:(c + 1) * P], scr[:, 1, c * P:(c + 1) * P], ident)
            last.then_inc(s_kt1, 1)
            for h2 in range(2):
                r = 64 * h2
                for c in range(TT):
                    last = pe.matmul(bank[4 + h2][:, c * P:(c + 1) * P], scr[r:r + 64, 1, c * P:(c + 1) * P],
                                     scr[r:r + 64, 0, c * P:(c + 1) * P], start=True, stop=True)
            last.then_inc(s_ra, 1)
            pe.wait_ge(s_kt2, hp + 1)
            for c in range(TT):
                last = pe.matmul(bank[3][:, c * P:(c + 1) * P], scr[:, 4, c * P:(c + 1) * P],
                                 rvtok[:, c, bass.ds(hp * P, P)], start=True, stop=True)
            last.then_inc(s_kv, 1)
            pe.wait_ge(s_rad, hp + 1)
            pe.wait_ge(s_st, hp + 1)
            pe.wait_ge(s_roc, 2 * hp + 1)
            for h2 in range(2):
                r = 64 * h2
                for c in range(TT):
                    last = pe.matmul(bank[6 + h2][:, c * HD:(c + 1) * HD], scr[:, 5 + h2, c * P:(c + 1) * P],
                                     rvtok[:, c, bass.ds(hp * P + r, HD)], start=True, stop=(c == 0))
                    if c:
                        last = pe.matmul(bank[6 + h2][:, c * HD:(c + 1) * HD], scr[r:r + 64, 2, c * P:(c + 1) * P],
                                         sst[r:r + 64, c - 1, :], start=False, stop=True)
            last.then_inc(s_ro, 1)
        pe.wait_ge(s_srot, 1)
        for n, x in enumerate((qrs, krs)):
            for hp in range(HP):
                last = pe.transpose(bank[0][:, (n * HP + hp) * S:(n * HP + hp + 1) * S], x[:, hp * P:(hp + 1) * P], ident[0:S, 0:S])
        last.then_inc(s_sqt, 1)
        pe.wait_ge(s_sqe, 1)
        for h2 in range(2):
            r = 64 * h2
            for hp in range(HP):
                last = pe.matmul(bank[4 + h2][0:S, hp * S:(hp + 1) * S], sT[r:r + 64, 1, hp, :], sT[r:r + 64, 0, hp, :],
                                 start=True, stop=True)
        last.then_inc(s_sa, 1)
        pe.wait_ge(s_sad, 1)
        pe.wait_ge(s_roc, 2 * HP + 1)
        pe.wait_ge(s_state, 16)
        for h2 in range(2):
            r = 64 * h2
            for hp in range(HP):
                at = 2 * W + (2 * hp + h2) * HD
                pe.matmul(bank[6 + h2][r:r + 64, hp * S:(hp + 1) * S], zs[:, at:at + HD], ats[:, 2 * hp + h2, :],
                          start=True, stop=False, skip_group_check=True)
                for b in range(NB_SEQ):
                    last = pe.matmul(bank[6 + h2][r:r + 64, hp * S + TS * b:hp * S + TS * (b + 1)],
                                     state[r:r + 64, b, hp, :], sT[r:r + 64, 2, hp, TS * b:TS * (b + 1)],
                                     start=False, stop=(b == NB_SEQ - 1), skip_group_check=True)
        last.then_inc(s_so, 1)
        pe.wait_ge(s_soc, 1)
        for hp in range(HP):
            last = pe.transpose(bank[0][0:S, hp * P:(hp + 1) * P], sT[:, 0, :, :].rearrange("p a b -> p (a b)")[:, hp * S:(hp + 1) * S], ident)
        last.then_inc(s_sot, 1)
        for b in range(NB_SEQ):
            pe.wait_ge(s_km, b + 1)
            if b >= 2:
                pe.wait_ge(s_sts, b - 1)
            for hp in range(HP):
                last = pe.matmul(bank[2 + b % 2][:, hp * P:(hp + 1) * P], kmask[b % 2][:, hp * P:(hp + 1) * P],
                                 zs[:, 2 * W + hp * P:2 * W + (hp + 1) * P], start=True, stop=True)
            last.then_inc(s_kvs, 1)
        pe.wait_ge(s_srn, 1)
        for hp in range(HP):
            last = pe.transpose(bank[1][:, hp * S:(hp + 1) * S], ret_s[:, hp * P:(hp + 1) * P], ident[0:S, 0:S])
        last.then_inc(s_srt, 1)
        pe.wait_ge(s_sas, 1)

        def scores(b, pair, par, u):
            r, n = 64 * par, (u + 1) * P
            pe.wait_ge(s_p, 4 * b + u + 1)
            pe.matmul(bank[5][:, 0:n], scr[r:r + 64, 0, n - P:n],
                      scr[r:r + 64, 3, 0:n], start=True, stop=True).then_inc(s_sc, 1)

        def turn(b, u):
            pe.wait_ge(s_pte, 4 * b + u + 1)
            pe.wait_ge(s_p, 4 * b + u + 2)
            for j in range(u + 1):
                last = pe.transpose(bank[6][:, j * P:(j + 1) * P], scr[:, 1, j * P:(j + 1) * P], ident)
            last.then_inc(s_ptp, 1)

        def weigh(b, pair, par, u):
            pe.wait_ge(s_on, 4 * b + u + 1)
            pe.wait_ge(s_pte, 4 * b + u + 2)
            for j in range(u + 1):
                last = pe.matmul(bank[7][:, 0:HD], scr[:, 2, j * P:(j + 1) * P],
                                 mvtok[:, j, bass.ds(pair * P + par * HD, HD)], start=(j == 0), stop=(j == u))
            last.then_inc(s_pv, 1)

        def keys(b, par, g):
            if g % 4 == 0:
                pe.wait_ge(s_le, 2 * b + g // 4 + 1)
            pe.wait_ge(s_kt, NGRP * b + g + 1)
            for jj in range(4):
                for gq in range(4):
                    j = 4 * gq + jj
                    last = pe.matmul(bank[g // 4][32 * gq:32 * gq + 32, (g % 4) * P:(g % 4 + 1) * P],
                                     qbd[par][:, j, :], KTb[g % 2][:, :, j, :], start=(jj == 0), stop=(jj == 3))
            last.then_inc(s_lg, 1)

        def own_keys(b, par):
            for jj in range(4):
                for gq in range(4):
                    j = 4 * gq + jj
                    last = pe.matmul(bank[3][32 * gq:32 * gq + 32, 64:64 + S], qbd[par][0:32, j, :], kbb[0:32, j, :],
                                     start=(jj == 0), stop=(jj == 3))
            last.then_inc(s_own, 1)

        def weigh_pages(b, g):
            for pg in range(GRP):
                s = (4 * g + pg) % 8
                pe.wait_ge(s_v[s], 16 * (4 * b + (4 * g + pg) // 8 + 1))
                pe.matmul(bank[4][32 * pg:32 * pg + 32, :], pT[:, g, 32 * pg:32 * pg + 32],
                          VB[s][:, :], start=(g == 0), stop=(g == NGRP - 1)).then_inc(s_vd, 1)

        def turn_probs(b, e):
            pe.wait_ge(s_ex, 2 * b + e + 1)
            if e:
                pe.wait_ge(s_te, 2 * b + 1)
            for g in range(4):
                last = pe.transpose(bank[2][:, g * P:(g + 1) * P], pe_x[:, 4 * e + g, :], ident)
            last.then_inc(s_tp, 1)

        def fold(b):
            pe.wait_ge(s_of, b + 1)
            pe.matmul(bank[3][0:32, 128:128 + HD], C("sum_pv"), sm[:, 832:896], start=True, stop=True).then_inc(s_oe, 1)

        def step(b, par, head=True, tail=True, rest=True):
            pair = b // 2 if isinstance(b, int) else (b - par) // 2
            prev = b - 1
            if head:
                pe.wait_ge(s_qd, b + 1)
                pe.wait_ge(s_qk, pair + 1)
            for slot in range(8):
                if head:
                    keys(b, par, slot)
                if tail and rest and slot == 0:
                    pe.wait_ge(s_oa, prev - 1)
                if rest and slot < 5:
                    weigh_pages(b - 2, slot + 3)
                if tail and slot == 0:
                    own_keys(prev, 1 - par)
                if tail and slot == 1:
                    pe.wait_ge(s_s1, prev + 1)
                    for n, name in enumerate(("pair0", "pair1", "own_pair")):
                        last = pe.matmul(bank[3][:, n * NGRP:(n + 1) * NGRP], C(name), sm[:, 0:NGRP], start=True, stop=True)
                    last.then_inc(s_gt, 1)
                if tail and slot == 2:
                    pe.wait_ge(s_mx, prev + 1)
                    pe.transpose(bank[3][0:1, 0:P], sm[:, 56:57], ident).then_inc(s_mxt, 1)
                if head and slot % 2:
                    turn(b, slot // 2)
                elif head:
                    if slot:
                        weigh(b, pair, par, slot // 2 - 1)
                    scores(b, pair, par, slot // 2)
                if tail and slot == 2:
                    pe.wait_ge(s_rm, prev + 1)
                    pe.matmul(bank[3][:, 0:1], sm[0:1, 384:512], ones[0:1, 0:1], start=True, stop=True).then_inc(s_mb, 1)
                if tail and slot in (3, 4):
                    turn_probs(prev, slot - 3)
                if tail and slot == 4:
                    pe.transpose(bank[3][0:S, 0:P], sm[:, 576:608], ident).then_inc(s_tt, 1)
                if tail and slot == 5:
                    pe.wait_ge(s_rsm, prev + 1)
                    pe.wait_ge(s_to, prev + 1)
                    pe.matmul(bank[3][0:32, 0:1], C("sum_g"), sm[:, 650:651], start=True, stop=True).then_inc(s_den, 1)
                    pe.wait_ge(s_te, 2 * prev + 2)
                    if rest:
                        pe.wait_ge(s_of, prev)
                if tail and slot >= 5:
                    weigh_pages(prev, slot - 5)
                if tail and slot == 5:
                    pe.matmul(bank[4][0:32, :], sm[0:S, 704:736], zs[:, 6 * W:7 * W], start=False, stop=False)
                if rest and slot == 6:
                    if tail:
                        pe.wait_ge(s_rcp, prev + 1)
                    fold(b - 2)
            if head:
                weigh(b, pair, par, 3)

        moba_steps(pe, step)
        for g in (3, 4):
            weigh_pages(NB_SEQ - 1, g)
        pe.wait_ge(s_hn, 2)
        for k in range(KT):
            src = rettok if k < 4 else mobatok
            if k >= 2:
                pe.wait_ge(s_stg, KT + k - 1)
            turn_rows(lambda i: src[:, i, (k % 4) * P:(k % 4 + 1) * P], k, KT + k, bank[k % 2])
            if k < 3:
                weigh_pages(NB_SEQ - 1, 5 + k)
        fold(NB_SEQ - 1)
        pe.wait_ge(s_hlo, 2 * KT)
        for q in range(2):
            pe.wait_ge(s_ev, F_OUT + q + 1)
            tile(F_OUT + q, q)
        pe.wait_ge(s_ofr, 1)
        for b in range(NB_SEQ):
            last = pe.transpose(bank[5][0:HD, b * 32:(b + 1) * 32], oall[:, b, :], ident[0:32, 0:32])
        last.then_inc(s_oft, 1)

        pe.wait_ge(s_x2l, 16)
        for k in range(KT):
            if k >= 2:
                pe.wait_ge(s_xr, k - 1)
            turn_rows(lambda i: xP2[:, i, k * P:(k + 1) * P], k, 2 * KT + k)

        def gates_to_rows(n):
            pe.wait_ge(s_hs, 2 + 2 * n)
            for k in range(KT):
                last = pe.transpose(bank[6 + k // 4][0:S, (k % 4) * P:(k % 4 + 1) * P], asm[:, k * S:(k + 1) * S], ident)
            last.then_inc(s_gmt, 1)

        gates_to_rows(0)
        pe.wait_ge(s_oas, 1)

        def sum_squares(k):
            pe.wait_ge(s_sqx, k + 1)
            pe.matmul(bank[2][:, :], ones, stage[k % 2][:, :], start=(k == 0), stop=(k == KT - 1)).then_inc(s_ssm, 1)

        pe.wait_ge(s_xr, KT)
        for f in range(1, KT):
            if f >= 2:
                pe.wait_ge(s_ev, F_OUT + f + 1)
                tile(F_OUT + f, f % 4)
                sum_squares(f - 2)
            if f % 2:
                pe.wait_ge(s_sev, N_OUT + f // 2 + 1)
                sample_chunk(f // 2 % 2, N_OUT, lambda k: asT[:, k, :])
        sum_squares(KT - 2)
        sum_squares(KT - 1)
        pe.wait_ge(s_x2n, 1)
        for k in range(KT):
            last = pe.transpose(bank[7][:, k * S:(k + 1) * S], xsn2[:, k * P:(k + 1) * P], ident[0:S, 0:S])
        last.then_inc(s_xst, 1)

        def turn_ff(n):
            pe.wait_ge(s_sev, N_FFN + n + 3)
            pe.transpose(bank[7][:, 0:P], asm[:, 64:192], ident).then_inc(s_smt, 1)

        def turn_before(i, q):
            if q % 2 == 0 and not (isinstance(i, int) and i + q == 0):
                turn_ff(2 * i + q // 2 - 1)

        stage_pair(F_FFN, N_FFN, 0, turn_before, ready=2 * KT, sample_ready=3)
        with pe.Fori(1, FT // 2) as i:
            stage_pair(F_FFN, N_FFN, i, turn_before)
        turn_ff(FT - 1)
        gates_to_rows(1)
        pe.wait_ge(s_fl, FT + 1)
        pe.wait_ge(s_sme, FT)
        c = 0
        for fb in range(DM // CHUNK):
            for n, kd in enumerate(KD):
                for half in range(2):
                    if n == 0 and fb != 1:
                        pe.wait_ge(s_ev, F_DOWN + half + (2 * fb - 1 if fb else 1))
                    tile(F_DOWN + 2 * c + half, half, kd, fhi, flo, 8 * n, bank[2 * (fb % 2) + half], n == 0, n == 2)
                if n == 0:
                    pe.wait_ge(s_sev, N_DOWN + fb + 1)
                sample_chunk(c % 2, 0, lambda k: aT[:, 8 * n + k, :], kd, n == 0, n == 2, bank[4 + fb % 2])
                c += 1
        pe.wait_ge(s_ev, F_DOWN + 8 + 2)
        for i in range(TT):
            if i >= 2:
                pe.wait_ge(s_y, i - 1)
            for k in range(KT):
                last = pe.transpose(bank[2 * (i % 2) + k // 4][:, (k % 4) * P:(k % 4 + 1) * P], x2T[:, k, i * P:(i + 1) * P], ident)
            last.then_inc(s_yt, 1)

    @block.vector
    def _(dve):
        tt, ts, cp = dve.tensor_tensor, dve.tensor_scalar, dve.tensor_copy
        for s in (s_ev, s_sev):
            dve.sem_inc(s, 2)
        for s in (s_fl, s_mp, s_on):
            dve.sem_inc(s, 1)
        dve.memset(cT[:, :, :], 0.0)
        dve.drain()

        def then(ins):
            dve.drain()
            return ins

        dve.wait_ge(s_ctp, 1)
        cp(cT[:, :, 0:NSEQ], bank[4][:, 0:KT * NSEQ].rearrange("p (k s) -> p k s", k=KT)).then_inc(s_ct, 1)
        dve.wait_ge(s_vtp, 1)
        then(cp(vT[:, :], bank[5][:, 0:NVEC]))
        dve.wait_ge(s_pt, 16)
        dve.wait_ge(s_const, 16)
        for g in range(GRP):
            q = slice(32 * g, 32 * g + 32)
            last = ts(kidx[q, :], pt[q, :].rearrange("p (n g) -> p n g", g=GRP)[:, :, g], 32.0, C("row32")[q, :], ALU.mult, ALU.add)
        last.then_inc(s_idx, 1)
        dve.wait_ge(s_sqd, 1)
        ts(st2[:, 8:12], st[:, 0:4], 1.0 / DM, EPS, ALU.mult, ALU.add)
        then(ts(st2[0:S, 12:13], st[0:S, 4:5], 1.0 / DM, EPS, ALU.mult, ALU.add))
        dve.reciprocal(st2[:, 8:12], st2[:, 8:12])
        dve.reciprocal(st2[0:S, 12:13], st2[0:S, 12:13])
        dve.drain().then_inc(s_rin, 1)

        def modulation(pair):
            dve.wait_ge(s_mtp, pair + 2)
            src = bank[3][:, 0:P].rearrange("p (f h2 s) -> p f h2 s", f=2, h2=2)
            for e in range(2):
                for h2 in range(2):
                    rows, f = slice(64 * h2, 64 * h2 + 64), bass.ds(4 * pair + 2 * e, 2)
                    tt(mT[rows, f, :], src[64 * e:64 * e + 64, :, h2, 0:NSEQ],
                       vT[rows, f].unsqueeze(2).broadcast_to((64, 2, NSEQ)), ALU.add)
            dve.drain().then_inc(s_mp, 1)

        def gains(f0, v0):
            dve.scalar_tensor_tensor(gain[:, :, :], mT[:, f0:f0 + KT, :], 1.0,
                                     vT[:, v0:v0 + KT].unsqueeze(2).broadcast_to((P, KT, NSEQ)), ALU.add, ALU.mult)
            dve.drain().then_inc(s_mt, 1)

        with dve.Fori(0, NMA // 2) as i:
            modulation(i)
        gains(8, V_N1)

        def act_lo(k, n):
            dve.wait_ge(s_hhi, n + 1)
            tt(alo[:, k, :], stage[k % 2][:, :], ahi[:, k, :].bitcast(F32), ALU.subtract).then_inc(s_hlo, 1)

        def split_lo(m, q, kd=KT):
            dve.wait_ge(s_hi, m + 1)
            tt(wlo[q % 2][:, 0:kd, :], raw[q // 2][:, 0:kd, q % 2 * P:(q % 2 + 1) * P],
               whi[q % 2][:, 0:kd, :].bitcast(F32), ALU.subtract).then_inc(s_lo, 1)

        split_lo(0, 0)
        for k in range(KT):
            act_lo(k, k)

        def by_seq(x):
            return x.unsqueeze(3).broadcast_to((P, KT, NB_SEQ, TS))

        asT4 = asT[:, :, :].rearrange("p k (b t) -> p k b t", t=TS)

        def sample_h(n, f_shift):
            dve.wait_ge(s_xst, n)
            then(tt(asT4, bank[7][:, 0:KT * S].rearrange("p (k b t) -> p k b t", k=KT, t=TS), by_seq(gain[:, :, 0:NB_SEQ]), ALU.mult))
            tt(asT4, asT4, by_seq(mT[:, f_shift:f_shift + KT, 0:NB_SEQ]), ALU.add).then_inc(s_hs, 1)

        sample_h(1, 0)

        def stage_pairs(F, pairs, evict, sample, peel=False):

            def body(i, last):
                for q in range(4):
                    if not (last and q == 3):
                        split_lo(F + 4 * i + q + 1, (q + 1) % 4)
                    if evict:
                        evict(i, q)
                    if q % 2:
                        sample(i, q // 2)

            if peel:
                body(0, False)
            with dve.Fori(int(peel), pairs - 1) as i:
                body(i, False)
            body(pairs - 1, True)

        def sample_z(i, u):
            dve.wait_ge(s_ss, 2 * i + u + 1)
            for g in range(4):
                last = cp(zs[:, bass.ds((2 * i + u) * CHUNK + 64 * g, 64)], bank[4 + u][32 * g:32 * g + 32, 0:64])
            last.then_inc(s_sev, 1)

        def mod_pair_before(i, q):
            if q == 0 and not (isinstance(i, int) and i == 0):
                modulation(NMA // 2 + i - 1)

        stage_pairs(0, NIN // 2, mod_pair_before, sample_z, peel=True)
        for pair in (NMOD // 2 - 2, NMOD // 2 - 1):
            modulation(pair)
        n = 0
        for dst in (scr, mvtok, rvtok):
            for j in range(4):
                dve.wait_ge(s_vt1, n + 1)
                cp(dst[:, 0:4, j * P:(j + 1) * P], bank[2 + n % 2][:, :].rearrange("p (i f) -> p i f", i=TT)).then_inc(s_vt2, 1)
                n += 1
        dec3 = C("decay")
        dve.wait_ge(s_kst, 16)
        with dve.Fori(0, HP) as hp:
            for n, sec in enumerate((RQ, RK)):
                dve.wait_ge(s_rr, 2 * hp + n + 1)
                tt(scr[:, 3, :], zT[:, bass.ds(sec + hp, 1), :].rearrange("p a t -> p (a t)"), C("cos"), ALU.mult)
                then(tt(stage[0][:, :], bank[n][:, :], C("sin"), ALU.mult))
                then(tt(scr[:, n, :], scr[:, 3, :], stage[0][:, :], ALU.add))
                if n == 0:
                    then(tt(scr[:, 2, :].rearrange("p (c i) -> p c i", c=4), scr[:, 0, :].rearrange("p (c i) -> p c i", c=4),
                            C("q_dec")[:, bass.ds(hp, 1), :].broadcast_to((P, 4, P)), ALU.mult))
                if n == 0:
                    dve.drain()
                else:
                    dve.drain().then_inc(s_rk, 1)
            dve.wait_ge(s_kt1, hp + 1)
            tt(scr[:, 4, :].rearrange("p (c h d) -> p c h d", c=4, h=2), bank[2][:, :].rearrange("p (c h d) -> p c h d", c=4, h=2),
               C("k_dec")[:, bass.ds(2 * hp, 2)].unsqueeze(1).unsqueeze(3).broadcast_to((P, 4, 2, HD)), ALU.mult).then_inc(s_kt2, 1)
            dve.wait_ge(s_ra, hp + 1)
            for h2 in range(2):
                last = tt(scr[:, 5 + h2, :].rearrange("p (c i) -> p c i", c=4), bank[4 + h2][:, :].rearrange("p (c i) -> p c i", c=4),
                          dec3[:, bass.ds(2 * hp + h2, 1), :].broadcast_to((P, 4, P)), ALU.mult)
            last.then_inc(s_rad, 1)
            dve.wait_ge(s_kv, hp + 1)
            dve.wait_ge(s_rs, 16 * hp + 16)
            for c in range(TT):
                for h2 in range(2):
                    r = 64 * h2
                    kv = bank[3][r:r + 64, c * P + r:c * P + r + HD]
                    if c == 0:
                        cp(sst[r:r + 64, 0, :], kv)
                    else:
                        dve.scalar_tensor_tensor(sst[r:r + 64, c, :], sst[r:r + 64, c - 1, :],
                                                 C("c_dec")[r:r + 64, bass.ds(hp, 1)], kv, ALU.mult, ALU.add)
                if c < TT - 1:
                    dve.drain()
                else:
                    dve.drain().then_inc(s_st, 1)
            dve.wait_ge(s_ro, hp + 1)
        dve.wait_ge(s_rs, 16 * HP + 16)
        cos = C("cos_s").unsqueeze(1).broadcast_to((S, H, 32))
        sin = C("sin_s").unsqueeze(1).broadcast_to((S, H, 32))
        ta = kmask[0][:, 0:256].rearrange("p (h d) -> p h d", h=H)
        tb = kmask[1][:, 0:256].rearrange("p (h d) -> p h d", h=H)
        for n, dst in enumerate((qrs, krs)):
            z = zs[:, n * W:(n + 1) * W].rearrange("p (h c d) -> p h c d", h=H, c=2)
            o = dst[:, :].rearrange("p (h c d) -> p h c d", h=H, c=2)
            tt(ta, z[:, :, 0, :], cos, ALU.mult)
            then(tt(tb, z[:, :, 1, :], sin, ALU.mult))
            then(tt(o[:, :, 0, :], ta, tb, ALU.subtract))
            tt(ta, z[:, :, 1, :], cos, ALU.mult)
            then(tt(tb, z[:, :, 0, :], sin, ALU.mult))
            then(tt(o[:, :, 1, :], ta, tb, ALU.add))
        dve.drain().then_inc(s_srot, 1)
        dve.wait_ge(s_sqt, 1)
        cp(sT[:, 0, :, :], bank[0][:, 0:P].rearrange("p (h s) -> p h s", h=HP))
        then(cp(sT[:, 1, :, :], bank[0][:, P:2 * P].rearrange("p (h s) -> p h s", h=HP)))
        tt(sT[:, 2, :, :], sT[:, 0, :, :], C("q_dec_s"), ALU.mult).then_inc(s_sqe, 1)
        dve.wait_ge(s_sa, 1)
        byh2 = lambda x: x.rearrange("p (hp h2) s -> p h2 hp s", h2=2)
        for h2 in range(2):
            last = tt(byh2(ats[:, :, :])[:, h2], bank[4 + h2][0:S, 0:P].rearrange("p (h s) -> p h s", h=HP),
                      byh2(C("decay_s"))[:, h2], ALU.mult)
        last.then_inc(s_sad, 1)
        dve.wait_ge(s_so, 1)
        for h2 in range(2):
            r = 64 * h2
            last = cp(sT[r:r + 64, 0, :, :], bank[6 + h2][r:r + 64, 0:P].rearrange("p (h s) -> p h s", h=HP))
        last.then_inc(s_soc, 1)
        cd = C("c_dec_s").unsqueeze(1).unsqueeze(3).broadcast_to((P, NB_SEQ, HP, HD))
        then(tt(state[:, :, :, :], state[:, :, :, :], cd, ALU.mult))

        def masked_k(b):
            if b >= 2:
                dve.wait_ge(s_kvs, b - 1)
            tt(kmask[b % 2][:, :].rearrange("p (h d) -> p h d", h=H), krs[:, :].rearrange("p (h d) -> p h d", h=H),
               C("k_dec_s")[:, b, :].unsqueeze(2).broadcast_to((S, H, HD)), ALU.mult).then_inc(s_km, 1)

        masked_k(0)
        for b in range(NB_SEQ):
            if b < NB_SEQ - 1:
                masked_k(b + 1)
            dve.wait_ge(s_kvs, b + 1)
            for h2 in range(2):
                r = 64 * h2
                last = tt(state[r:r + 64, b, :, :], state[r:r + 64, b, :, :],
                          bank[2 + b % 2][r:r + 64, :].rearrange("p (h c) -> p h c", h=HP)[:, :, r:r + HD], ALU.add)
            last.then_inc(s_sts, 1)
        dve.wait_ge(s_sot, 1)
        dve.wait_ge(s_ssg, 1)
        r3 = ret_s[:, :].rearrange("p (h d) -> p h d", h=H)
        k3 = kmask[0][:, :].rearrange("p (h d) -> p h d", h=H)
        sp3 = lambda x: x.unsqueeze(2).broadcast_to((S, H, HD))
        dve.drain()
        dve.wait_ge(s_kvs, NB_SEQ)
        then(dve.tensor_reduce(st[0:S, 0:H], bank[0][0:S, :].rearrange("p (h d) -> p h d", h=H), AX.X, ALU.add))
        then(ts(st[0:S, 0:H], st[0:S, 0:H], 1.0 / HD, None, ALU.mult))
        then(tt(r3, bank[0][0:S, :].rearrange("p (h d) -> p h d", h=H), sp3(st[0:S, 0:H]), ALU.subtract))
        then(tt(k3, r3, r3, ALU.mult))
        then(dve.tensor_reduce(st[0:S, 8:8 + H], k3, AX.X, ALU.add))
        then(ts(st2[0:S, 8:8 + H], st[0:S, 8:8 + H], 1.0 / HD, EPS, ALU.mult, ALU.add))
        dve.reciprocal(st2[0:S, 8:8 + H], st2[0:S, 8:8 + H]).then_inc(s_ssq, 1)
        dve.wait_ge(s_srs, 1)
        then(tt(r3, r3, sp3(st2[0:S, 0:H]), ALU.mult))
        tt(ret_s[:, :], ret_s[:, :], zs[:, 3 * W:4 * W], ALU.mult).then_inc(s_srn, 1)
        dve.wait_ge(s_srt, 1)
        tt(asT[:, 0:4, :], bank[1][:, 0:P].rearrange("p (h s) -> p h s", h=HP),
           vT[:, V_GN:V_GN + 4].unsqueeze(2).broadcast_to((P, HP, S)), ALU.mult).then_inc(s_sas, 1)

        def negmax(b, u):
            n = (u + 1) * P
            dve.wait_ge(s_sc, 4 * b + u + 1)
            then(tt(bank[5][:, n - P:n], bank[5][:, n - P:n], C("causal"), ALU.add))
            then(dve.tensor_reduce(st2[:, 16 + u % 2:17 + u % 2], bank[5][:, 0:n], AX.X, ALU.max))
            then(ts(st2[:, 20 + u % 2:21 + u % 2], st2[:, 16 + u % 2:17 + u % 2], -SCALE, None, ALU.mult)).then_inc(s_nm, 1)

        def norm(b, pair, par, u):
            dve.wait_ge(s_pv, 4 * b + u + 2)
            then(dve.reciprocal(st2[:, 24 + u % 2:25 + u % 2], st[:, 16 + u:17 + u]))
            then(ts(mobatok[:, u, bass.ds(pair * P + par * HD, HD)], bank[7][:, 0:HD],
                    st2[:, 24 + u % 2:25 + u % 2], None, ALU.mult)).then_inc(s_on, 1)

        def turn_keys(b, g):
            dve.wait_ge(s_k[g % 4], 16 * (2 * b + g // 4 + 1))
            dve.wait_ge(s_lg, NGRP * b + g + 1)
            dve.transpose(KTb[g % 2][:, :, :, :], Kb[g % 4][:, :]).then_inc(s_kt, 1)

        def block_diagonal(b, par):
            qv = qbd[par][:, :, :].rearrange("p (g hh half) c -> p g hh half c", g=4, hh=2)
            qi = qbb[0:32, :, :].rearrange("p (g hh half) s -> p g hh half s", g=4, hh=2)
            for pg in range(GRP):
                for hh in range(2):
                    cp(qv[32 * pg:32 * pg + 32, :, hh, :, hh * 16 + pg * 4:hh * 16 + pg * 4 + 4],
                       qi[:, :, hh, :, bass.ds(TS * b, TS)])
            dve.drain().then_inc(s_qd, 1)

        def block_sums(b):
            dve.wait_ge(s_le, 2 * b + 4)
            dve.tensor_reduce(sm[:, 0:NGRP], lgs[:, :, :], AX.X, ALU.add)
            dve.tensor_reduce(sm[:, 8:8 + NGRP], lgs[:, :, :], AX.X, ALU.max)
            dve.wait_ge(s_own, b + 1)
            tt(sm[:, 512:544], bank[3][:, 64:64 + S], C("own_mask")[:, bass.ds(b, 1), :].rearrange("p a s -> p (a s)"), ALU.add)
            dve.drain().then_inc(s_s1, 1)

        def select(b):
            dve.wait_ge(s_gt, b + 1)
            cp(sm[:, 16:32].rearrange("p (g e) -> p e g", e=2), bank[3][:, 0:16].rearrange("p (e g) -> p e g", e=2))
            then(cp(sm[:, 32:40], bank[3][:, 16:24]))
            gall = sm[:, 16:32].unsqueeze(1).broadcast_to((P, NGRP, NBLK))
            gown = sm[:, 32:40].unsqueeze(2).broadcast_to((P, NGRP, NBLK))
            gt = sm[:, 64:192].rearrange("p (n m) -> p n m", n=NGRP)
            eq = sm[:, 192:320].rearrange("p (n m) -> p n m", n=NGRP)
            tt(gt, gall, gown, ALU.is_gt)
            then(tt(eq, gall, gown, ALU.is_equal))
            then(tt(eq, eq, C("earlier"), ALU.mult))
            then(tt(gt, gt, eq, ALU.add))
            then(dve.tensor_reduce(sm[:, 40:48], gt, AX.X, ALU.add))
            then(ts(sm[:, 48:56], sm[:, 40:48], TOPK - 0.5, -BIG, ALU.is_gt, ALU.mult))
            then(tt(sm[:, 8:16], sm[:, 8:16], sm[:, 48:56], ALU.add))
            dve.tensor_reduce(sm[:, 57:58], sm[:, 8:16], AX.X, ALU.max)
            then(dve.tensor_reduce(sm[:, 58:59], sm[:, 512:544], AX.X, ALU.max))
            then(tt(sm[:, 56:57], sm[:, 57:58], sm[:, 58:59], ALU.max)).then_inc(s_mx, 1)

        def row_max(b):
            dve.wait_ge(s_mxt, b + 1)
            then(dve.tensor_reduce(sm[0:1, 900:932], bank[3][0:1, 0:P].rearrange("p (h g t) -> p h t g", g=4, t=4), AX.X, ALU.max))
            then(cp(sm[0:1, 384:512].rearrange("p (h g t) -> p h g t", g=4, t=4),
                    sm[0:1, 900:932].rearrange("p (h t) -> p h t", t=4).unsqueeze(2).broadcast_to((1, 8, 4, 4)))).then_inc(s_rm, 1)

        def exp_bias(b):
            dve.wait_ge(s_mb, b + 1)
            then(ts(sm[:, 328:329], bank[3][:, 0:1], -SCALE, None, ALU.mult))
            then(ts(sm[:, 320:328], sm[:, 48:56], SCALE, sm[:, 328:329], ALU.mult, ALU.add)).then_inc(s_nb, 1)

        def denominators(b):
            dve.wait_ge(s_ex, 2 * b + 2)
            dve.tensor_reduce(sm[:, 650:651], sm[:, 640:649], AX.X, ALU.add).then_inc(s_rsm, 1)
            dve.wait_ge(s_tt, b + 1)
            cp(by_page(sm[0:S, 704:832]), turned(bank[3][0:S, 0:P])).then_inc(s_to, 1)

        def fold_heads(b):
            dve.wait_ge(s_vd, NPAGE * (b + 1))
            then(tt(od[:, :, :], bank[4][:, :].rearrange("p (h d) -> p h d", h=H),
                    C("head_diag").unsqueeze(2).broadcast_to((P, H, HD)), ALU.mult))
            then(dve.tensor_reduce(sm[:, 832:896], od[:, :, :].rearrange("p h d -> p d h"), AX.X, ALU.add)).then_inc(s_of, 1)

        def keep_out(b, par):
            dve.wait_ge(s_oe, b + 1)
            then(ts(oall[:, bass.ds(b, 1), :].rearrange("p a d -> p (a d)"), bank[3][0:32, 128:128 + HD],
                    sm[0:32, 940 + par:941 + par], None, ALU.mult)).then_inc(s_oa, 1)

        heads = lambda x: x.rearrange("p i (h d) -> p i h d", h=H)
        s1 = gain[:, 0:4, 0:8]
        s2 = gain[:, 4:8, 0:8]
        spread = lambda x: x.unsqueeze(3).broadcast_to((P, TT, H, HD))

        def centre_retention():
            dve.wait_ge(s_roc, 2 * HP + 1)
            then(dve.tensor_reduce(s1, heads(rettok), AX.X, ALU.add))
            then(ts(s1, s1, 1.0 / HD, None, ALU.mult))
            then(tt(heads(rettok), heads(rettok), spread(s1), ALU.subtract)).then_inc(s_hn, 1)

        def step(b, par, head=True, tail=True, rest=True):
            pair = b // 2 if isinstance(b, int) else (b - par) // 2
            prev = b - 1
            first, last_head = isinstance(b, int) and b == 0, isinstance(b, int) and b >= NB_SEQ - 1
            for slot in range(8):
                if head and slot < 7:
                    turn_keys(b, slot + 1)
                elif head and not last_head:
                    block_diagonal(b + 1, 1 - par)
                    turn_keys(b + 1, 0)
                if tail and slot == 0:
                    block_sums(prev)
                if tail and slot == 1:
                    select(prev)
                if tail and slot == 2:
                    row_max(prev)
                if head and slot % 2 == 0:
                    negmax(b, slot // 2)
                elif slot > 1 and head:
                    norm(b, pair, par, slot // 2 - 1)
                elif slot == 1 and not first and (head or tail):
                    norm(prev, (prev - (1 - par)) // 2, 1 - par, 3)
                if tail and slot == 2:
                    exp_bias(prev)
                if not head and slot == 3:
                    centre_retention()
                if rest and slot == 4:
                    fold_heads(b - 2)
                if tail and slot == 4:
                    denominators(prev)
                if tail and slot == 5:
                    dve.wait_ge(s_den, prev + 1)
                    then(dve.reciprocal(sm[0:32, 941 - par:942 - par], bank[3][0:32, 0:1])).then_inc(s_rcp, 1)
                if rest and slot == 6:
                    keep_out(b - 2, par)
        dve.wait_ge(s_sas, 1)
        dve.wait_ge(s_sst, 16)
        dve.transpose(qbb[0:32, :, :], zs[:, 4 * W:5 * W])
        dve.transpose(kbb[0:32, :, :], zs[:, 5 * W:6 * W])
        for x in qbd:
            dve.memset(x[:, :, :], 0.0)
        dve.drain()
        block_diagonal(0, 0)
        turn_keys(0, 0)
        moba_steps(dve, step)
        dve.wait_ge(s_hsq, 1)
        dve.drain()
        dve.tensor_reduce(s1, heads(sq_ret), AX.X, ALU.add)
        then(dve.tensor_reduce(s2, heads(sq_moba), AX.X, ALU.add))
        both = gain[:, :, 0:8]
        then(ts(both, both, 1.0 / HD, EPS, ALU.mult, ALU.add))
        dve.reciprocal(both, both).then_inc(s_hri, 1)
        dve.wait_ge(s_hrs, 1)
        tt(heads(rettok), heads(rettok), spread(s1), ALU.mult)
        tt(heads(mobatok), heads(mobatok), spread(s2), ALU.mult).then_inc(s_hn, 1)
        dve.wait_ge(s_sg, 1)
        for k in range(KT):
            dve.wait_ge(s_xt, KT + k + 1)
            if k < 4:
                dve.scalar_tensor_tensor(stage[k % 2][:, :], bank[k % 2][:, :], vT[:, V_GN + k:V_GN + k + 1],
                                         zT[:, RG + k, :], ALU.mult, ALU.mult).then_inc(s_stg, 1)
            else:
                ts(stage[k % 2][:, :], bank[k % 2][:, :], vT[:, V_MN + k - 4:V_MN + k - 3], None, ALU.mult).then_inc(s_stg, 1)
            act_lo(k, KT + k)
            dve.drain()
        fold_heads(NB_SEQ - 1)
        keep_out(NB_SEQ - 1, 1)
        for q in range(2):
            split_lo(F_OUT + q, q)
        dve.drain()
        o2 = sm[0:32, 0:512].rearrange("p (b d) -> p b d", b=NB_SEQ)
        then(tt(o2, oall[:, :, :], oall[:, :, :], ALU.mult))
        then(dve.tensor_reduce(st[0:32, 0:8], o2, AX.X, ALU.add))
        then(ts(st2[0:32, 8:16], st[0:32, 0:8], 1.0 / HD, EPS, ALU.mult, ALU.add))
        dve.reciprocal(st2[0:32, 8:16], st2[0:32, 8:16]).then_inc(s_ofs, 1)
        dve.wait_ge(s_ofq, 1)
        tt(oall[:, :, :], oall[:, :, :], st2[0:32, 0:8].unsqueeze(2).broadcast_to((32, NB_SEQ, HD)), ALU.mult).then_inc(s_ofr, 1)
        dve.wait_ge(s_oft, 1)
        for h2 in range(2):
            for hp in range(HP):
                ob = bank[5][0:HD, 0:256].rearrange("p (b h t) -> p h b t", b=NB_SEQ, t=TS)[:, 2 * hp + h2]
                cp(asT[64 * h2:64 * h2 + 64, 4 + hp, :].rearrange("p (b t) -> p b t", t=TS), ob)
        dve.drain()
        tt(asT[:, 4:8, :], asT[:, 4:8, :], vT[:, V_MN:V_MN + 4].unsqueeze(2).broadcast_to((P, HP, S)), ALU.mult)
        dve.drain().then_inc(s_oas, 1)

        asm4 = asm[:, 0:256].rearrange("p (k b t) -> p k b t", k=KT, t=TS)

        def gates(f0, n, dst):
            cp(asm4, by_seq(mT[:, f0:f0 + KT, 0:NB_SEQ]))
            dve.drain().then_inc(s_hs, 1)
            dve.wait_ge(s_gmt, n + 1)
            for e in range(2):
                cp(dst[:, e * 512:(e + 1) * 512], bank[6 + e][0:S, :])
            dve.drain()

        gates(16, 0, gmod)
        dve.wait_ge(s_xr, KT)

        def residual(f, gate_col, out):
            g = mT[:, gate_col, NB_SEQ:NSEQ]
            dve.scalar_tensor_tensor(x2T[:, f, :], out[:, :], g, x2T[:, f, :], ALU.mult, ALU.add).then_inc(s_ev, 1)

        def evict_out(i, q):
            f = 4 * i + q
            dve.wait_ge(s_ft, F_OUT + f + 3)
            residual(f, 16 + f, bank[q % 2])

        def sample_rows(n, at, src, g, base):
            for e in range(4):
                c = slice(at + 64 * e, at + 64 * e + 64)
                tt(xtmp[:, 64 * e:64 * e + 64], src[32 * e:32 * e + 32, 0:64], g[:, c], ALU.mult)
            dve.drain().then_inc(s_sev, 1)
            tt(x2s[:, at:at + CHUNK], base[:, at:at + CHUNK], xtmp[:, 0:256], ALU.add)
            dve.drain()

        def sample_out(i, u):
            dve.wait_ge(s_ss, N_OUT + 2 * i + u + 1)
            sample_rows(2 * i + u, (2 * i + u) * CHUNK, bank[4 + u], gmod, xs)

        for f in range(KT):
            if 2 <= f + 1 < KT:
                split_lo(F_OUT + f + 1, (f + 1) % 4)
            evict_out(f // 4, f % 4)
            if f % 2:
                sample_out(f // 4, f % 4 // 2)
        dve.drain().then_inc(s_x2s, 1)
        gains(32, V_N2)
        split_lo(F_FFN, 0)
        dve.wait_ge(s_ssm, KT)
        then(ts(rb[:, :], bank[2][:, :], 1.0 / DM, EPS, ALU.mult, ALU.add))
        dve.reciprocal(rb[:, :], rb[:, :]).then_inc(s_r1, 1)
        dve.wait_ge(s_x2q, 1)
        then(ts(st2[0:S, 0:1], st[0:S, 0:1], 1.0 / DM, EPS, ALU.mult, ALU.add))
        dve.reciprocal(st2[0:S, 0:1], st2[0:S, 0:1]).then_inc(s_x2i, 1)
        dve.wait_ge(s_r2, 1)
        for k in range(KT):
            tt(stage[k % 2][:, :], x2T[:, k, :], rb[:, :], ALU.mult).then_inc(s_nx, 1)
            if k >= 1:
                act_lo(k - 1, 2 * KT + k - 1)
                dve.drain()
        act_lo(KT - 1, 3 * KT - 1)
        sample_h(2, 24)

        def evict_ffn(i, q):
            n = 2 * i + q // 2
            if q % 2 == 0 and not (isinstance(n, int) and n == 0):
                keep_turned(n - 1)
            if q % 2:
                dve.wait_ge(s_ft, F_FFN + 4 * i + q + 3)
                dve.wait_ge(s_ev, F_FFN + 4 * i + q + 2)
                tt(stage[1][:, :], stage[0][:, :], bank[1][:, :], ALU.mult).then_inc(s_ev, 1)
                dve.wait_ge(s_fh, n + 1)
                tt(flo[:, bass.ds(n, 1), :].rearrange("p a t -> p (a t)"), stage[1][:, :],
                   fhi[:, bass.ds(n, 1), :].rearrange("p a t -> p (a t)").bitcast(F32), ALU.subtract)
                dve.drain().then_inc(s_fl, 1)

        def sample_ffn(i, u):
            n = 2 * i + u
            dve.wait_ge(s_ssl, n + 1)
            tt(asm[0:64, 64:128], asm[0:64, 0:64], bank[4 + u][64:128, 0:64], ALU.mult).then_inc(s_sev, 1)

        def keep_turned(n):
            dve.wait_ge(s_smt, n + 1)
            for e in range(2):
                cp(aT[64 * e:64 * e + 64, bass.ds(n, 1), :].rearrange("p a s -> p (a s)"), bank[7][0:64, 32 * e:32 * e + 32])
            dve.drain().then_inc(s_sme, 1)

        stage_pairs(F_FFN, FT // 2, evict_ffn, sample_ffn, peel=True)
        keep_turned(FT - 1)
        gates(40, 1, gmod2)

        def evict_down(fb, half):
            dve.wait_ge(s_ft, F_DOWN + 6 * fb + 4 + half + 3)
            residual(2 * fb + half, 40 + 2 * fb + half, bank[2 * (fb % 2) + half])

        def sample_down(fb):
            dve.wait_ge(s_ss, N_DOWN + 3 * fb + 3)
            sample_rows(fb, fb * CHUNK, bank[4 + fb % 2], gmod2, x2s)

        c = 0
        for fb in range(DM // CHUNK):
            for n, kd in enumerate(KD):
                for half in range(2):
                    split_lo(F_DOWN + 2 * c + half, 2 * (c % 2) + half, kd)
                    if n == 0 and fb:
                        evict_down(fb - 1, half)
                c += 1
                if n == 0 and fb:
                    sample_down(fb - 1)
        for half in range(2):
            evict_down(DM // CHUNK - 1, half)
        sample_down(DM // CHUNK - 1)
        dve.drain().then_inc(s_x3, 1)
        dve.wait_ge(s_fw, 16)
        for i in range(TT + 1):
            n = P if i < TT else S
            dve.wait_ge(s_ysq, i + 1)
            if i < TT:
                then(tt(st2[0:n, 2:3], st[0:n, 0:1], st[0:n, 1:2], ALU.add))
                then(ts(st2[0:n, 0:1], st2[0:n, 2:3], 1.0 / DM, EPS, ALU.mult, ALU.add))
            else:
                then(ts(st2[0:n, 0:1], st[0:n, 0:1], 1.0 / DM, EPS, ALU.mult, ALU.add))
            dve.reciprocal(st2[0:n, 0:1], st2[0:n, 0:1]).then_inc(s_yi, 1)
            dve.wait_ge(s_yr, i + 1)
            for e in range(2):
                c = slice(512 * e, 512 * e + 512)
                if i < TT:
                    dve.scalar_tensor_tensor(ytok[i % 2][:, c], bank[2 * (i % 2) + e][:, :], st2[:, 1:2], fw[:, c], ALU.mult, ALU.mult)
                else:
                    dve.scalar_tensor_tensor(x2s[:, c], x2s[:, c], st2[0:S, 1:2], fw[0:S, c], ALU.mult, ALU.mult)
            dve.drain().then_inc(s_y, 1)

    persist.close()


_INS = ['x_prompt', 'x_sample', 'cache_k', 'cache_v', 'state_ret', 'page_table', 'c_prompt', 'c_sample',
        'norm1_w', 'norm2_w', 'final_w', 'w_mod', 'b_mod', 'w_in', 'ret_gn_w', 'moba_norm_w', 'w_out',
        'w_gate', 'w_up', 'w_down']
_OUTS = [(1, T, DM), (NB_SEQ, TS, DM), (1, 1, T, H, HD), (1, 1, T, H, HD), (1, 1, H, HD, HD),
         (1, NB_SEQ, TS, H, HD), (1, NB_SEQ, TS, H, HD), (1, NB_SEQ, H, HD, HD)]


def kernel(**inputs):
    import concourse.bacc as bacc
    from concourse.bass_utils import run_bass_kernel_spmd

    nc = bacc.Bacc("TRN2", target_bir_lowering=False, num_devices=1)
    const, where = constants()
    arrays, args = {}, []
    for name, a in [(n, inputs[n]) for n in _INS] + [("const", const)]:
        a = np.ascontiguousarray(a)
        arrays[f"in_{name}"] = a
        args.append(nc.dram_tensor(f"in_{name}", a.shape, mybir.dt.from_np(a.dtype), kind="ExternalInput").ap())
    args.append(where)
    for i, shape in enumerate(_OUTS):
        args.append(nc.dram_tensor(f"out_{i}", shape, F32, kind="ExternalOutput").ap())
    decoder_step(nc, *args)
    r = run_bass_kernel_spmd(nc, [arrays], core_ids=[0])
    return tuple(r.results[0][f"out_{i}"] for i in range(len(_OUTS)))
```

```python
from contextlib import ExitStack

import numpy as np
import concourse.bass as bass
from concourse import mybir

F32, F32R, I32 = mybir.dt.float32, mybir.dt.float32r, mybir.dt.int32
ALU, ACT, AX = mybir.AluOpType, mybir.ActivationFunctionType, mybir.AxisListType

P = 128
DM = 1024
T = 512
NB_SEQ, TS = 8, 4
S = NB_SEQ * TS
HD = 64
H = 8
HP = H // 2
W = H * HD
PAST, PAGE, BLOCK, TOPK = 4096, 128, 256, 3
NPAGE = PAST // PAGE
NBLK = PAST // BLOCK
GRP = 4
NGRP = NPAGE // GRP
ROWS = PAGE // 32
DFF = 2816
KT = DM // P
FT = DFF // P
TT = T // P
EPS = 1e-6
BIG = 1e30
SCALE = HD ** -0.5
NSEQ = NB_SEQ + 1
CHUNK = 256
NIN = (4 * W + 3 * W) // CHUNK
NMOD = 6 * DM // CHUNK
RQ, RK, RV, RG, MQ, MK, MV = (W // P * i for i in range(7))
V_BMOD, V_N1, V_N2, V_GN, V_MN = 0, 48, 56, 64, 68
NVEC = 72


def constants():
    f = np.float32
    log_g = np.log1p(-np.exp2(-5.0 - np.arange(H))).astype(np.float64)
    p = np.arange(P)
    out, where = [], {}

    def put(name, a):
        a = np.asarray(a, f)
        full = np.zeros((P, int(np.prod(a.shape[1:]))), f)
        full[: a.shape[0]] = a.reshape(a.shape[0], -1)
        at = sum(x.shape[1] for x in out)
        where[name] = (at, a.shape)
        out.append(full)

    put("ident", np.eye(P))
    put("ones", np.ones((P, P)))
    inv = (f(10000.0) ** (-np.arange(32, dtype=f) / f(32))).astype(f)
    ang = (np.arange(T, dtype=f)[None, :] * inv[p % 32][:, None]).astype(f)
    put("cos", np.cos(ang))
    put("sin", np.sin(ang))
    rot = np.zeros((P, P))
    for m in range(P):
        if m % 64 < 32:
            rot[m + 32, m] = -1.0
        else:
            rot[m - 32, m] = 1.0
    put("rot", rot)
    angs = ((PAST + np.arange(S) % TS).astype(f)[:, None] * inv[None, :]).astype(f)
    put("cos_s", np.cos(angs))
    put("sin_s", np.sin(angs))
    i = np.arange(P)
    diff = i[None, :] - i[:, None]
    d = [np.where(diff >= 0, np.exp(np.maximum(diff, 0) * g) * SCALE, 0.0) for g in log_g]
    put("decay", np.stack(d, 1))
    s = np.arange(S)
    diff = s[None, :] - s[:, None]
    ok = (s[None, :] // TS == s[:, None] // TS) & (diff >= 0)
    put("decay_s", np.stack([np.where(ok, np.exp(np.maximum(diff, 0) * g) * SCALE, 0.0) for g in log_g], 1))
    hp_of = lambda hp: 2 * hp + p // 64
    put("q_dec", np.stack([np.exp((i[None, :] + 1) * log_g[hp_of(hp)][:, None]) for hp in range(HP)], 1))
    put("q_dec_s", np.stack([np.exp((s[None, :] % TS + 1) * log_g[hp_of(hp)][:, None]) for hp in range(HP)], 1))
    put("k_dec", np.exp((P - 1 - i)[:, None] * log_g[None, :]) * SCALE)
    kb = np.exp((TS - 1 - s % TS)[:, None] * log_g[None, :]) * SCALE
    put("k_dec_s", np.where((s // TS)[:, None, None] == np.arange(NB_SEQ)[None, :, None], kb[:, None, :], 0.0))
    put("c_dec", np.stack([np.exp(P * log_g[hp_of(hp)]) for hp in range(HP)], 1))
    put("c_dec_s", np.stack([np.exp(TS * log_g[hp_of(hp)]) for hp in range(HP)], 1))
    put("causal", np.where(i[None, :] <= i[:, None], 0.0, -BIG))
    h, g, t = p // 16, p // 4 % 4, p % 4
    same = (h[:, None] == h[None, :]) & (t[:, None] == t[None, :])
    put("pair0", same & (g[:, None] < 2))
    put("pair1", same & (g[:, None] >= 2))
    put("own_pair", same & (g[:, None] // 2 == g[None, :] // 2))
    n_own = 2 * np.arange(NGRP)[None, :] + (g // 2)[:, None]
    put("earlier", np.arange(NBLK)[None, None, :] < n_own[:, :, None])
    ht = np.arange(32)
    put("sum_g", (h * 4 + t)[:, None] == ht[None, :])
    put("sum_pv", (p % 32)[:, None] == ht[None, :])
    tok = np.arange(S)
    seq = np.arange(NB_SEQ)
    ok = (g == 0)[:, None, None] & (tok[None, None, :] // TS == seq[None, :, None]) & (tok % TS <= t[:, None])[:, None, :]
    put("own_mask", np.where(ok, 0.0, -BIG))
    put("head_diag", (p % 32 // 4)[:, None] == np.arange(H)[None, :])
    put("row32", (p % 32)[:, None])
    put("row128", p[:, None])
    return np.ascontiguousarray(np.concatenate(out, 1)), where


def decoder_step(nc, x_prompt, x_sample, cache_k, cache_v, state_ret, page_table, c_prompt, c_sample,
                 norm1_w, norm2_w, final_w, w_mod, b_mod, w_in, ret_gn_w, moba_norm_w, w_out,
                 w_gate, w_up, w_down, const, where,
                 y_prompt, y_sample, k_prompt, v_prompt, ret_prompt, k_sample, v_sample, ret_sample):
    NC = const.shape[1]
    persist, mid = ExitStack(), ExitStack()

    def sem(name):
        return persist.enter_context(nc.semaphore(name))

    def allocator(stack):
        return lambda name, shape, dt=F32: stack.enter_context(nc.sbuf_tensor(name, shape, dt))

    sb = allocator(persist)
    ct = sb("ct", [P, NC])

    def C(name):
        at, shape = where[name]
        n = int(np.prod(shape[1:]))
        v = ct[:shape[0], at:at + n]
        return v.rearrange("p (a b) -> p a b", a=shape[1]) if len(shape) == 3 else v

    ident, ones = C("ident"), C("ones")
    asT = sb("asT", [P, KT, S])
    vT = sb("vT", [P, NVEC])
    mT = sb("mT", [P, 48, NSEQ])
    gain = sb("gain", [P, KT, NSEQ])
    xs = sb("xs", [S, DM])
    stage = [sb(f"stage{i}", [P, T]) for i in range(2)]
    st = sb("st", [P, 64])
    st2 = sb("st2", [P, 64])
    kidx = sb("kidx", [P, NB_SEQ * NGRP], I32)
    kix = [sb(f"kix{i}", [P, 1], I32) for i in range(4)]
    pt = sb("pt", [P, NB_SEQ * NPAGE], I32)
    asm = sb("asm", [P, 256])
    xtmp = sb("xtmp", [S, CHUNK])

    dense = ExitStack()
    tmp = allocator(dense)
    raw = [tmp(f"raw{i}", [P, KT, CHUNK]) for i in range(2)]
    whi = [tmp(f"whi{i}", [P, KT, P], F32R) for i in range(2)]
    wlo = [tmp(f"wlo{i}", [P, KT, P], F32R) for i in range(2)]
    ahi = tmp("ahi", [P, KT, T], F32R)
    alo = tmp("alo", [P, KT, T], F32R)
    dense.close()
    tmp = allocator(dense)
    qrs, krs = tmp("qrs", [S, W]), tmp("krs", [S, W])
    kmask = [tmp(f"kmask{i}", [S, W]) for i in range(2)]
    ret_s = tmp("ret_s", [S, W])
    sT = tmp("sT", [P, 3, HP, S])
    ats = tmp("ats", [S, H, S])
    dense.close()
    KTb = [sb(f"KT{i}", [P, ROWS, W // 32, 32]) for i in range(2)]
    VB = [sb(f"V{i}", [P, W]) for i in range(8)]
    Kb = [sb(f"K{i}", [P, ROWS * W]) for i in range(4)]
    sb2 = allocator(mid)
    zs = sb2("zs", [S, NIN * CHUNK])
    cT = sb2("cT", [P, KT, 32])
    sm = sb2("sm", [P, 960])
    mst = sb2("mst", [P, 2 * CHUNK])

    era1 = ExitStack()
    tmp = allocator(era1)
    zT = tmp("zT", [P, 28, T])
    era1a = ExitStack()
    tmp = allocator(era1a)
    vrow = tmp("vrow", [NVEC, P])
    crow = tmp("crow", [NSEQ, DM])
    xP = tmp("xP", [P, TT, DM])
    sq = tmp("sq", [P, DM])
    rawm = tmp("rawm", [P, KT, CHUNK])
    era1a.close()
    era1b = ExitStack()
    tmp = allocator(era1b)
    rvtok = tmp("rvtok", [P, TT, W])
    mvtok = tmp("mvtok", [P, TT, W])
    scr = tmp("scr", [P, 7, T])
    sst = tmp("sst", [P, 4, HD])
    era1b.close()
    sq_ret = Kb[2][:, :].rearrange("p (i w) -> p i w", i=TT)
    sq_moba = Kb[3][:, :].rearrange("p (i w) -> p i w", i=TT)
    rettok = zT[:, RV:RV + 4, :]
    mobatok = zT[:, MV:MV + 4, :]
    era1.close()

    era2 = ExitStack()
    tmp = allocator(era2)
    state = tmp("state", [P, NB_SEQ, HP, HD])
    era2.close()
    tmp = allocator(era2)
    lgs = tmp("lgs", [P, NGRP, P])
    pe_x = tmp("pe_x", [P, NGRP, P])
    pT = tmp("pT", [P, NGRP, P])
    qbb = tmp("qbb", [P, W // 32, S])
    kbb = tmp("kbb", [P, W // 32, S])
    era2.close()
    tmp = allocator(era2)
    below_values = tmp("below_values", [P, 28, T])
    qbd = [tmp(f"qbd{i}", [P, W // 32, 32]) for i in range(2)]
    od = tmp("od", [P, H, HD])
    oall = tmp("oall", [32, NB_SEQ, HD])
    era2.close()
    mid.close()

    era3 = ExitStack()
    tmp = allocator(era3)
    x2T = tmp("x2T", [P, KT, T])
    aT = tmp("aT", [P, FT, S])
    x2s = tmp("x2s", [S, DM])
    era3a = ExitStack()
    tmp = allocator(era3a)
    xP2 = tmp("xP2", [P, TT, DM])
    gmod = tmp("gmod", [S, DM])
    rb = tmp("rb", [P, T])
    xsn2 = tmp("xsn2", [S, DM])
    era3a.close()
    era3b = ExitStack()
    tmp = allocator(era3b)
    fhi = tmp("fhi", [P, FT, T], F32R)
    flo = tmp("flo", [P, FT, T], F32R)
    era3b.close()
    era4 = ExitStack()
    tmp = allocator(era4)
    fw = tmp("fw", [P, DM])
    ytok = [tmp(f"ytok{i}", [P, DM]) for i in range(2)]
    gmod2 = xs
    era4.close()
    era3.close()

    bank = [persist.enter_context(nc.psum_tensor(f"bank{i}", [P, 512], F32)) for i in range(8)]

    s_ident = sem("ident_loaded")
    s_const, s_x, s_xs, s_c = sem("const_loaded"), sem("x_loaded"), sem("xs_loaded"), sem("c_loaded")
    s_vec, s_pt, s_state = sem("vec_loaded"), sem("pt_loaded"), sem("state_loaded")
    s_w = [sem(f"w_loaded{i}") for i in range(2)]
    s_x2l, s_fw = sem("x_reloaded"), sem("final_w_loaded")
    s_out = sem("out_stored")
    s_ytok = [sem(f"y_tile_stored{i}") for i in range(2)]
    s_hi, s_lo, s_ft, s_ev = sem("w_hi"), sem("w_lo"), sem("tile_done+2"), sem("tile_evicted+2")
    s_ss, s_sev = sem("sample_done"), sem("sample_evicted+2")
    s_md, s_mt, s_wm = sem("mod_chunk_done"), sem("gain_ready"), sem("mod_w_loaded")
    s_mev, s_mtp, s_mp = sem("mod_copied+2"), sem("mod_turned+1"), sem("mod_pair_kept+1")
    s_silu, s_ctp, s_ct, s_vtp = sem("c_silu"), sem("c_turned"), sem("cT_ready"), sem("vec_turned")
    s_sqd, s_rin, s_xn, s_xsn = sem("squares"), sem("rms_inverse"), sem("x_normed"), sem("xs_normed")
    s_xt, s_stg, s_hhi, s_hlo = sem("act_turned"), sem("act_staged"), sem("act_hi"), sem("act_lo")
    s_xst, s_hs = sem("xs_turned"), sem("asT_ready")
    s_vt1, s_vt2 = sem("values_turned"), sem("values_copied")
    s_qk, s_sc, s_nm, s_p = sem("moba_qk"), sem("moba_scores"), sem("moba_negmax"), sem("moba_probs+1")
    s_ptp, s_pte, s_pv, s_on = sem("moba_turned+1"), sem("moba_probsT+1"), sem("moba_out+1"), sem("moba_normed+1")
    s_rr, s_rk, s_kt1, s_kt2 = sem("ret_rotated"), sem("ret_k"), sem("ret_kT"), sem("ret_ktok")
    s_ra, s_rad, s_kv, s_st = sem("ret_scores"), sem("ret_decayed"), sem("ret_kv"), sem("ret_state")
    s_ro, s_roc = sem("ret_out+1"), sem("ret_copied+1")
    s_rs, s_hsq, s_hri, s_hrs = sem("ret_state_stored+16"), sem("head_squares"), sem("head_inverse"), sem("head_rstd")
    s_hn, s_sg = sem("heads_normed"), sem("gate_silu")
    s_kst, s_vst, s_sst = sem("k_prompt_stored"), sem("v_prompt_stored"), sem("ret_sample_stored")
    s_srot, s_sqt, s_sqe, s_sa = sem("s_rotated"), sem("s_qk_turned"), sem("s_qkT"), sem("s_scores")
    s_sad, s_so, s_soc, s_sot = sem("s_decayed"), sem("s_out"), sem("s_out_copied"), sem("s_out_turned")
    s_ssq, s_srs, s_srn, s_srt = sem("s_squares"), sem("s_rstd"), sem("s_normed"), sem("s_norm_turned")
    s_sas, s_ssg = sem("s_ret_mixed"), sem("s_gate_silu")
    s_sdc = sem("s_state_decayed")
    s_km, s_kvs, s_sts = sem("s_kmask"), sem("s_kv"), sem("s_state_new")
    s_idx, s_qd, s_ask = sem("page_rows"), sem("qbd_ready"), sem("k_asked")
    s_k = [sem(f"k_loaded{i}") for i in range(4)]
    s_v = [sem(f"v_loaded{i}") for i in range(8)]
    s_kt, s_lg, s_own, s_s1 = sem("k_turned"), sem("logits+2"), sem("own_logits"), sem("block_sums")
    s_gt, s_mx, s_mxt, s_rm = sem("gates"), sem("part_max"), sem("part_max_turned"), sem("row_max")
    s_mb, s_nb, s_ex, s_tp = sem("max_spread"), sem("exp_bias"), sem("exps"), sem("probs_turned")
    s_te, s_rsm, s_den, s_vd = sem("probsT_copied"), sem("part_den"), sem("denominators"), sem("page_used")
    s_od, s_of, s_oe = sem("out_masked"), sem("out_folded"), sem("out_kept")
    s_ofs, s_ofr, s_ofq, s_oft = sem("o_squares"), sem("o_inverse"), sem("o_rstd"), sem("o_turned")
    s_oas = sem("o_mixed")
    s_tt, s_oa, s_rcp = sem("own_probs_turned"), sem("out_row_kept"), sem("denominators_inverse")
    s_le, s_to = sem("logits_kept+2"), sem("own_probsT_copied")
    s_sqx, s_ssm, s_r1, s_r2 = sem("x2_squares"), sem("x2_sums"), sem("x2_inverse"), sem("x2_rstd")
    s_nx, s_gmt = sem("x2_scaled"), sem("gmod_turned")
    s_xr, s_x2s, s_x2q, s_x2i = sem("x2T_ready"), sem("x2s_ready"), sem("x2s_squares"), sem("x2s_inverse")
    s_x2n = sem("x2s_normed")
    s_fh, s_fl = sem("ff_hi"), sem("ff_lo+1")
    s_spr = sem("s_ffn_product")
    s_ssl, s_smt, s_sme = sem("s_ffn_silu"), sem("s_ffn_turned"), sem("s_ffn_aT")
    s_x3, s_yt, s_ysq, s_yi = sem("x3_ready"), sem("y_turned"), sem("y_squares"), sem("y_inverse")
    s_yr, s_y = sem("y_rstd"), sem("y_ready")

    kview = lambda w: w[0].rearrange("(k p) f -> p k f", p=P)
    w_mod_v, w_in_v, w_out_v = kview(w_mod), kview(w_in), kview(w_out)
    w_gate_v, w_up_v, w_down_v = kview(w_gate), kview(w_up), kview(w_down)

    NMA = 2 * DM // CHUNK
    KD = (8, 8, 6)
    B_IN = NMA // 2
    B_MODB = B_IN + NIN // 2
    B_OUT = B_MODB + 1
    B_FFN = B_OUT + 2
    F_OUT, N_OUT = 2 * NIN, NIN
    F_FFN, N_FFN = F_OUT + 8, N_OUT + 4
    F_DOWN, N_DOWN = F_FFN + 2 * FT, N_FFN + FT
    N_STORES = [0]

    turned = lambda x: x.rearrange("p (h g t) -> p g h t", g=GRP, t=TS)
    by_page = lambda x: x.rearrange("p (g h t) -> p g h t", g=GRP, t=TS)

    def moba_steps(eng, step):
        step(0, 0, tail=False, rest=False)
        step(1, 1, rest=False)
        with eng.Fori(1, NB_SEQ // 2 - 1) as i:
            step(2 * i, 0)
            step(2 * i + 1, 1)
        step(NB_SEQ - 2, 0)
        step(NB_SEQ - 1, 1)
        step(NB_SEQ, 0, head=False)

    cv = cache_v[0].rearrange("n p h d -> n p (h d)")
    V_SHARED = (NB_SEQ * NPAGE - 48) // 8

    block = persist.enter_context(nc.Block())

    @block.sync
    def _(sp):
        def store(dst, src):
            sp.dma_start(dst, src).then_inc(s_out, 16)
            N_STORES[0] += 1

        def chunk(u, view, at):
            sp.dma_start(raw[u][:, :, :], view[:, :, at]).then_inc(s_w[u], 16)

        sp.sem_inc(s_rs, 16)
        sp.dma_start(crow[0:NB_SEQ, :], c_sample).then_inc(s_c, 16)
        sp.dma_start(crow[NB_SEQ:NSEQ, :], c_prompt).then_inc(s_c, 16)
        sp.dma_start(ct[:, 0:P], const[:, 0:P]).then_inc(s_ident, 16)
        for u in range(2):
            chunk(u, w_mod_v, slice(u * CHUNK, (u + 1) * CHUNK))
        sp.dma_start(vrow[V_BMOD:V_N1, :], b_mod[0].rearrange("(r c) -> r c", c=P)).then_inc(s_vec, 16)
        for at, v in ((V_N1, norm1_w), (V_N2, norm2_w), (V_GN, ret_gn_w), (V_MN, moba_norm_w)):
            n = v.shape[1] // P
            sp.dma_start(vrow[at:at + n, :], v[0].rearrange("(r c) -> r c", c=P)).then_inc(s_vec, 16)
        sp.dma_start(xP[:, :, :], x_prompt[0].rearrange("(i p) d -> p i d", p=P)).then_inc(s_x, 16)
        sp.dma_start(xs[:, :], x_sample.rearrange("b t d -> (b t) d")).then_inc(s_xs, 16)
        sp.dma_start(pt[:, :], page_table.rearrange("b n -> (b n)").partition_broadcast(P)).then_inc(s_pt, 16)
        with sp.Fori(1, NMA // 2) as i:
            for u in range(2):
                sp.wait_ge(s_md, 2 * i + u - 1)
                chunk(u, w_mod_v, bass.ds((2 * i + u) * CHUNK, CHUNK))
        for u in range(2):
            sp.wait_ge(s_md, NMA - 1 + u)
            chunk(u, w_in_v, slice(u * CHUNK, (u + 1) * CHUNK))
        def mod_beside(n):
            sp.dma_start(rawm[:, :, :], w_mod_v[:, :, bass.ds((NMA + n) * CHUNK, CHUNK)]).then_inc(s_wm, 16)

        mod_beside(0)
        sp.dma_start(ct[:, P:], const[:, P:]).then_inc(s_const, 16)
        with sp.Fori(1, NIN // 2) as i:
            for u in range(2):
                sp.wait_ge(s_ss, 2 * i + u - 1)
                chunk(u, w_in_v, bass.ds((2 * i + u) * CHUNK, CHUNK))
                sp.wait_ge(s_md, NMA + 2 * i + u - 1)
                mod_beside(2 * i + u - 1)
        sp.wait_ge(s_md, NMA + NIN - 1)
        mod_beside(NIN - 1)
        for u in range(2):
            sp.wait_ge(s_ss, NIN - 1 + u)
            chunk(u, w_mod_v, slice((NMA + NIN + u) * CHUNK, (NMA + NIN + u + 1) * CHUNK))
        sp.wait_ge(s_vt2, 4)
        sp.dma_start(k_prompt[0, 0].rearrange("(i p) h d -> p i (h d)", p=P), scr[:, 3:7, :]).then_inc(s_kst, 16)
        sp.wait_ge(s_vt2, 8)
        sp.dma_start(v_prompt[0, 0].rearrange("(i p) h d -> p i (h d)", p=P), mvtok[:, :, :]).then_inc(s_vst, 16)
        sp.wait_ge(s_sev, NIN + 2)
        store(k_sample[0].rearrange("b t h d -> (b t) (h d)"), zs[:, 5 * W:6 * W])
        store(v_sample[0].rearrange("b t h d -> (b t) (h d)"), zs[:, 6 * W:7 * W])
        sp.wait_ge(s_ss, NIN)
        for s in range(8):
            r = sp.value_load(pt[0:1, s:s + 1], min_val=0, max_val=cv.shape[0] - 1)
            sp.dma_start(VB[s][:, :], cv[bass.ds(r, 1), :, :].rearrange("a p c -> (a p) c")).then_inc(s_v[s], 16)
        with sp.Fori(0, HP) as hp:
            sp.wait_ge(s_st, hp + 1)
            sp.dma_start(ret_prompt[0, 0].rearrange("h d v -> (h d) v")[bass.ds(hp * P, P), :], sst[:, 3, :]).then_inc(s_rs, 16)
        sp.wait_ge(s_rk, 2 * HP)
        sp.dma_start(state[:, :, :, :], state_ret[0].rearrange("b (hp h2) d v -> (h2 d) b hp v", h2=2)).then_inc(s_state, 16)
        sp.wait_ge(s_sts, NB_SEQ)
        sp.dma_start(ret_sample[0].rearrange("b (hp h2) d v -> (h2 d) b hp v", h2=2), state[:, :, :, :]).then_inc(s_sst, 16)
        with sp.Fori(1, V_SHARED) as i:
            for s in range(8):
                r = sp.value_load(pt[0:1, bass.ds(i * 8 + s, 1)], min_val=0, max_val=cv.shape[0] - 1)
                sp.wait_ge(s_vd, i * 8 + s - 7)
                sp.dma_start(VB[s][:, :], cv[bass.ds(r, 1), :, :].rearrange("a p c -> (a p) c")).then_inc(s_v[s], 16)
        with sp.Fori(V_SHARED, NB_SEQ * NPAGE // 8) as i:
            for s in range(0, 8, 2):
                r = sp.value_load(pt[0:1, bass.ds(i * 8 + s, 1)], min_val=0, max_val=cv.shape[0] - 1)
                sp.wait_ge(s_vd, i * 8 + s - 7)
                sp.dma_start(VB[s][:, :], cv[bass.ds(r, 1), :, :].rearrange("a p c -> (a p) c")).then_inc(s_v[s], 16)
        for u in range(2):
            sp.wait_ge(s_lg, NGRP * NB_SEQ + 2)
            sp.wait_ge(s_md, NMOD - 1 + u)
            chunk(u, w_out_v, slice(u * CHUNK, (u + 1) * CHUNK))
        sp.wait_ge(s_vst, 16)
        sp.wait_ge(s_hlo, 2 * KT)
        sp.wait_ge(s_vd, NB_SEQ * NPAGE)
        sp.dma_start(xP2[:, :, :], x_prompt[0].rearrange("(i p) d -> p i d", p=P)).then_inc(s_x2l, 16)
        for u in range(2):
            sp.wait_ge(s_ss, N_OUT + u + 1)
            chunk(u, w_out_v, slice((2 + u) * CHUNK, (3 + u) * CHUNK))

        def ffn_chunk(u, at):
            sp.dma_start(raw[u][:, :, 0:P], w_gate_v[:, :, at]).then_inc(s_w[u], 16)
            sp.dma_start(raw[u][:, :, P:2 * P], w_up_v[:, :, at]).then_inc(s_w[u], 16)

        for u in range(2):
            sp.wait_ge(s_ss, N_OUT + 2 + u + 1)
            ffn_chunk(u, slice(u * P, (u + 1) * P))
        with sp.Fori(1, FT // 2) as i:
            for u in range(2):
                sp.wait_ge(s_ss, N_FFN + 2 * i + u - 1)
                ffn_chunk(u, bass.ds((2 * i + u) * P, P))
        c = 0
        for fb in range(DM // CHUNK):
            for n, kd in enumerate(KD):
                sp.wait_ge(s_ss, N_DOWN + c - 1)
                sp.dma_start(raw[c % 2][:, 0:kd, :], w_down_v[:, 8 * n:8 * n + kd, fb * CHUNK:(fb + 1) * CHUNK]).then_inc(s_w[c % 2], 16)
                c += 1
        sp.wait_ge(s_ft, F_DOWN + 24 + 2)
        sp.dma_start(fw[:, :], final_w.partition_broadcast(P)).then_inc(s_fw, 16)
        for i in range(TT):
            sp.wait_ge(s_y, i + 1)
            sp.dma_start(y_prompt[0, i * P:(i + 1) * P, :], ytok[i % 2][:, :]).then_inc(s_ytok[i % 2], 16)
        sp.wait_ge(s_y, TT + 1)
        store(y_sample.rearrange("b t d -> (b t) d"), x2s[:, :])
        for i in range(2):
            sp.wait_ge(s_ytok[i], 16 * TT // 2)
        sp.wait_ge(s_out, 16 * N_STORES[0])

    @block.gpsimd
    def _(pool):
        pool.wait_ge(s_sev, NIN + 2)
        pool.wait_ge(s_md, NMOD)
        pool.wait_ge(s_const, 16)
        cos = C("cos_s").unsqueeze(1).broadcast_to((S, H, 32))
        sin = C("sin_s").unsqueeze(1).broadcast_to((S, H, 32))
        ta = kmask[0][:, 0:256].rearrange("p (h d) -> p h d", h=H)
        tb = kmask[1][:, 0:256].rearrange("p (h d) -> p h d", h=H)
        for n, dst in enumerate((qrs, krs)):
            z = zs[:, n * W:(n + 1) * W].rearrange("p (h c d) -> p h c d", h=H, c=2)
            o = dst[:, :].rearrange("p (h c d) -> p h c d", h=H, c=2)
            for half, op in enumerate((ALU.subtract, ALU.add)):
                pool.tensor_tensor(ta, z[:, :, half, :], cos, ALU.mult)
                pool.tensor_tensor(tb, z[:, :, 1 - half, :], sin, ALU.mult)
                pool.drain()
                pool.tensor_tensor(o[:, :, half, :], ta, tb, op)
                pool.drain()
        pool.sem_inc(s_srot, 1)

        def masked_k(b):
            if b >= 2:
                pool.wait_ge(s_kvs, b - 1)
            pool.tensor_tensor(kmask[b % 2][:, :].rearrange("p (h d) -> p h d", h=H), krs[:, :].rearrange("p (h d) -> p h d", h=H),
                               C("k_dec_s")[:, b, :].unsqueeze(2).broadcast_to((S, H, HD)), ALU.mult).then_inc(s_km, 1)

        pool.wait_ge(s_idx, 1)
        pool.wait_ge(s_ss, NIN)
        ck = cache_k[0].rearrange("n (a r) h d -> (n a) (r h d)", r=ROWS)
        for u in range(4):
            pool.indirect_dma_start(Kb[u][:, :], None, ck, bass.IndirectOffsetOnAxis(kidx[:, u:u + 1], 0)).then_inc(s_k[u], 16)
        masked_k(0)
        masked_k(1)
        pool.wait_ge(s_so, 1)
        pool.tensor_tensor(state[:, :, :, :], state[:, :, :, :],
                           C("c_dec_s").unsqueeze(1).unsqueeze(3).broadcast_to((P, NB_SEQ, HP, HD)), ALU.mult).then_inc(s_sdc, 1)
        for b in range(2, NB_SEQ):
            masked_k(b)
        with pool.Fori(1, NB_SEQ * NGRP // 4) as i:
            for u in range(4):
                pool.wait_ge(s_kt, 4 * i + u - 3)
                pool.sem_inc(s_ask, 1)
                pool.indirect_dma_start(Kb[u][:, :], None, ck, bass.IndirectOffsetOnAxis(kix[u][:, :], 0)).then_inc(s_k[u], 16)
        pool.wait_ge(s_kt, NB_SEQ * NGRP)
        with pool.Fori(V_SHARED, NB_SEQ * NPAGE // 8) as i:
            for s in range(1, 8, 2):
                r = pool.value_load(pt[0:1, bass.ds(i * 8 + s, 1)], min_val=0, max_val=cv.shape[0] - 1)
                pool.wait_ge(s_vd, i * 8 + s - 7)
                pool.dma_start(VB[s][:, :], cv[bass.ds(r, 1), :, :].rearrange("a p c -> (a p) c")).then_inc(s_k[s // 2], 16)

    @block.scalar
    def _(act):
        for s in (s_p, s_pte):
            act.sem_inc(s, 1)
        act.sem_inc(s_le, 2)
        act.sem_inc(s_roc, 1)
        act.wait_ge(s_c, 32)
        act.activation(crow[:, :], crow[:, :], ACT.Silu).then_inc(s_silu, 1)

        act.wait_ge(s_x, 16)
        for i in range(TT):
            act.activation(sq[:, :], xP[:, i, :], ACT.Square, accum_out=st[:, i:i + 1])
            act.drain()
        act.wait_ge(s_xs, 16)
        act.activation(sq[0:S, :], xs[:, :], ACT.Square, accum_out=st[0:S, 4:5]).then_inc(s_sqd, 1)
        act.wait_ge(s_rin, 1)
        act.activation(st2[:, 0:4], st2[:, 8:12], ACT.Sqrt)
        act.activation(st2[0:S, 4:5], st2[0:S, 12:13], ACT.Sqrt)
        act.drain()
        for i in range(TT):
            last = act.activation(xP[:, i, :], xP[:, i, :], ACT.Copy, scale=st2[:, i:i + 1])
        last.then_inc(s_xn, 1)
        act.activation(sq[0:S, :], xs[:, :], ACT.Copy, scale=st2[0:S, 4:5]).then_inc(s_xsn, 1)
        act.wait_ge(s_mt, 1)

        def stage_hi(k, n):
            act.wait_ge(s_stg, n + 1)
            act.activation(ahi[:, k, :], stage[k % 2][:, :], ACT.Copy).then_inc(s_hhi, 1)

        def split_hi(m, q, kd=KT):
            act.wait_ge(s_ft, m + 1)
            act.activation(whi[q % 2][:, 0:kd, :], raw[q // 2][:, 0:kd, q % 2 * P:(q % 2 + 1) * P], ACT.Copy).then_inc(s_hi, 1)

        act.wait_ge(s_w[0], 16 * (B_IN + 1))
        split_hi(0, 0)
        for k in range(KT):
            act.wait_ge(s_xt, k + 1)
            if k >= 2:
                act.wait_ge(s_hlo, k - 1)
            act.activation(stage[k % 2][:, :], bank[2 + k % 2][:, :], ACT.Identity,
                           scale=gain[:, k, NB_SEQ:NSEQ], bias=mT[:, k, NB_SEQ:NSEQ]).then_inc(s_stg, 1)
            stage_hi(k, k)

        def stage_pairs(F, B, pairs, loads, evict, peel=False, split_next=None):
            def body(i, last):
                for q in range(4):
                    if not (last and q == 3):
                        n = (q + 1) % 4
                        if n % 2 == 0:
                            act.wait_ge(s_w[n // 2], loads(i + (n == 0)))
                        split_hi(F + 4 * i + q + 1, n)
                    elif split_next:
                        split_next()
                    if evict:
                        evict(i, q)

            if peel:
                body(0, False)
            with act.Fori(int(peel), pairs - 1) as i:
                body(i, False)
            body(pairs - 1, True)

        def evict_z(i, q):
            act.wait_ge(s_ft, 4 * i + q + 3)
            act.activation(zT[:, bass.ds(4 * i + q, 1), :].rearrange("p a t -> p (a t)"), bank[q % 2][:, :], ACT.Copy).then_inc(s_ev, 1)

        stage_pairs(0, B_IN, NIN // 2, lambda i: 16 * (B_IN + i + 1), evict_z)

        act.wait_ge(s_sev, NIN + 2)
        act.activation(zs[:, 3 * W:4 * W], zs[:, 3 * W:4 * W], ACT.Silu).then_inc(s_ssg, 1)
        n = 0
        for dst in (scr[:, 3:7, :], mvtok, rvtok):
            for j in range(4):
                act.wait_ge(s_vt1, n + 1)
                act.activation(dst[:, :, j * P:(j + 1) * P], bank[4 + n % 2][:, :].rearrange("p (i f) -> p i f", i=TT),
                               ACT.Copy).then_inc(s_vt2, 1)
                n += 1
        with act.Fori(0, HP) as hp:
            act.wait_ge(s_ro, hp + 2)
            for h2 in range(2):
                act.activation(rettok[:, :, bass.ds(hp * P + h2 * HD, HD)],
                               bank[6 + h2][:, 0:4 * HD].rearrange("p (c v) -> p c v", c=4), ACT.Copy).then_inc(s_roc, 1)
        act.wait_ge(s_ssq, 1)
        act.activation(st2[0:S, 0:H], st2[0:S, 8:8 + H], ACT.Sqrt).then_inc(s_srs, 1)

        def copy_qk(hp):
            act.activation(scr[:, 3, :], zT[:, bass.ds(MK + hp, 1), :].rearrange("p a t -> p (a t)"), ACT.Copy)
            act.activation(scr[:, 0, :], zT[:, bass.ds(MQ + hp, 1), :].rearrange("p a t -> p (a t)"), ACT.Copy).then_inc(s_qk, 1)

        def probs(b, u):
            n = (u + 1) * P
            act.wait_ge(s_nm, 4 * b + u + 1)
            act.wait_ge(s_ptp, 4 * b + u + 1)
            act.activation(scr[:, 1, 0:n], bank[5][:, 0:n], ACT.Exp, scale=SCALE,
                           bias=st2[:, 20 + u % 2:21 + u % 2], accum_out=st[:, 16 + u:17 + u]).then_inc(s_p, 1)

        def probs_t(b, u):
            n = (u + 1) * P
            act.wait_ge(s_ptp, 4 * b + u + 2)
            act.wait_ge(s_pv, 4 * b + u + 1)
            act.activation(scr[:, 2, 0:n], bank[6][:, 0:n], ACT.Copy).then_inc(s_pte, 1)

        def keep_logits(b, e):
            act.wait_ge(s_lg, NGRP * b + 4 * e + 6)
            act.activation(lgs[:, 4 * e:4 * e + 4, :], bank[e][:, :].rearrange("p (g c) -> p g c", g=4), ACT.Copy).then_inc(s_le, 1)

        def exps(b):
            act.wait_ge(s_nb, b + 1)
            for g in range(NGRP):
                last = act.activation(pe_x[:, g, :].rearrange("p (a r) -> p r a", r=ROWS), lgs[:, g, :].rearrange("p (r a) -> p r a", r=ROWS),
                                      ACT.Exp, scale=SCALE, bias=sm[:, 320 + g:321 + g], accum_out=sm[:, 640 + g:641 + g])
                if g == 3:
                    last.then_inc(s_ex, 1)
            act.activation(sm[:, 576:608], sm[:, 512:544], ACT.Exp, scale=SCALE, bias=sm[:, 328:329],
                           accum_out=sm[:, 648:649]).then_inc(s_ex, 1)

        def keep_probs(b, e):
            act.wait_ge(s_tp, 2 * b + e + 1)
            for n in range(4):
                last = act.activation(by_page(pT[:, 4 * e + n, :]), turned(bank[2][:, n * P:(n + 1) * P]), ACT.Copy)
            last.then_inc(s_te, 1)

        def step(b, par, head=True, tail=True, rest=True):
            for slot in range(8):
                if head:
                    (probs if slot % 2 == 0 else probs_t)(b, slot // 2)
                if tail and slot == 2:
                    exps(b - 1)
                if tail and slot in (3, 4):
                    keep_probs(b - 1, slot - 3)
                if head and slot in (3, 7):
                    if isinstance(b, int) and b == 0 and slot == 3:
                        act.wait_ge(s_sst, 16)
                    keep_logits(b, slot // 4)
            if head and par == 1:
                act.wait_ge(s_sc, 4 * b + 4)
                if isinstance(b, int) and b == NB_SEQ - 1:
                    return
                copy_qk(b // 2 + 1 if isinstance(b, int) else (b - 1) // 2 + 1)

        act.wait_ge(s_ro, HP + 1)
        copy_qk(0)
        moba_steps(act, step)
        act.wait_ge(s_hn, 1)
        act.activation(sq_ret, rettok, ACT.Square)
        act.wait_ge(s_on, 4 * H + 1)
        act.activation(sq_moba, mobatok, ACT.Square).then_inc(s_hsq, 1)
        act.activation(zT[:, RG:RG + 4, :], zT[:, RG:RG + 4, :], ACT.Silu).then_inc(s_sg, 1)
        act.wait_ge(s_hri, 1)
        act.activation(gain[:, :, 0:8].rearrange("p a b -> p a b"), gain[:, :, 0:8], ACT.Sqrt).then_inc(s_hrs, 1)
        for k in range(KT):
            stage_hi(k, KT + k)
            if k == 3:
                act.wait_ge(s_vd, NB_SEQ * NPAGE)
                act.wait_ge(s_w[0], 16 * (B_OUT + 1))
            if k in (3, 4):
                split_hi(F_OUT + k - 3, k - 3)

        act.wait_ge(s_ofs, 1)
        act.activation(st2[0:32, 0:8], st2[0:32, 8:16], ACT.Sqrt).then_inc(s_ofq, 1)

        act.wait_ge(s_oas, 1)
        for k in range(KT):
            act.wait_ge(s_xt, 2 * KT + k + 1)
            act.activation(x2T[:, k, :], bank[2 + k % 2][:, :], ACT.Copy).then_inc(s_xr, 1)
        for f in range(KT):
            if f + 2 < KT:
                if f % 2 == 0:
                    act.wait_ge(s_w[(f + 2) // 2 % 2], 16 * (B_OUT + (f + 2) // 4 + 1))
                split_hi(F_OUT + f + 2, (f + 2) % 4)
            if f == KT - 1:
                act.wait_ge(s_w[0], 16 * (B_FFN + 2))
                split_hi(F_FFN, 0)
            act.wait_ge(s_ev, F_OUT + f + 3)
            if f >= 2:
                act.wait_ge(s_ssm, f - 1)
            act.activation(stage[f % 2][:, :], x2T[:, f, :], ACT.Square).then_inc(s_sqx, 1)
        act.wait_ge(s_x2s, 1)
        act.activation(xsn2[:, :], x2s[:, :], ACT.Square, accum_out=st[0:S, 0:1]).then_inc(s_x2q, 1)
        act.wait_ge(s_x2i, 1)
        act.activation(st2[0:S, 1:2], st2[0:S, 0:1], ACT.Sqrt)
        act.drain()
        act.activation(xsn2[:, :], x2s[:, :], ACT.Copy, scale=st2[0:S, 1:2]).then_inc(s_x2n, 1)
        act.wait_ge(s_r1, 1)
        act.activation(rb[:, :], rb[:, :], ACT.Sqrt).then_inc(s_r2, 1)
        for k in range(KT):
            act.wait_ge(s_nx, k + 1)
            act.activation(stage[k % 2][:, :], stage[k % 2][:, :], ACT.Identity,
                           scale=gain[:, k, NB_SEQ:NSEQ], bias=mT[:, 24 + k, NB_SEQ:NSEQ]).then_inc(s_stg, 1)
            stage_hi(k, 2 * KT + k)

        def sample_silu(n):
            act.wait_ge(s_sev, N_FFN + n + 3)
            act.activation(xtmp[:, 0:P], xtmp[:, 0:P], ACT.Silu).then_inc(s_ssl, 1)

        def evict_ffn(i, q):
            act.wait_ge(s_ft, F_FFN + 4 * i + q + 3)
            if q % 2 == 0:
                act.wait_ge(s_fl, 2 * i + q // 2 + 1)
                act.activation(stage[0][:, :], bank[0][:, :], ACT.Silu).then_inc(s_ev, 1)
                if not (isinstance(i, int) and i + q == 0):
                    sample_silu(2 * i + q // 2 - 1)
            else:
                act.wait_ge(s_ev, F_FFN + 4 * i + q + 3)
                act.activation(fhi[:, bass.ds(2 * i + q // 2, 1), :].rearrange("p a t -> p (a t)"), stage[1][:, :], ACT.Copy).then_inc(s_fh, 1)

        def split_down(c, half, kd):
            act.wait_ge(s_w[c % 2], 16 * (B_FFN + FT + c // 2 + 1))
            split_hi(F_DOWN + 2 * c + half, 2 * (c % 2) + half, kd)

        stage_pairs(F_FFN, B_FFN, FT // 2, lambda i: 16 * (B_FFN + 2 * i + 2), evict_ffn, peel=True,
                    split_next=lambda: split_down(0, 0, KD[0]))
        c = 0
        for fb in range(DM // CHUNK):
            for n, kd in enumerate(KD):
                for half in range(2):
                    if c or half:
                        split_down(c, half, kd)
                if c == 0:
                    sample_silu(FT - 1)
                c += 1
        for i in range(TT + 1):
            n = P if i < TT else S
            if i < TT:
                act.wait_ge(s_yt, i + 1)
            else:
                act.wait_ge(s_x3, 1)
            y = ytok[i % 2][0:n, :] if i < TT else x2s[:, :]
            if i >= 2 and i < TT:
                act.wait_ge(s_ytok[i % 2], 16)
            if i < TT:
                for e in range(2):
                    act.activation(y[:, e * 512:(e + 1) * 512], bank[2 * (i % 2) + e][0:n, :], ACT.Square,
                                   accum_out=st[0:n, e:e + 1])
            else:
                act.activation(gmod2[:, :], x2s[:, :], ACT.Square, accum_out=st[0:n, 0:1])
            act.drain().then_inc(s_ysq, 1)
            act.wait_ge(s_yi, i + 1)
            act.activation(st2[0:n, 1:2], st2[0:n, 0:1], ACT.Sqrt).then_inc(s_yr, 1)

    @block.tensor
    def _(pe):
        for s in (s_ft, s_lg):
            pe.sem_inc(s, 2)
        for s in (s_ptp, s_pv, s_mtp, s_ro):
            pe.sem_inc(s, 1)
        pe.wait_ge(s_ident, 16)
        pe.wait_ge(s_silu, 1)
        for k in range(KT):
            last = pe.transpose(bank[4][:, k * NSEQ:(k + 1) * NSEQ], crow[:, k * P:(k + 1) * P], ident[0:NSEQ, 0:NSEQ])
        last.then_inc(s_ctp, 1)
        pe.wait_ge(s_vec, 80)
        pe.transpose(bank[5][:, 0:NVEC], vrow[:, :], ident[0:NVEC, 0:NVEC]).then_inc(s_vtp, 1)
        pe.wait_ge(s_ct, 1)

        def rows_by_k(out, lhs, rhs, kd, first, final):
            for k in range(kd):
                g = k % 4
                last = pe.matmul(out[32 * g:32 * g + 32, 0:CHUNK], lhs(k), rhs[:, k, :],
                                 start=(first and k < 4), stop=(final and k >= kd - 4))
            return last

        def mod_chunk(buf, pair, e):
            pe.wait_ge(s_mev, 2 * pair + e + 1)
            rows_by_k(bank[6 + e], lambda k: cT[:, k, :], buf, KT, True, True).then_inc(s_md, 1)

        def turn_mod(pair):
            pe.wait_ge(s_mp, pair + 1)
            pe.wait_ge(s_mev, 2 * pair + 4)
            for f in range(4):
                last = pe.transpose(bank[3][:, f * P:(f + 1) * P], mst[:, f * P:(f + 1) * P], ident)
            last.then_inc(s_mtp, 1)

        with pe.Fori(0, NMA // 2) as i:
            for u in range(2):
                pe.wait_ge(s_w[u], 16 * (i + 1))
                mod_chunk(raw[u], i, u)
            turn_mod(i)
        pe.wait_ge(s_mp, NMA // 2 + 1)
        pe.wait_ge(s_xn, 1)

        def turn_rows(src, k, n, out=None):
            out = bank[2 + k % 2] if out is None else out
            for i in range(TT):
                last = pe.transpose(out[:, i * P:(i + 1) * P], src(i), ident)
            last.then_inc(s_xt, 1)

        for k in range(KT):
            if k >= 2:
                pe.wait_ge(s_stg, k - 1)
            turn_rows(lambda i: xP[:, i, k * P:(k + 1) * P], k, k)
        pe.wait_ge(s_xsn, 1)
        for k in range(KT):
            last = pe.transpose(bank[7][:, k * S:(k + 1) * S], sq[0:S, k * P:(k + 1) * P], ident[0:S, 0:S])
        last.then_inc(s_xst, 1)

        def tile(m, q, kd=KT, hi=None, lo=None, k0=0, out=None, first=True, final=True, ready=None):
            hi, lo = (ahi, alo) if hi is None else (hi, lo)
            out = bank[q % 2] if out is None else out
            pe.wait_ge(s_lo, m + 1)
            for k in range(kd):
                if ready is not None:
                    pe.wait_ge(s_hlo, ready + k + 1)
                pe.matmul(out[:, :], whi[q % 2][:, k, :], hi[:, k0 + k, :], start=(first and k == 0), stop=False)
                pe.matmul(out[:, :], whi[q % 2][:, k, :], lo[:, k0 + k, :], start=False, stop=False)
                last = pe.matmul(out[:, :], wlo[q % 2][:, k, :], hi[:, k0 + k, :], start=False, stop=(final and k == kd - 1))
            last.then_inc(s_ft, 1)

        def sample_chunk(u, lhs, kd=KT, first=True, final=True, out=None):
            rows_by_k(bank[4 + u] if out is None else out, lhs, raw[u], kd, first, final).then_inc(s_ss, 1)

        def stage_pair(F, N, i, after=None, ready=None, sample_ready=None):
            for q in range(4):
                pe.wait_ge(s_ev, F + 4 * i + q + 1)
                tile(F + 4 * i + q, q, ready=ready if q == 0 else None)
                if q == 1 and sample_ready is not None:
                    pe.wait_ge(s_hs, sample_ready)
                if q % 2:
                    pe.wait_ge(s_sev, N + 2 * i + q // 2 + 1)
                    sample_chunk(q // 2, lambda k: asT[:, k, :])
                if after:
                    after(i, q)

        def mod_between(i, q):
            if q % 2:
                pe.wait_ge(s_wm, 16 * (2 * i + q // 2 + 1))
                mod_chunk(rawm, NMA // 2 + i, q // 2)
            elif q == 0 and not isinstance(i, int):
                turn_mod(NMA // 2 + i - 1)

        stage_pair(0, 0, 0, mod_between, ready=0, sample_ready=1)
        with pe.Fori(1, NIN // 2) as i:
            stage_pair(0, 0, i, mod_between)
        def rotate(hp):
            for n, sec in enumerate((RK, RQ)):
                pe.matmul(bank[n][:, :], C("rot"), zT[:, bass.ds(sec + hp, 1), :].rearrange("p a t -> p (a t)"),
                          start=True, stop=True).then_inc(s_rr, 1)

        pe.wait_ge(s_ev, 2 * NIN + 2)
        pe.wait_ge(s_const, 16)
        rotate(0)
        pe.wait_ge(s_sev, NIN + 2)
        n = 0
        for sec in (MK, MV, RV):
            for j in range(4):
                if n == 4:
                    turn_mod(NMOD // 2 - 2)
                    for u in range(2):
                        pe.wait_ge(s_w[u], 16 * (B_MODB + 1))
                        mod_chunk(raw[u], NMOD // 2 - 1, u)
                if n >= 2:
                    pe.wait_ge(s_vt2, n - 1)
                for i in range(TT):
                    last = pe.transpose(bank[4 + n % 2][:, i * P:(i + 1) * P], zT[:, sec + j, i * P:(i + 1) * P], ident)
                last.then_inc(s_vt1, 1)
                n += 1
        turn_mod(NMOD // 2 - 1)
        pe.wait_ge(s_vt2, 12)
        pe.wait_ge(s_mp, NMOD // 2 + 1)
        def retention(hp, last_pair):
            pe.wait_ge(s_rk, 2 * hp + 1)
            for c in range(TT):
                last = pe.transpose(bank[2][:, c * P:(c + 1) * P], scr[:, 1, c * P:(c + 1) * P], ident)
            last.then_inc(s_kt1, 1)
            pe.wait_ge(s_rk, 2 * hp + 2)
            for h2 in range(2):
                r = 64 * h2
                for c in range(TT):
                    last = pe.matmul(bank[4 + h2][:, c * P:(c + 1) * P], scr[r:r + 64, 1, c * P:(c + 1) * P],
                                     scr[r:r + 64, 0, c * P:(c + 1) * P], start=True, stop=True)
            last.then_inc(s_ra, 1)
            pe.wait_ge(s_kt2, hp + 1)
            for c in range(TT):
                last = pe.matmul(bank[3][:, c * P:(c + 1) * P], scr[:, 4, c * P:(c + 1) * P],
                                 rvtok[:, c, bass.ds(hp * P, P)], start=True, stop=True)
            last.then_inc(s_kv, 1)
            if not last_pair:
                rotate(hp + 1)
            else:
                pe.wait_ge(s_srot, 1)
                for n, x in enumerate((qrs, krs)):
                    for j in range(HP):
                        last = pe.transpose(bank[2][:, (n * HP + j) * S:(n * HP + j + 1) * S], x[:, j * P:(j + 1) * P], ident[0:S, 0:S])
                last.then_inc(s_sqt, 1)
            pe.wait_ge(s_rad, hp + 1)
            pe.wait_ge(s_st, hp + 1)
            pe.wait_ge(s_roc, 2 * hp + 1)
            for h2 in range(2):
                r = 64 * h2
                for c in range(TT):
                    last = pe.matmul(bank[6 + h2][:, c * HD:(c + 1) * HD], scr[:, 5 + h2, c * P:(c + 1) * P],
                                     rvtok[:, c, bass.ds(hp * P + r, HD)], start=True, stop=(c == 0))
                    if c:
                        last = pe.matmul(bank[6 + h2][:, c * HD:(c + 1) * HD], scr[r:r + 64, 2, c * P:(c + 1) * P],
                                         sst[r:r + 64, c - 1, :], start=False, stop=True)
            last.then_inc(s_ro, 1)

        with pe.Fori(0, HP - 1) as hp:
            retention(hp, False)
        retention(HP - 1, True)
        pe.wait_ge(s_sqe, 1)
        for h2 in range(2):
            r = 64 * h2
            for hp in range(HP):
                last = pe.matmul(bank[4 + h2][0:S, hp * S:(hp + 1) * S], sT[r:r + 64, 1, hp, :], sT[r:r + 64, 0, hp, :],
                                 start=True, stop=True)
        last.then_inc(s_sa, 1)
        pe.wait_ge(s_sad, 1)
        pe.wait_ge(s_roc, 2 * HP + 1)
        pe.wait_ge(s_state, 16)
        for h2 in range(2):
            r = 64 * h2
            for hp in range(HP):
                at = 2 * W + (2 * hp + h2) * HD
                pe.matmul(bank[6 + h2][r:r + 64, hp * S:(hp + 1) * S], zs[:, at:at + HD], ats[:, 2 * hp + h2, :],
                          start=True, stop=False, skip_group_check=True)
                for b in range(NB_SEQ):
                    last = pe.matmul(bank[6 + h2][r:r + 64, hp * S + TS * b:hp * S + TS * (b + 1)],
                                     state[r:r + 64, b, hp, :], sT[r:r + 64, 2, hp, TS * b:TS * (b + 1)],
                                     start=False, stop=(b == NB_SEQ - 1), skip_group_check=True)
        last.then_inc(s_so, 1)
        pe.wait_ge(s_soc, 1)
        for hp in range(HP):
            last = pe.transpose(bank[0][0:S, hp * P:(hp + 1) * P], sT[:, 0, :, :].rearrange("p a b -> p (a b)")[:, hp * S:(hp + 1) * S], ident)
        last.then_inc(s_sot, 1)
        for b in range(NB_SEQ):
            pe.wait_ge(s_km, b + 1)
            if b >= 4:
                pe.wait_ge(s_sts, b - 3)
            for hp in range(HP):
                last = pe.matmul(bank[2 + b % 4][:, hp * P:(hp + 1) * P], kmask[b % 2][:, hp * P:(hp + 1) * P],
                                 zs[:, 2 * W + hp * P:2 * W + (hp + 1) * P], start=True, stop=True)
            last.then_inc(s_kvs, 1)
        pe.wait_ge(s_srn, 1)
        for hp in range(HP):
            last = pe.transpose(bank[1][:, hp * S:(hp + 1) * S], ret_s[:, hp * P:(hp + 1) * P], ident[0:S, 0:S])
        last.then_inc(s_srt, 1)
        pe.wait_ge(s_sas, 1)

        def scores(b, pair, par, u):
            r, n = 64 * par, (u + 1) * P
            pe.wait_ge(s_p, 4 * b + u + 1)
            pe.matmul(bank[5][:, 0:n], scr[r:r + 64, 0, n - P:n],
                      scr[r:r + 64, 3, 0:n], start=True, stop=True).then_inc(s_sc, 1)

        def turn(b, u):
            pe.wait_ge(s_pte, 4 * b + u + 1)
            pe.wait_ge(s_p, 4 * b + u + 2)
            for j in range(u + 1):
                last = pe.transpose(bank[6][:, j * P:(j + 1) * P], scr[:, 1, j * P:(j + 1) * P], ident)
            last.then_inc(s_ptp, 1)

        def weigh(b, pair, par, u):
            pe.wait_ge(s_on, 4 * b + u + 1)
            pe.wait_ge(s_pte, 4 * b + u + 2)
            for j in range(u + 1):
                last = pe.matmul(bank[7][:, 0:HD], scr[:, 2, j * P:(j + 1) * P],
                                 mvtok[:, j, bass.ds(pair * P + par * HD, HD)], start=(j == 0), stop=(j == u))
            last.then_inc(s_pv, 1)

        def keys(b, par, g):
            if g % 4 == 0:
                pe.wait_ge(s_le, 2 * b + g // 4 + 1)
            pe.wait_ge(s_kt, NGRP * b + g + 1)
            for jj in range(4):
                for gq in range(4):
                    j = 4 * gq + jj
                    last = pe.matmul(bank[g // 4][32 * gq:32 * gq + 32, (g % 4) * P:(g % 4 + 1) * P],
                                     qbd[par][:, j, :], KTb[g % 2][:, :, j, :], start=(jj == 0), stop=(jj == 3))
            last.then_inc(s_lg, 1)

        def own_keys(b, par):
            for jj in range(4):
                for gq in range(4):
                    j = 4 * gq + jj
                    last = pe.matmul(bank[3][32 * gq:32 * gq + 32, 64:64 + S], qbd[par][0:32, j, :], kbb[0:32, j, :],
                                     start=(jj == 0), stop=(jj == 3))
            last.then_inc(s_own, 1)

        def weigh_pages(b, g):
            for pg in range(GRP):
                s = (4 * g + pg) % 8
                rounds = 4 * b + (4 * g + pg) // 8
                if s % 2 and isinstance(b, int) and rounds >= V_SHARED:
                    pe.wait_ge(s_k[s // 2], 16 * (NB_SEQ * NGRP // 4 + rounds - V_SHARED + 1))
                else:
                    pe.wait_ge(s_v[s], 16 * (rounds + 1))
                pe.matmul(bank[4][32 * pg:32 * pg + 32, :], pT[:, g, 32 * pg:32 * pg + 32],
                          VB[s][:, :], start=(g == 0), stop=(g == NGRP - 1)).then_inc(s_vd, 1)

        def turn_probs(b, e):
            pe.wait_ge(s_ex, 2 * b + e + 1)
            if e:
                pe.wait_ge(s_te, 2 * b + 1)
            for g in range(4):
                last = pe.transpose(bank[2][:, g * P:(g + 1) * P], pe_x[:, 4 * e + g, :], ident)
            last.then_inc(s_tp, 1)

        def fold(b):
            pe.wait_ge(s_of, b + 1)
            pe.matmul(bank[3][0:32, 128:128 + HD], C("sum_pv"), sm[:, 832:896], start=True, stop=True).then_inc(s_oe, 1)

        def step(b, par, head=True, tail=True, rest=True):
            pair = b // 2 if isinstance(b, int) else (b - par) // 2
            prev = b - 1
            if head:
                pe.wait_ge(s_qd, b + 1)
                pe.wait_ge(s_qk, pair + 1)
            for slot in range(8):
                if head:
                    keys(b, par, slot)
                if tail and rest and slot == 0:
                    pe.wait_ge(s_oa, prev - 1)
                if rest and slot < 5:
                    weigh_pages(b - 2, slot + 3)
                if tail and slot == 0:
                    own_keys(prev, 1 - par)
                if tail and slot == 1:
                    pe.wait_ge(s_s1, prev + 1)
                    for n, name in enumerate(("pair0", "pair1", "own_pair")):
                        last = pe.matmul(bank[3][:, n * NGRP:(n + 1) * NGRP], C(name), sm[:, 0:NGRP], start=True, stop=True)
                    last.then_inc(s_gt, 1)
                if tail and slot == 2:
                    pe.wait_ge(s_mx, prev + 1)
                    pe.transpose(bank[3][0:1, 0:P], sm[:, 56:57], ident).then_inc(s_mxt, 1)
                if head and slot % 2:
                    turn(b, slot // 2)
                elif head:
                    if slot:
                        weigh(b, pair, par, slot // 2 - 1)
                    scores(b, pair, par, slot // 2)
                if tail and slot == 2:
                    pe.wait_ge(s_rm, prev + 1)
                    pe.matmul(bank[3][:, 0:1], sm[0:1, 384:512], ones[0:1, 0:1], start=True, stop=True).then_inc(s_mb, 1)
                if tail and slot in (3, 4):
                    turn_probs(prev, slot - 3)
                if tail and slot == 4:
                    pe.transpose(bank[3][0:S, 0:P], sm[:, 576:608], ident).then_inc(s_tt, 1)
                if tail and slot == 5:
                    pe.wait_ge(s_rsm, prev + 1)
                    pe.wait_ge(s_to, prev + 1)
                    pe.matmul(bank[3][0:32, 0:1], C("sum_g"), sm[:, 650:651], start=True, stop=True).then_inc(s_den, 1)
                    pe.wait_ge(s_te, 2 * prev + 2)
                    if rest:
                        pe.wait_ge(s_of, prev)
                if tail and slot >= 5:
                    weigh_pages(prev, slot - 5)
                if tail and slot == 5:
                    pe.matmul(bank[4][0:32, :], sm[0:S, 704:736], zs[:, 6 * W:7 * W], start=False, stop=False)
                if rest and slot == 6:
                    if tail:
                        pe.wait_ge(s_rcp, prev + 1)
                    fold(b - 2)
            if head:
                weigh(b, pair, par, 3)

        moba_steps(pe, step)
        for g in (3, 4):
            weigh_pages(NB_SEQ - 1, g)
        pe.wait_ge(s_hn, 2)
        for k in range(KT):
            src = rettok if k < 4 else mobatok
            if k >= 2:
                pe.wait_ge(s_stg, KT + k - 1)
            turn_rows(lambda i: src[:, i, (k % 4) * P:(k % 4 + 1) * P], k, KT + k, bank[k % 2])
            if k < 3:
                weigh_pages(NB_SEQ - 1, 5 + k)
            if k == 5:
                fold(NB_SEQ - 1)
        for q in range(2):
            pe.wait_ge(s_ev, F_OUT + q + 1)
            pe.wait_ge(s_stg, 2 * KT - 1 + q)
            tile(F_OUT + q, q, ready=KT if q == 0 else None)
        pe.wait_ge(s_ofr, 1)
        for b in range(NB_SEQ):
            last = pe.transpose(bank[5][0:HD, b * 32:(b + 1) * 32], oall[:, b, :], ident[0:32, 0:32])
        last.then_inc(s_oft, 1)

        pe.wait_ge(s_x2l, 16)
        for k in range(KT):
            if k >= 2:
                pe.wait_ge(s_xr, k - 1)
            turn_rows(lambda i: xP2[:, i, k * P:(k + 1) * P], k, 2 * KT + k)

        def gates_to_rows(n):
            pe.wait_ge(s_hs, 2 + 2 * n)
            for k in range(KT):
                last = pe.transpose(bank[6 + k // 4][0:S, (k % 4) * P:(k % 4 + 1) * P], asm[:, k * S:(k + 1) * S], ident)
            last.then_inc(s_gmt, 1)

        gates_to_rows(0)
        pe.wait_ge(s_oas, 1)

        def sum_squares(k):
            pe.wait_ge(s_sqx, k + 1)
            pe.matmul(bank[2][:, :], ones, stage[k % 2][:, :], start=(k == 0), stop=(k == KT - 1)).then_inc(s_ssm, 1)

        pe.wait_ge(s_xr, KT)
        for f in range(1, KT):
            if f >= 2:
                pe.wait_ge(s_ev, F_OUT + f + 1)
                tile(F_OUT + f, f % 4)
                sum_squares(f - 2)
            if f % 2:
                pe.wait_ge(s_sev, N_OUT + f // 2 + 1)
                sample_chunk(f // 2 % 2, lambda k: asT[:, k, :])
        sum_squares(KT - 2)
        sum_squares(KT - 1)
        pe.wait_ge(s_x2n, 1)
        for k in range(KT):
            last = pe.transpose(bank[7][:, k * S:(k + 1) * S], xsn2[:, k * P:(k + 1) * P], ident[0:S, 0:S])
        last.then_inc(s_xst, 1)

        def turn_ff(n):
            pe.wait_ge(s_spr, n + 1)
            pe.transpose(bank[7][:, 0:P], asm[:, 0:P], ident).then_inc(s_smt, 1)

        def turn_before(i, q):
            if q % 2 and not (isinstance(i, int) and i + q == 1):
                turn_ff(2 * i + q // 2 - 1)

        stage_pair(F_FFN, N_FFN, 0, turn_before, ready=2 * KT, sample_ready=3)
        with pe.Fori(1, FT // 2) as i:
            stage_pair(F_FFN, N_FFN, i, turn_before)
        c = 0
        for fb in range(DM // CHUNK):
            for n, kd in enumerate(KD):
                pe.wait_ge(s_fl, 8 * n + kd + 1)
                for half in range(2):
                    if c == 0 and half == 1:
                        turn_ff(FT - 1)
                        gates_to_rows(1)
                    if n == 0 and fb != 1:
                        pe.wait_ge(s_ev, F_DOWN + half + (2 * fb - 1 if fb else 1))
                    tile(F_DOWN + 2 * c + half, half, kd, fhi, flo, 8 * n, bank[2 * (fb % 2) + half], n == 0, n == 2)
                if n == 0:
                    pe.wait_ge(s_sev, N_DOWN + fb + 1)
                pe.wait_ge(s_sme, 8 * n + kd)
                sample_chunk(c % 2, lambda k: aT[:, 8 * n + k, :], kd, n == 0, n == 2, bank[4 + fb % 2])
                c += 1
        pe.wait_ge(s_ev, F_DOWN + 8 + 2)
        for i in range(TT):
            if i >= 2:
                pe.wait_ge(s_y, i - 1)
            for k in range(KT):
                last = pe.transpose(bank[2 * (i % 2) + k // 4][:, (k % 4) * P:(k % 4 + 1) * P], x2T[:, k, i * P:(i + 1) * P], ident)
            last.then_inc(s_yt, 1)

    @block.vector
    def _(dve):
        tt, ts, cp = dve.tensor_tensor, dve.tensor_scalar, dve.tensor_copy
        for s in (s_ev, s_sev, s_mev):
            dve.sem_inc(s, 2)
        for s in (s_fl, s_mp, s_on):
            dve.sem_inc(s, 1)
        dve.memset(cT[:, :, :], 0.0)
        dve.memset(mst[:, :], 0.0)
        dve.drain()

        def then(ins):
            dve.drain()
            return ins

        dve.wait_ge(s_ctp, 1)
        cp(cT[:, :, 0:NSEQ], bank[4][:, 0:KT * NSEQ].rearrange("p (k s) -> p k s", k=KT)).then_inc(s_ct, 1)
        dve.wait_ge(s_vtp, 1)
        then(cp(vT[:, :], bank[5][:, 0:NVEC]))
        def fold_groups(dst, src, done):
            then(cp(dst, src[0:32, 0:CHUNK]))
            for g in range(1, 4):
                last = then(tt(dst, dst, src[32 * g:32 * g + 32, 0:CHUNK], ALU.add))
            last.then_inc(done, 1)

        def keep_mod(pair, e):
            dve.wait_ge(s_md, 2 * pair + e + 1)
            fold_groups(mst[0:32, CHUNK * e:CHUNK * (e + 1)], bank[6 + e], s_mev)

        def modulation(pair):
            dve.wait_ge(s_mtp, pair + 2)
            f = bass.ds(4 * pair, 4)
            then(tt(mT[:, f, :], bank[3][:, :].rearrange("p (f s) -> p f s", f=4)[:, :, 0:NSEQ],
                    vT[:, f].unsqueeze(2).broadcast_to((P, 4, NSEQ)), ALU.add)).then_inc(s_mp, 1)

        def gains(f0, v0):
            dve.scalar_tensor_tensor(gain[:, :, :], mT[:, f0:f0 + KT, :], 1.0,
                                     vT[:, v0:v0 + KT].unsqueeze(2).broadcast_to((P, KT, NSEQ)), ALU.add, ALU.mult)
            dve.drain().then_inc(s_mt, 1)

        for pair in range(NMA // 2):
            for e in range(2):
                keep_mod(pair, e)
            modulation(pair)
            if pair == 0:
                dve.wait_ge(s_sqd, 1)
                ts(st2[:, 8:12], st[:, 0:4], 1.0 / DM, EPS, ALU.mult, ALU.add)
                then(ts(st2[0:S, 12:13], st[0:S, 4:5], 1.0 / DM, EPS, ALU.mult, ALU.add))
                dve.reciprocal(st2[:, 8:12], st2[:, 8:12])
                dve.reciprocal(st2[0:S, 12:13], st2[0:S, 12:13])
                dve.drain().then_inc(s_rin, 1)
        dve.drain()
        gains(8, V_N1)

        def act_lo(k, n):
            dve.wait_ge(s_hhi, n + 1)
            tt(alo[:, k, :], stage[k % 2][:, :], ahi[:, k, :].bitcast(F32), ALU.subtract).then_inc(s_hlo, 1)

        def split_lo(m, q, kd=KT):
            dve.wait_ge(s_hi, m + 1)
            tt(wlo[q % 2][:, 0:kd, :], raw[q // 2][:, 0:kd, q % 2 * P:(q % 2 + 1) * P],
               whi[q % 2][:, 0:kd, :].bitcast(F32), ALU.subtract).then_inc(s_lo, 1)

        split_lo(0, 0)
        for k in range(KT):
            act_lo(k, k)

        def by_seq(x):
            return x.unsqueeze(3).broadcast_to((P, KT, NB_SEQ, TS))

        asT4 = asT[:, :, :].rearrange("p k (b t) -> p k b t", t=TS)

        def sample_h(n, f_shift):
            dve.wait_ge(s_xst, n)
            then(tt(asT4, bank[7][:, 0:KT * S].rearrange("p (k b t) -> p k b t", k=KT, t=TS), by_seq(gain[:, :, 0:NB_SEQ]), ALU.mult))
            tt(asT4, asT4, by_seq(mT[:, f_shift:f_shift + KT, 0:NB_SEQ]), ALU.add).then_inc(s_hs, 1)

        sample_h(1, 0)
        dve.wait_ge(s_pt, 16)
        dve.wait_ge(s_const, 16)
        for g in range(GRP):
            q = slice(32 * g, 32 * g + 32)
            last = ts(kidx[q, :], pt[q, :].rearrange("p (n g) -> p n g", g=GRP)[:, :, g], 32.0, C("row32")[q, :], ALU.mult, ALU.add)
        last.then_inc(s_idx, 1)

        def stage_pairs(F, pairs, evict, sample, peel=False, split_next=None):

            def body(i, last):
                for q in range(4):
                    if not (last and q == 3):
                        split_lo(F + 4 * i + q + 1, (q + 1) % 4)
                    elif split_next:
                        split_next()
                    if evict:
                        evict(i, q)
                    if q % 2:
                        sample(i, q // 2)

            if peel:
                body(0, False)
            with dve.Fori(int(peel), pairs - 1) as i:
                body(i, False)
            body(pairs - 1, True)

        def sample_z(i, u):
            dve.wait_ge(s_ss, 2 * i + u + 1)
            fold_groups(zs[:, bass.ds((2 * i + u) * CHUNK, CHUNK)], bank[4 + u], s_sev)
            keep_mod(NMA // 2 + i, u)

        def mod_pair_before(i, q):
            if q == 0 and not (isinstance(i, int) and i == 0):
                modulation(NMA // 2 + i - 1)

        stage_pairs(0, NIN // 2, mod_pair_before, sample_z, peel=True)
        modulation(NMOD // 2 - 2)
        dec3 = C("decay")

        def rotated(hp):
            for n, sec in enumerate((RK, RQ)):
                dve.wait_ge(s_rr, 2 * hp + n + 1)
                tt(stage[1][:, :], zT[:, bass.ds(sec + hp, 1), :].rearrange("p a t -> p (a t)"), C("cos"), ALU.mult)
                then(tt(stage[0][:, :], bank[n][:, :], C("sin"), ALU.mult))
                then(tt(scr[:, 1 - n, :], stage[1][:, :], stage[0][:, :], ALU.add))
                dve.drain().then_inc(s_rk, 1)

        def retention(hp, last_pair):
            dve.wait_ge(s_kt1, hp + 1)
            tt(scr[:, 4, :].rearrange("p (c h d) -> p c h d", c=4, h=2), bank[2][:, :].rearrange("p (c h d) -> p c h d", c=4, h=2),
               C("k_dec")[:, bass.ds(2 * hp, 2)].unsqueeze(1).unsqueeze(3).broadcast_to((P, 4, 2, HD)), ALU.mult).then_inc(s_kt2, 1)
            dve.wait_ge(s_ra, hp + 1)
            dve.wait_ge(s_ro, hp + 1)
            for h2 in range(2):
                tt(scr[:, 5 + h2, :].rearrange("p (c i) -> p c i", c=4), bank[4 + h2][:, :].rearrange("p (c i) -> p c i", c=4),
                   dec3[:, bass.ds(2 * hp + h2, 1), :].broadcast_to((P, 4, P)), ALU.mult)
            tt(scr[:, 2, :].rearrange("p (c i) -> p c i", c=4), scr[:, 0, :].rearrange("p (c i) -> p c i", c=4),
               C("q_dec")[:, bass.ds(hp, 1), :].broadcast_to((P, 4, P)), ALU.mult).then_inc(s_rad, 1)
            dve.wait_ge(s_kv, hp + 1)
            dve.wait_ge(s_rs, 16 * hp + 16)
            for c in range(TT):
                for h2 in range(2):
                    r = 64 * h2
                    kv = bank[3][r:r + 64, c * P + r:c * P + r + HD]
                    if c == 0:
                        cp(sst[r:r + 64, 0, :], kv)
                    else:
                        dve.scalar_tensor_tensor(sst[r:r + 64, c, :], sst[r:r + 64, c - 1, :],
                                                 C("c_dec")[r:r + 64, bass.ds(hp, 1)], kv, ALU.mult, ALU.add)
                if c < TT - 1:
                    dve.drain()
                else:
                    dve.drain().then_inc(s_st, 1)
            if not last_pair:
                rotated(hp + 1)

        dve.wait_ge(s_const, 16)
        rotated(0)
        for e in range(2):
            keep_mod(NMOD // 2 - 1, e)
        modulation(NMOD // 2 - 1)
        dve.wait_ge(s_kst, 16)
        with dve.Fori(0, HP - 1) as hp:
            retention(hp, False)
        retention(HP - 1, True)
        dve.wait_ge(s_sqt, 1)
        cp(sT[:, 0, :, :], bank[2][:, 0:P].rearrange("p (h s) -> p h s", h=HP))
        then(cp(sT[:, 1, :, :], bank[2][:, P:2 * P].rearrange("p (h s) -> p h s", h=HP)))
        tt(sT[:, 2, :, :], sT[:, 0, :, :], C("q_dec_s"), ALU.mult).then_inc(s_sqe, 1)
        dve.wait_ge(s_sa, 1)
        byh2 = lambda x: x.rearrange("p (hp h2) s -> p h2 hp s", h2=2)
        for h2 in range(2):
            last = tt(byh2(ats[:, :, :])[:, h2], bank[4 + h2][0:S, 0:P].rearrange("p (h s) -> p h s", h=HP),
                      byh2(C("decay_s"))[:, h2], ALU.mult)
        last.then_inc(s_sad, 1)
        dve.wait_ge(s_so, 1)
        for h2 in range(2):
            r = 64 * h2
            last = cp(sT[r:r + 64, 0, :, :], bank[6 + h2][r:r + 64, 0:P].rearrange("p (h s) -> p h s", h=HP))
        last.then_inc(s_soc, 1)
        def block_diagonal(b, par):
            qv = qbd[par][:, :, :].rearrange("p (g hh half) c -> p g hh half c", g=4, hh=2)
            qi = qbb[0:32, :, :].rearrange("p (g hh half) s -> p g hh half s", g=4, hh=2)
            for pg in range(GRP):
                for hh in range(2):
                    cp(qv[32 * pg:32 * pg + 32, :, hh, :, hh * 16 + pg * 4:hh * 16 + pg * 4 + 4],
                       qi[:, :, hh, :, bass.ds(TS * b, TS)])
            dve.drain().then_inc(s_qd, 1)

        dve.transpose(qbb[0:32, :, :], zs[:, 4 * W:5 * W])
        dve.transpose(kbb[0:32, :, :], zs[:, 5 * W:6 * W])
        for x in qbd:
            dve.memset(x[:, :, :], 0.0)
        dve.drain()
        block_diagonal(0, 0)
        dve.wait_ge(s_sot, 1)
        dve.wait_ge(s_ssg, 1)
        r3 = ret_s[:, :].rearrange("p (h d) -> p h d", h=H)
        k3 = qrs[:, :].rearrange("p (h d) -> p h d", h=H)
        sp3 = lambda x: x.unsqueeze(2).broadcast_to((S, H, HD))
        then(dve.tensor_reduce(st[0:S, 0:H], bank[0][0:S, :].rearrange("p (h d) -> p h d", h=H), AX.X, ALU.add))
        then(ts(st[0:S, 0:H], st[0:S, 0:H], 1.0 / HD, None, ALU.mult))
        then(tt(r3, bank[0][0:S, :].rearrange("p (h d) -> p h d", h=H), sp3(st[0:S, 0:H]), ALU.subtract))
        then(tt(k3, r3, r3, ALU.mult))
        then(dve.tensor_reduce(st[0:S, 8:8 + H], k3, AX.X, ALU.add))
        then(ts(st2[0:S, 8:8 + H], st[0:S, 8:8 + H], 1.0 / HD, EPS, ALU.mult, ALU.add))
        dve.reciprocal(st2[0:S, 8:8 + H], st2[0:S, 8:8 + H]).then_inc(s_ssq, 1)
        dve.wait_ge(s_srs, 1)
        then(tt(r3, r3, sp3(st2[0:S, 0:H]), ALU.mult))
        tt(ret_s[:, :], ret_s[:, :], zs[:, 3 * W:4 * W], ALU.mult).then_inc(s_srn, 1)
        dve.wait_ge(s_sdc, 1)
        for b in range(NB_SEQ):
            dve.wait_ge(s_kvs, b + 1)
            for h2 in range(2):
                r = 64 * h2
                last = tt(state[r:r + 64, b, :, :], state[r:r + 64, b, :, :],
                          bank[2 + b % 4][r:r + 64, :].rearrange("p (h c) -> p h c", h=HP)[:, :, r:r + HD], ALU.add)
            last.then_inc(s_sts, 1)
        dve.wait_ge(s_srt, 1)
        tt(asT[:, 0:4, :], bank[1][:, 0:P].rearrange("p (h s) -> p h s", h=HP),
           vT[:, V_GN:V_GN + 4].unsqueeze(2).broadcast_to((P, HP, S)), ALU.mult).then_inc(s_sas, 1)

        def negmax(b, u):
            n = (u + 1) * P
            dve.wait_ge(s_sc, 4 * b + u + 1)
            then(tt(bank[5][:, n - P:n], bank[5][:, n - P:n], C("causal"), ALU.add))
            then(dve.tensor_reduce(st2[:, 16 + u % 2:17 + u % 2], bank[5][:, 0:n], AX.X, ALU.max))
            then(ts(st2[:, 20 + u % 2:21 + u % 2], st2[:, 16 + u % 2:17 + u % 2], -SCALE, None, ALU.mult)).then_inc(s_nm, 1)

        def norm(b, pair, par, u):
            dve.wait_ge(s_pv, 4 * b + u + 2)
            then(dve.reciprocal(st2[:, 24 + u % 2:25 + u % 2], st[:, 16 + u:17 + u]))
            then(ts(mobatok[:, u, bass.ds(pair * P + par * HD, HD)], bank[7][:, 0:HD],
                    st2[:, 24 + u % 2:25 + u % 2], None, ALU.mult)).then_inc(s_on, 1)

        def turn_keys(b, g):
            dve.wait_ge(s_k[g % 4], 16 * (2 * b + g // 4 + 1))
            following = NGRP * b + g + 4
            if not (isinstance(following, int) and following >= NB_SEQ * NGRP):
                cp(kix[g % 4][:, :], kidx[:, bass.ds(following, 1)])
            dve.wait_ge(s_lg, NGRP * b + g + 1)
            dve.transpose(KTb[g % 2][:, :, :, :], Kb[g % 4][:, :]).then_inc(s_kt, 1)

        def block_sums(b):
            dve.wait_ge(s_le, 2 * b + 4)
            dve.tensor_reduce(sm[:, 0:NGRP], lgs[:, :, :], AX.X, ALU.add)
            dve.tensor_reduce(sm[:, 8:8 + NGRP], lgs[:, :, :], AX.X, ALU.max)
            dve.wait_ge(s_own, b + 1)
            tt(sm[:, 512:544], bank[3][:, 64:64 + S], C("own_mask")[:, bass.ds(b, 1), :].rearrange("p a s -> p (a s)"), ALU.add)
            dve.drain().then_inc(s_s1, 1)

        def select(b):
            dve.wait_ge(s_gt, b + 1)
            cp(sm[:, 16:32].rearrange("p (g e) -> p e g", e=2), bank[3][:, 0:16].rearrange("p (e g) -> p e g", e=2))
            then(cp(sm[:, 32:40], bank[3][:, 16:24]))
            gall = sm[:, 16:32].unsqueeze(1).broadcast_to((P, NGRP, NBLK))
            gown = sm[:, 32:40].unsqueeze(2).broadcast_to((P, NGRP, NBLK))
            gt = sm[:, 64:192].rearrange("p (n m) -> p n m", n=NGRP)
            eq = sm[:, 192:320].rearrange("p (n m) -> p n m", n=NGRP)
            tt(gt, gall, gown, ALU.is_gt)
            then(tt(eq, gall, gown, ALU.is_equal))
            then(tt(eq, eq, C("earlier"), ALU.mult))
            then(tt(gt, gt, eq, ALU.add))
            then(dve.tensor_reduce(sm[:, 40:48], gt, AX.X, ALU.add))
            then(ts(sm[:, 48:56], sm[:, 40:48], TOPK - 0.5, -BIG, ALU.is_gt, ALU.mult))
            then(tt(sm[:, 8:16], sm[:, 8:16], sm[:, 48:56], ALU.add))
            dve.tensor_reduce(sm[:, 57:58], sm[:, 8:16], AX.X, ALU.max)
            then(dve.tensor_reduce(sm[:, 58:59], sm[:, 512:544], AX.X, ALU.max))
            then(tt(sm[:, 56:57], sm[:, 57:58], sm[:, 58:59], ALU.max)).then_inc(s_mx, 1)

        def row_max(b):
            dve.wait_ge(s_mxt, b + 1)
            then(dve.tensor_reduce(sm[0:1, 900:932], bank[3][0:1, 0:P].rearrange("p (h g t) -> p h t g", g=4, t=4), AX.X, ALU.max))
            then(cp(sm[0:1, 384:512].rearrange("p (h g t) -> p h g t", g=4, t=4),
                    sm[0:1, 900:932].rearrange("p (h t) -> p h t", t=4).unsqueeze(2).broadcast_to((1, 8, 4, 4)))).then_inc(s_rm, 1)

        def exp_bias(b):
            dve.wait_ge(s_mb, b + 1)
            then(ts(sm[:, 328:329], bank[3][:, 0:1], -SCALE, None, ALU.mult))
            then(ts(sm[:, 320:328], sm[:, 48:56], SCALE, sm[:, 328:329], ALU.mult, ALU.add)).then_inc(s_nb, 1)

        def denominators(b):
            dve.wait_ge(s_ex, 2 * b + 2)
            dve.tensor_reduce(sm[:, 650:651], sm[:, 640:649], AX.X, ALU.add).then_inc(s_rsm, 1)
            dve.wait_ge(s_tt, b + 1)
            cp(by_page(sm[0:S, 704:832]), turned(bank[3][0:S, 0:P])).then_inc(s_to, 1)

        def fold_heads(b):
            dve.wait_ge(s_vd, NPAGE * (b + 1))
            then(tt(od[:, :, :], bank[4][:, :].rearrange("p (h d) -> p h d", h=H),
                    C("head_diag").unsqueeze(2).broadcast_to((P, H, HD)), ALU.mult))
            then(dve.tensor_reduce(sm[:, 832:896], od[:, :, :].rearrange("p h d -> p d h"), AX.X, ALU.add)).then_inc(s_of, 1)

        def keep_out(b, par):
            dve.wait_ge(s_oe, b + 1)
            then(ts(oall[:, bass.ds(b, 1), :].rearrange("p a d -> p (a d)"), bank[3][0:32, 128:128 + HD],
                    sm[0:32, 940 + par:941 + par], None, ALU.mult)).then_inc(s_oa, 1)

        heads = lambda x: x.rearrange("p i (h d) -> p i h d", h=H)
        s1 = gain[:, 0:4, 0:8]
        s2 = gain[:, 4:8, 0:8]
        spread = lambda x: x.unsqueeze(3).broadcast_to((P, TT, H, HD))

        def centre_retention():
            dve.wait_ge(s_roc, 2 * HP + 1)
            then(dve.tensor_reduce(s1, heads(rettok), AX.X, ALU.add))
            then(ts(s1, s1, 1.0 / HD, None, ALU.mult))
            then(tt(heads(rettok), heads(rettok), spread(s1), ALU.subtract)).then_inc(s_hn, 1)

        def step(b, par, head=True, tail=True, rest=True):
            pair = b // 2 if isinstance(b, int) else (b - par) // 2
            prev = b - 1
            first, last_head = isinstance(b, int) and b == 0, isinstance(b, int) and b >= NB_SEQ - 1
            for slot in range(8):
                if head and slot < 7:
                    turn_keys(b, slot + 1)
                elif head and not last_head:
                    block_diagonal(b + 1, 1 - par)
                    turn_keys(b + 1, 0)
                if tail and slot == 0:
                    block_sums(prev)
                if tail and slot == 1:
                    select(prev)
                if tail and slot == 2:
                    row_max(prev)
                if head and slot % 2 == 0:
                    negmax(b, slot // 2)
                elif slot > 1 and head:
                    norm(b, pair, par, slot // 2 - 1)
                elif slot == 1 and not first and (head or tail):
                    norm(prev, (prev - (1 - par)) // 2, 1 - par, 3)
                if tail and slot == 2:
                    exp_bias(prev)
                if not head and slot == 3:
                    centre_retention()
                if rest and slot == 4:
                    fold_heads(b - 2)
                if tail and slot == 4:
                    denominators(prev)
                if tail and slot == 5:
                    dve.wait_ge(s_den, prev + 1)
                    then(dve.reciprocal(sm[0:32, 941 - par:942 - par], bank[3][0:32, 0:1])).then_inc(s_rcp, 1)
                if rest and slot == 6:
                    keep_out(b - 2, par)
        turn_keys(0, 0)
        moba_steps(dve, step)
        dve.wait_ge(s_hsq, 1)
        dve.drain()
        dve.tensor_reduce(s1, heads(sq_ret), AX.X, ALU.add)
        then(dve.tensor_reduce(s2, heads(sq_moba), AX.X, ALU.add))
        both = gain[:, :, 0:8]
        then(ts(both, both, 1.0 / HD, EPS, ALU.mult, ALU.add))
        dve.reciprocal(both, both).then_inc(s_hri, 1)
        dve.wait_ge(s_hrs, 1)
        tt(heads(rettok), heads(rettok), spread(s1), ALU.mult)
        tt(heads(mobatok), heads(mobatok), spread(s2), ALU.mult).then_inc(s_hn, 1)
        dve.wait_ge(s_sg, 1)
        for k in range(KT):
            dve.wait_ge(s_xt, KT + k + 1)
            if k < 4:
                dve.scalar_tensor_tensor(stage[k % 2][:, :], bank[k % 2][:, :], vT[:, V_GN + k:V_GN + k + 1],
                                         zT[:, RG + k, :], ALU.mult, ALU.mult).then_inc(s_stg, 1)
            else:
                ts(stage[k % 2][:, :], bank[k % 2][:, :], vT[:, V_MN + k - 4:V_MN + k - 3], None, ALU.mult).then_inc(s_stg, 1)
            act_lo(k, KT + k)
            dve.drain()
            if k == 3:
                fold_heads(NB_SEQ - 1)
            if k in (4, 5):
                split_lo(F_OUT + k - 4, k - 4)
        keep_out(NB_SEQ - 1, 1)
        dve.drain()
        o2 = sm[0:32, 0:512].rearrange("p (b d) -> p b d", b=NB_SEQ)
        then(tt(o2, oall[:, :, :], oall[:, :, :], ALU.mult))
        then(dve.tensor_reduce(st[0:32, 0:8], o2, AX.X, ALU.add))
        then(ts(st2[0:32, 8:16], st[0:32, 0:8], 1.0 / HD, EPS, ALU.mult, ALU.add))
        dve.reciprocal(st2[0:32, 8:16], st2[0:32, 8:16]).then_inc(s_ofs, 1)
        dve.wait_ge(s_ofq, 1)
        tt(oall[:, :, :], oall[:, :, :], st2[0:32, 0:8].unsqueeze(2).broadcast_to((32, NB_SEQ, HD)), ALU.mult).then_inc(s_ofr, 1)
        dve.wait_ge(s_oft, 1)
        for h2 in range(2):
            for hp in range(HP):
                ob = bank[5][0:HD, 0:256].rearrange("p (b h t) -> p h b t", b=NB_SEQ, t=TS)[:, 2 * hp + h2]
                cp(asT[64 * h2:64 * h2 + 64, 4 + hp, :].rearrange("p (b t) -> p b t", t=TS), ob)
        dve.drain()
        tt(asT[:, 4:8, :], asT[:, 4:8, :], vT[:, V_MN:V_MN + 4].unsqueeze(2).broadcast_to((P, HP, S)), ALU.mult)
        dve.drain().then_inc(s_oas, 1)

        asm4 = asm[:, 0:256].rearrange("p (k b t) -> p k b t", k=KT, t=TS)

        def gates(f0, n, dst):
            cp(asm4, by_seq(mT[:, f0:f0 + KT, 0:NB_SEQ]))
            dve.drain().then_inc(s_hs, 1)
            dve.wait_ge(s_gmt, n + 1)
            for e in range(2):
                cp(dst[:, e * 512:(e + 1) * 512], bank[6 + e][0:S, :])
            dve.drain()

        gates(16, 0, gmod)
        dve.wait_ge(s_xr, KT)

        def residual(f, gate_col, out):
            g = mT[:, gate_col, NB_SEQ:NSEQ]
            dve.scalar_tensor_tensor(x2T[:, f, :], out[:, :], g, x2T[:, f, :], ALU.mult, ALU.add).then_inc(s_ev, 1)

        def evict_out(i, q):
            f = 4 * i + q
            dve.wait_ge(s_ft, F_OUT + f + 3)
            residual(f, 16 + f, bank[q % 2])

        def sample_rows(at, src, g, base):
            c = slice(at, at + CHUNK)
            fold_groups(xtmp[:, :], src, s_sev)
            then(tt(xtmp[:, :], xtmp[:, :], g[:, c], ALU.mult))
            then(tt(x2s[:, c], base[:, c], xtmp[:, :], ALU.add))

        def sample_out(i, u):
            dve.wait_ge(s_ss, N_OUT + 2 * i + u + 1)
            sample_rows((2 * i + u) * CHUNK, bank[4 + u], gmod, xs)

        for f in range(KT):
            if 2 <= f + 1 < KT:
                split_lo(F_OUT + f + 1, (f + 1) % 4)
            if f == KT - 1:
                split_lo(F_FFN, 0)
            evict_out(f // 4, f % 4)
            if f % 2:
                sample_out(f // 4, f % 4 // 2)
        dve.drain().then_inc(s_x2s, 1)
        dve.wait_ge(s_ssm, KT)
        then(ts(rb[:, :], bank[2][:, :], 1.0 / DM, EPS, ALU.mult, ALU.add))
        gains(32, V_N2)
        dve.wait_ge(s_x2q, 1)
        then(ts(st2[0:S, 0:1], st[0:S, 0:1], 1.0 / DM, EPS, ALU.mult, ALU.add))
        dve.reciprocal(st2[0:S, 0:1], st2[0:S, 0:1]).then_inc(s_x2i, 1)
        dve.reciprocal(rb[:, :], rb[:, :]).then_inc(s_r1, 1)
        dve.wait_ge(s_r2, 1)
        for k in range(KT):
            tt(stage[k % 2][:, :], x2T[:, k, :], rb[:, :], ALU.mult).then_inc(s_nx, 1)
            if k >= 1:
                act_lo(k - 1, 2 * KT + k - 1)
                dve.drain()
        act_lo(KT - 1, 3 * KT - 1)
        sample_h(2, 24)

        def evict_ffn(i, q):
            n = 2 * i + q // 2
            if q % 2 == 0 and not (isinstance(n, int) and n == 0):
                sample_product(n - 1)
            if q % 2:
                dve.wait_ge(s_ft, F_FFN + 4 * i + q + 3)
                dve.wait_ge(s_ev, F_FFN + 4 * i + q + 2)
                tt(stage[1][:, :], stage[0][:, :], bank[1][:, :], ALU.mult).then_inc(s_ev, 1)
                dve.wait_ge(s_fh, n + 1)
                tt(flo[:, bass.ds(n, 1), :].rearrange("p a t -> p (a t)"), stage[1][:, :],
                   fhi[:, bass.ds(n, 1), :].rearrange("p a t -> p (a t)").bitcast(F32), ALU.subtract)
                dve.drain().then_inc(s_fl, 1)

        def sample_ffn(i, u):
            n = 2 * i + u
            dve.wait_ge(s_ss, N_FFN + n + 1)
            fold_groups(xtmp[:, :], bank[4 + u], s_sev)
            if not (isinstance(n, int) and n == 0):
                keep_turned(n - 1)

        def sample_product(n):
            dve.wait_ge(s_ssl, n + 1)
            then(tt(asm[0:S, 0:P], xtmp[:, 0:P], xtmp[:, P:2 * P], ALU.mult)).then_inc(s_spr, 1)

        def keep_turned(n):
            dve.wait_ge(s_smt, n + 1)
            cp(aT[:, bass.ds(n, 1), :].rearrange("p a s -> p (a s)"), bank[7][:, 0:S])
            dve.drain().then_inc(s_sme, 1)

        stage_pairs(F_FFN, FT // 2, evict_ffn, sample_ffn, peel=True,
                    split_next=lambda: split_lo(F_DOWN, 0, KD[0]))

        def evict_down(fb, half):
            dve.wait_ge(s_ft, F_DOWN + 6 * fb + 4 + half + 3)
            residual(2 * fb + half, 40 + 2 * fb + half, bank[2 * (fb % 2) + half])

        def sample_down(fb):
            dve.wait_ge(s_ss, N_DOWN + 3 * fb + 3)
            sample_rows(fb * CHUNK, bank[4 + fb % 2], gmod2, x2s)

        c = 0
        for fb in range(DM // CHUNK):
            for n, kd in enumerate(KD):
                for half in range(2):
                    if c or half:
                        split_lo(F_DOWN + 2 * c + half, 2 * (c % 2) + half, kd)
                    if n == 0 and fb:
                        evict_down(fb - 1, half)
                if c == 0:
                    sample_product(FT - 1)
                    keep_turned(FT - 1)
                    gates(40, 1, gmod2)
                c += 1
                if n == 0 and fb:
                    sample_down(fb - 1)
        for half in range(2):
            evict_down(DM // CHUNK - 1, half)
        sample_down(DM // CHUNK - 1)
        dve.drain().then_inc(s_x3, 1)
        dve.wait_ge(s_fw, 16)
        for i in range(TT + 1):
            n = P if i < TT else S
            dve.wait_ge(s_ysq, i + 1)
            if i < TT:
                then(tt(st2[0:n, 2:3], st[0:n, 0:1], st[0:n, 1:2], ALU.add))
                then(ts(st2[0:n, 0:1], st2[0:n, 2:3], 1.0 / DM, EPS, ALU.mult, ALU.add))
            else:
                then(ts(st2[0:n, 0:1], st[0:n, 0:1], 1.0 / DM, EPS, ALU.mult, ALU.add))
            dve.reciprocal(st2[0:n, 0:1], st2[0:n, 0:1]).then_inc(s_yi, 1)
            dve.wait_ge(s_yr, i + 1)
            for e in range(2):
                c = slice(512 * e, 512 * e + 512)
                if i < TT:
                    dve.scalar_tensor_tensor(ytok[i % 2][:, c], bank[2 * (i % 2) + e][:, :], st2[:, 1:2], fw[:, c], ALU.mult, ALU.mult)
                else:
                    dve.scalar_tensor_tensor(x2s[:, c], x2s[:, c], st2[0:S, 1:2], fw[0:S, c], ALU.mult, ALU.mult)
            dve.drain().then_inc(s_y, 1)

    persist.close()


_INS = ['x_prompt', 'x_sample', 'cache_k', 'cache_v', 'state_ret', 'page_table', 'c_prompt', 'c_sample',
        'norm1_w', 'norm2_w', 'final_w', 'w_mod', 'b_mod', 'w_in', 'ret_gn_w', 'moba_norm_w', 'w_out',
        'w_gate', 'w_up', 'w_down']
_OUTS = [(1, T, DM), (NB_SEQ, TS, DM), (1, 1, T, H, HD), (1, 1, T, H, HD), (1, 1, H, HD, HD),
         (1, NB_SEQ, TS, H, HD), (1, NB_SEQ, TS, H, HD), (1, NB_SEQ, H, HD, HD)]


def kernel(**inputs):
    import concourse.bacc as bacc
    from concourse.bass_utils import run_bass_kernel_spmd

    nc = bacc.Bacc("TRN2", target_bir_lowering=False, num_devices=1)
    const, where = constants()
    arrays, args = {}, []
    for name, a in [(n, inputs[n]) for n in _INS] + [("const", const)]:
        a = np.ascontiguousarray(a)
        arrays[f"in_{name}"] = a
        args.append(nc.dram_tensor(f"in_{name}", a.shape, mybir.dt.from_np(a.dtype), kind="ExternalInput").ap())
    args.append(where)
    for i, shape in enumerate(_OUTS):
        args.append(nc.dram_tensor(f"out_{i}", shape, F32, kind="ExternalOutput").ap())
    decoder_step(nc, *args)
    r = run_bass_kernel_spmd(nc, [arrays], core_ids=[0])
    return tuple(r.results[0][f"out_{i}"] for i in range(len(_OUTS)))
```
